# Optimizing a Trainium2 kernel written in Bass

```python
import math
import jax, jax.numpy as jnp
from jax import lax
import numpy as np

D_MODEL = 1024
BATCH = 1
SEQ = 256
DEPTH = 2

N_BRANCH = 4
A_HEADS = 4
A_HEAD_DIM = 128
A_WIDTH = A_HEADS * A_HEAD_DIM
IDX_HEADS = 4
IDX_DIM = 64
TOPK_MAX = 256
CB_WIDTH = 512
CB_CONV = 31
CC_WIDTH = 512
CC_CONV = 3
SB_HEADS = 4
SB_HEAD_DIM = 128
SB_WIDTH = SB_HEADS * SB_HEAD_DIM
D_FF = 2816
FFN_CONV = 3
ROPE_THETA = 500000.0
ROT_FRACTION_DIV = 4
BLOCK_Q = 128
NORM_EPS = 1e-6

SPLIT_SIZES = (A_WIDTH, A_WIDTH, A_WIDTH, IDX_HEADS * IDX_DIM, IDX_DIM, IDX_HEADS,
               2 * CB_WIDTH, 3 * CC_WIDTH, 3 * SB_WIDTH, N_BRANCH * D_MODEL)
N_IN = sum(SPLIT_SIZES)


def _split_offsets(sizes):
    offs, acc = [], 0
    for s in sizes[:-1]:
        acc += s
        offs.append(acc)
    return offs

def rms_norm(x, g):
    xf = x.astype(jnp.float32)
    y = xf * lax.rsqrt(jnp.mean(xf * xf, axis=-1, keepdims=True) + NORM_EPS)
    return (y * g.astype(jnp.float32)).astype(x.dtype)

def layer_norm(x, g, b):
    xf = x.astype(jnp.float32)
    mu = jnp.mean(xf, axis=-1, keepdims=True)
    xc = xf - mu
    y = xc * lax.rsqrt(jnp.mean(xc * xc, axis=-1, keepdims=True) + NORM_EPS)
    return (y * g.astype(jnp.float32) + b.astype(jnp.float32)).astype(x.dtype)

def partial_rope(x, pos):
    d = x.shape[-1]
    rot = d // ROT_FRACTION_DIV
    half = rot // 2
    inv_freq = ROPE_THETA ** (-(jnp.arange(half, dtype=jnp.float32) * 2.0) / rot)
    ang = pos.astype(jnp.float32)[..., None] * inv_freq
    cos = jnp.cos(ang)[:, :, None, :]
    sin = jnp.sin(ang)[:, :, None, :]
    xf = x.astype(jnp.float32)
    x1, x2 = xf[..., :half], xf[..., half:rot]
    out = jnp.concatenate([x1 * cos - x2 * sin, x2 * cos + x1 * sin, xf[..., rot:]], axis=-1)
    return out.astype(x.dtype)

def causal_dwconv(x, w, b=None):
    width = w.shape[0]
    y = lax.conv_general_dilated(
        x, w.astype(x.dtype)[:, None, :], window_strides=(1,), padding=[(width - 1, 0)],
        dimension_numbers=('NWC', 'WIO', 'NWC'), feature_group_count=x.shape[-1])
    if b is not None:
        y = y + b.astype(x.dtype)
    return y

def _to_blocks(a, nb):
    return jnp.moveaxis(a.reshape((a.shape[0], nb, BLOCK_Q) + a.shape[2:]), 1, 0)

def _from_blocks(a):
    a = jnp.moveaxis(a, 0, 1)
    return a.reshape(a.shape[0], -1, a.shape[-2] * a.shape[-1])

def dsa_attention(q, k, v, q_idx, k_idx, w_idx):
    bsz, seq = q.shape[0], q.shape[1]
    nb = seq // BLOCK_Q
    k_sel = min(TOPK_MAX, seq // 4)
    kv = jnp.stack([k, v], axis=2)
    s_idx = jnp.arange(seq)
    k_idx_f = k_idx.astype(jnp.float32)

    def block(args):
        qb, qib, wb, tb = args
        rel = jax.nn.relu(jnp.einsum('bthd,bsd->bths', qib.astype(jnp.float32), k_idx_f) * IDX_DIM ** -0.5)
        score = jnp.einsum('bths,bth->bts', rel, wb.astype(jnp.float32)) * IDX_HEADS ** -0.5
        causal = s_idx[None, :] <= tb[:, None]
        score = jnp.where(causal[None], score, -jnp.inf)
        _, sel = lax.top_k(score, k_sel)
        valid = sel <= tb[None, :, None]
        kv_sel = jax.vmap(lambda a, i: a[i])(kv, sel)
        logits = jnp.einsum('bthd,btkhd->bthk', qb.astype(jnp.float32),
                            kv_sel[:, :, :, 0].astype(jnp.float32)) * A_HEAD_DIM ** -0.5
        logits = jnp.where(valid[:, :, None, :], logits, -jnp.inf)
        p = jax.nn.softmax(logits, axis=-1)
        out = jnp.einsum('bthk,btkhd->bthd', p, kv_sel[:, :, :, 1].astype(jnp.float32))
        return out.astype(qb.dtype)

    t_blocks = jnp.arange(seq).reshape(nb, BLOCK_Q)
    out = lax.map(block, (_to_blocks(q, nb), _to_blocks(q_idx, nb), _to_blocks(w_idx, nb), t_blocks))
    return _from_blocks(out)

def stick_breaking_attention(q, k, v):
    seq = q.shape[1]
    nb = seq // BLOCK_Q
    s_idx = jnp.arange(seq)
    k_f = k.astype(jnp.float32)
    v_f = v.astype(jnp.float32)

    def block(args):
        qb, tb = args
        z = jnp.einsum('bthd,bshd->bhts', qb.astype(jnp.float32), k_f) * SB_HEAD_DIM ** -0.5
        mask = (s_idx[None, :] < tb[:, None])[None, None]
        log_keep = jnp.where(mask, jax.nn.log_sigmoid(-z), 0.0)
        between = lax.cumsum(log_keep, axis=3, reverse=True) - log_keep
        a = jnp.where(mask, jnp.exp(jax.nn.log_sigmoid(z) + between), 0.0)
        return jnp.einsum('bhts,bshd->bthd', a, v_f).astype(qb.dtype)

    t_blocks = jnp.arange(seq).reshape(nb, BLOCK_Q)
    out = lax.map(block, (_to_blocks(q, nb), t_blocks))
    return _from_blocks(out)

def first_inputs(seed: int = 0) -> dict:
    key = jax.random.key(seed)
    ks = jax.random.split(key, 24)
    f32 = jnp.float32

    def nrm(k, shape, scale):
        return jax.random.normal(k, shape, f32) * scale

    def gain(k, shape):
        return 1.0 + 0.05 * jax.random.normal(k, shape, f32)

    L, D = DEPTH, D_MODEL
    return {
        "x": jax.random.normal(ks[0], (BATCH, SEQ, D), f32),
        "positions": jnp.broadcast_to(jnp.arange(SEQ, dtype=jnp.int32), (BATCH, SEQ)),
        "g_mix": gain(ks[1], (L, D)),
        "w_in": nrm(ks[2], (L, D, N_IN), D ** -0.5),
        "b_gate": nrm(ks[3], (L, N_BRANCH * D), 0.1),
        "g_qa": gain(ks[4], (L, A_HEAD_DIM)),
        "g_ka": gain(ks[5], (L, A_HEAD_DIM)),
        "g_kidx": gain(ks[6], (L, IDX_DIM)),
        "w_oa": nrm(ks[7], (L, A_WIDTH, D), A_WIDTH ** -0.5),
        "cb_conv_w": nrm(ks[8], (L, CB_CONV, CB_WIDTH), CB_CONV ** -0.5),
        "cb_conv_b": nrm(ks[9], (L, CB_WIDTH), 0.02),
        "cb_ln_g": gain(ks[10], (L, CB_WIDTH)),
        "cb_ln_b": nrm(ks[11], (L, CB_WIDTH), 0.02),
        "w_ob": nrm(ks[12], (L, CB_WIDTH, D), CB_WIDTH ** -0.5),
        "cc_conv_w": nrm(ks[13], (L, CC_CONV, CC_WIDTH), CC_CONV ** -0.5),
        "w_oc": nrm(ks[14], (L, CC_WIDTH, D), CC_WIDTH ** -0.5),
        "w_od": nrm(ks[15], (L, SB_WIDTH, D), SB_WIDTH ** -0.5),
        "w_merge": nrm(ks[16], (L, D, D), D ** -0.5),
        "g_ffn": gain(ks[17], (L, D)),
        "w_ffn_gate": nrm(ks[18], (L, D, D_FF), D ** -0.5),
        "w_ffn_up": nrm(ks[19], (L, D, D_FF), D ** -0.5),
        "ffn_conv_w": nrm(ks[20], (L, FFN_CONV, D_FF), FFN_CONV ** -0.5),
        "w_ffn_down": nrm(ks[21], (L, D_FF, D), D_FF ** -0.5),
    }

def first_block(x, positions, g_mix, w_in, b_gate, g_qa, g_ka, g_kidx, w_oa,
              cb_conv_w, cb_conv_b, cb_ln_g, cb_ln_b, w_ob, cc_conv_w, w_oc, w_od,
              w_merge, g_ffn, w_ffn_gate, w_ffn_up, ffn_conv_w, w_ffn_down):
    bsz, seq, dm = x.shape
    offs = _split_offsets(SPLIT_SIZES)
    for l in range(DEPTH):
        h = rms_norm(x, g_mix[l])
        proj = h @ w_in[l]
        aq, ak, av, iq, ik, iw, glu_in, cc_in, sb_in, gate_in = jnp.split(proj, offs, axis=-1)

        qa = partial_rope(rms_norm(aq.reshape(bsz, seq, A_HEADS, A_HEAD_DIM), g_qa[l]), positions)
        ka = partial_rope(rms_norm(ak.reshape(bsz, seq, A_HEADS, A_HEAD_DIM), g_ka[l]), positions)
        va = av.reshape(bsz, seq, A_HEADS, A_HEAD_DIM)
        qi = partial_rope(iq.reshape(bsz, seq, IDX_HEADS, IDX_DIM), positions)
        ki = partial_rope(rms_norm(ik, g_kidx[l])[:, :, None, :], positions)[:, :, 0]
        y_a = dsa_attention(qa, ka, va, qi, ki, iw) @ w_oa[l]

        glu_a, glu_b = jnp.split(glu_in, 2, axis=-1)
        u = causal_dwconv(glu_a * jax.nn.sigmoid(glu_b), cb_conv_w[l], cb_conv_b[l])
        y_b = jax.nn.silu(layer_norm(u, cb_ln_g[l], cb_ln_b[l])) @ w_ob[l]

        gb, gc, xc = jnp.split(cc_in, 3, axis=-1)
        y_c = (gb * causal_dwconv(gc * xc, cc_conv_w[l])) @ w_oc[l]

        sq, sk, sv = jnp.split(sb_in, 3, axis=-1)
        shp = (bsz, seq, SB_HEADS, SB_HEAD_DIM)
        y_d = stick_breaking_attention(sq.reshape(shp), sk.reshape(shp), sv.reshape(shp)) @ w_od[l]

        gates = jax.nn.sigmoid(gate_in + b_gate[l]).reshape(bsz, seq, N_BRANCH, dm)
        merged = (gates[:, :, 0] * y_a + gates[:, :, 1] * y_b
                  + gates[:, :, 2] * y_c + gates[:, :, 3] * y_d)
        x = x + merged @ w_merge[l]

        h2 = rms_norm(x, g_ffn[l])
        gt = causal_dwconv(h2 @ w_ffn_gate[l], ffn_conv_w[l])
        x = x + (jax.nn.silu(gt) * (h2 @ w_ffn_up[l])) @ w_ffn_down[l]
    return x


RMS_EPS = 1e-6
Q_BLOCK = 128

MLA_HEADS = 4
MLA_NOPE = 64
MLA_ROPE = 32
MLA_V = 64
MLA_Q_LORA = 256
MLA_KV_LORA = 128
MLA_WIDTH = MLA_HEADS * MLA_V
ROPE_THETA_2 = 10000.0

GDN_HEADS = 4
GDN_DK = 128
GDN_DV = 128
GDN_CONV = 4
GDN_CHUNK = 64
GDN_WIDTH = GDN_HEADS * GDN_DV

MOBA_HEADS = 4
MOBA_DH = 64
MOBA_BLOCK = 256
MOBA_TOPK = 3
MOBA_WIDTH = MOBA_HEADS * MOBA_DH

T5_BUCKETS = 32
T5_MAX_DIST = 2048

MIX_WIDTH = MLA_WIDTH + GDN_WIDTH + MOBA_WIDTH

IN_SIZES = (
    MLA_Q_LORA, MLA_KV_LORA, MLA_ROPE, MLA_WIDTH,
    GDN_HEADS * GDN_DK, GDN_HEADS * GDN_DK, GDN_WIDTH, GDN_WIDTH,
    GDN_HEADS, GDN_HEADS,
    MOBA_WIDTH, MOBA_WIDTH, MOBA_WIDTH, MOBA_WIDTH,
)
IN_COLS = sum(IN_SIZES)


def rmsnorm(x, w):
    xf = x.astype(jnp.float32)
    y = xf * lax.rsqrt(jnp.mean(xf * xf, axis=-1, keepdims=True) + RMS_EPS)
    return (y * w.astype(jnp.float32)).astype(x.dtype)

def l2norm(x):
    xf = x.astype(jnp.float32)
    return xf * lax.rsqrt(jnp.sum(xf * xf, axis=-1, keepdims=True) + 1e-6)

def rope_tables(seq, dim):
    inv = 1.0 / (ROPE_THETA_2 ** (jnp.arange(0, dim, 2, dtype=jnp.float32) / dim))
    ang = jnp.arange(seq, dtype=jnp.float32)[:, None] * inv[None, :]
    return jnp.cos(ang), jnp.sin(ang)

def apply_rope(x, cos, sin):
    half = x.shape[-1] // 2
    xf = x.astype(jnp.float32)
    x1, x2 = xf[..., :half], xf[..., half:]
    c, s = cos[None, :, None, :], sin[None, :, None, :]
    return jnp.concatenate([x1 * c - x2 * s, x1 * s + x2 * c], axis=-1).astype(x.dtype)

def t5_bucket(rel):
    n = jnp.maximum(rel, 0)
    max_exact = T5_BUCKETS // 2
    nf = jnp.maximum(n, 1).astype(jnp.float32)
    large = max_exact + (jnp.log(nf / max_exact) / math.log(T5_MAX_DIST / max_exact)
                         * (T5_BUCKETS - max_exact)).astype(jnp.int32)
    large = jnp.minimum(large, T5_BUCKETS - 1)
    return jnp.where(n < max_exact, n, large)

def causal_block_attention(q, k, v, scale):
    B, S, H, Dk = q.shape
    Dv = v.shape[-1]
    nqb = S // Q_BLOCK
    qb = q.reshape(B, nqb, Q_BLOCK, H, Dk).transpose(1, 0, 2, 3, 4)
    kpos = jnp.arange(S)

    def one(args):
        i, qi = args
        logits = jnp.einsum('bqhd,bkhd->bhqk', qi, k, preferred_element_type=jnp.float32) * scale
        qpos = i * Q_BLOCK + jnp.arange(Q_BLOCK)
        logits = jnp.where(kpos[None, :] <= qpos[:, None], logits, -jnp.inf)
        p = jax.nn.softmax(logits, axis=-1).astype(v.dtype)
        return jnp.einsum('bhqk,bkhd->bqhd', p, v)

    out = lax.map(one, (jnp.arange(nqb), qb))
    return out.transpose(1, 0, 2, 3, 4).reshape(B, S, H, Dv)

def mla_mixer(c_q, c_kv, k_rope, q_norm_w, w_uq, kv_norm_w, w_ukv, cos, sin):
    B, S, _ = c_q.shape
    q = (rmsnorm(c_q, q_norm_w) @ w_uq).reshape(B, S, MLA_HEADS, MLA_NOPE + MLA_ROPE)
    q_nope, q_pe = q[..., :MLA_NOPE], q[..., MLA_NOPE:]
    q_pe = apply_rope(q_pe, cos, sin)
    kv = (rmsnorm(c_kv, kv_norm_w) @ w_ukv).reshape(B, S, MLA_HEADS, MLA_NOPE + MLA_V)
    k_nope, v = kv[..., :MLA_NOPE], kv[..., MLA_NOPE:]
    k_pe = apply_rope(k_rope[:, :, None, :], cos, sin)
    k = jnp.concatenate([k_nope, jnp.broadcast_to(k_pe, (B, S, MLA_HEADS, MLA_ROPE))], axis=-1)
    qh = jnp.concatenate([q_nope, q_pe], axis=-1)
    o = causal_block_attention(qh, k, v, (MLA_NOPE + MLA_ROPE) ** -0.5)
    return o.reshape(B, S, MLA_WIDTH)

def causal_conv(x, w):
    K = w.shape[0]
    S = x.shape[1]
    xp = jnp.pad(x, ((0, 0), (K - 1, 0), (0, 0)))
    return sum(xp[:, j:j + S] * w[j] for j in range(K))

def chunk_gated_delta_rule(q, k, v, beta, g):
    B, S, H, DK = q.shape
    DV = v.shape[-1]
    C = GDN_CHUNK
    N = S // C

    def chunks(t):
        return t.reshape(B, N, C, H, t.shape[-1]).transpose(0, 3, 1, 2, 4)

    qc, kc, vc = chunks(q), chunks(k), chunks(v)
    bc = beta.reshape(B, N, C, H).transpose(0, 3, 1, 2)
    gc = jnp.cumsum(g.reshape(B, N, C, H).transpose(0, 3, 1, 2), axis=-1)

    idx = jnp.arange(C)
    strict = idx[:, None] > idx[None, :]
    incl = idx[:, None] >= idx[None, :]
    diff = gc[..., :, None] - gc[..., None, :]
    decay = jnp.exp(jnp.where(incl, diff, -jnp.inf))

    kk = jnp.einsum('bhntd,bhnjd->bhntj', kc, kc)
    L = jnp.where(strict, bc[..., :, None] * kk * decay, 0.0)
    rhs = jnp.concatenate([kc * (bc * jnp.exp(gc))[..., None], vc * bc[..., None]], axis=-1)
    sol = lax.linalg.triangular_solve(L + jnp.eye(C, dtype=L.dtype), rhs,
                                      left_side=True, lower=True, unit_diagonal=True)
    W, U0 = sol[..., :DK], sol[..., DK:]
    A_qk = jnp.einsum('bhntd,bhnjd->bhntj', qc, kc) * decay
    q_g = qc * jnp.exp(gc)[..., None]
    k_end = kc * jnp.exp(gc[..., -1:] - gc)[..., None]
    g_end = jnp.exp(gc[..., -1])

    def step(state, xs):
        W_n, U0_n, A_n, qg_n, ke_n, ge_n = xs
        U = U0_n - jnp.einsum('bhcd,bhde->bhce', W_n, state)
        o = jnp.einsum('bhcd,bhde->bhce', qg_n, state) + jnp.einsum('bhtj,bhje->bhte', A_n, U)
        new_state = ge_n[..., None, None] * state + jnp.einsum('bhcd,bhce->bhde', ke_n, U)
        return new_state, o

    xs = tuple(jnp.moveaxis(t, 2, 0) for t in (W, U0, A_qk, q_g, k_end, g_end))
    s0 = jnp.zeros((B, H, DK, DV), jnp.float32)
    _, o = lax.scan(step, s0, xs)
    return o.transpose(1, 0, 3, 2, 4).reshape(B, S, H, DV)

def gdn_mixer(q, k, v, z, b, a, conv_w, A_log, dt_bias, norm_w):
    B, S, _ = q.shape
    qkv = jax.nn.silu(causal_conv(jnp.concatenate([q, k, v], axis=-1), conv_w))
    nk = GDN_HEADS * GDN_DK
    q, k, v = qkv[..., :nk], qkv[..., nk:2 * nk], qkv[..., 2 * nk:]
    q = l2norm(q.reshape(B, S, GDN_HEADS, GDN_DK)) * (GDN_DK ** -0.5)
    k = l2norm(k.reshape(B, S, GDN_HEADS, GDN_DK))
    v = v.reshape(B, S, GDN_HEADS, GDN_DV).astype(jnp.float32)
    beta = jax.nn.sigmoid(b.astype(jnp.float32))
    g = -jnp.exp(A_log.astype(jnp.float32)) * jax.nn.softplus(
        a.astype(jnp.float32) + dt_bias.astype(jnp.float32))
    o = chunk_gated_delta_rule(q, k, v, beta, g).astype(z.dtype)
    o = rmsnorm(o, norm_w) * jax.nn.silu(z.reshape(B, S, GDN_HEADS, GDN_DV))
    return o.reshape(B, S, GDN_WIDTH)

def moba_mixer(q, k, v, t5_table):
    B, S, _ = q.shape
    H, Dh, BS = MOBA_HEADS, MOBA_DH, MOBA_BLOCK
    q = q.reshape(B, S, H, Dh).transpose(0, 2, 1, 3)
    k = k.reshape(B, S, H, Dh).transpose(0, 2, 1, 3)
    v = v.reshape(B, S, H, Dh).transpose(0, 2, 1, 3)
    NB = -(-S // BS)
    pad = NB * BS - S
    kp = jnp.pad(k, ((0, 0), (0, 0), (0, pad), (0, 0)))
    vp = jnp.pad(v, ((0, 0), (0, 0), (0, pad), (0, 0)))
    kblk = kp.reshape(B, H, NB, BS, Dh)
    vblk = vp.reshape(B, H, NB, BS, Dh)
    kmean = jnp.mean(kblk.astype(jnp.float32), axis=3).astype(k.dtype)
    topk = min(MOBA_TOPK, NB)
    scale = Dh ** -0.5
    nqb = S // Q_BLOCK
    qb = jnp.moveaxis(q.reshape(B, H, nqb, Q_BLOCK, Dh), 2, 0)
    bi = jnp.arange(B)[:, None, None, None]
    hi = jnp.arange(H)[None, :, None, None]
    hi5 = jnp.arange(H)[None, :, None, None, None]
    blk_iota = jnp.arange(BS)

    def one(args):
        i, qi = args
        qpos = i * Q_BLOCK + jnp.arange(Q_BLOCK)
        own = (i * Q_BLOCK) // BS
        gate = jnp.einsum('bhqd,bhnd->bhqn', qi, kmean, preferred_element_type=jnp.float32)
        gate = jnp.where(jnp.arange(NB) < own, gate, -jnp.inf)
        _, sel = lax.top_k(gate, topk)
        valid = sel < own
        ksel = kblk[bi, hi, sel]
        vsel = vblk[bi, hi, sel]
        kpos_sel = sel[..., None] * BS + blk_iota
        bias_sel = t5_table[t5_bucket(qpos[None, None, :, None, None] - kpos_sel), hi5]
        l_sel = jnp.einsum('bhqd,bhqnkd->bhqnk', qi, ksel, preferred_element_type=jnp.float32) * scale
        l_sel = jnp.where(valid[..., None], l_sel + bias_sel.astype(jnp.float32), -jnp.inf)
        kown = lax.dynamic_slice_in_dim(kp, own * BS, BS, axis=2)
        vown = lax.dynamic_slice_in_dim(vp, own * BS, BS, axis=2)
        kpos_own = own * BS + blk_iota
        rel_own = qpos[:, None] - kpos_own[None, :]
        bias_own = t5_table[t5_bucket(rel_own)].transpose(2, 0, 1)[None]
        l_own = jnp.einsum('bhqd,bhkd->bhqk', qi, kown, preferred_element_type=jnp.float32) * scale
        l_own = jnp.where(rel_own[None, None] >= 0, l_own + bias_own.astype(jnp.float32), -jnp.inf)
        logits = jnp.concatenate([l_sel.reshape(B, H, Q_BLOCK, topk * BS), l_own], axis=-1)
        p = jax.nn.softmax(logits, axis=-1).astype(v.dtype)
        p_sel = p[..., :topk * BS].reshape(B, H, Q_BLOCK, topk, BS)
        p_own = p[..., topk * BS:]
        return (jnp.einsum('bhqnk,bhqnkd->bhqd', p_sel, vsel)
                + jnp.einsum('bhqk,bhkd->bhqd', p_own, vown))

    out = lax.map(one, (jnp.arange(nqb), qb))
    out = out.transpose(1, 2, 0, 3, 4).reshape(B, H, S, Dh)
    return out.transpose(0, 2, 1, 3).reshape(B, S, MOBA_WIDTH)

def hybrid_layer(x, norm_w, w_in, mla_q_norm, mla_w_uq, mla_kv_norm, mla_w_ukv,
                 gdn_conv_w, gdn_A_log, gdn_dt_bias, gdn_norm_w, w_out, t5_table, cos, sin):
    h = rmsnorm(x, norm_w)
    proj = h @ w_in
    split_points = np.cumsum(IN_SIZES)[:-1].tolist()
    (m_cq, m_ckv, m_kr, m_gate, g_q, g_k, g_v, g_z, g_b, g_a,
     c_q, c_k, c_v, c_gate) = jnp.split(proj, split_points, axis=-1)
    y_mla = mla_mixer(m_cq, m_ckv, m_kr, mla_q_norm, mla_w_uq, mla_kv_norm, mla_w_ukv,
                      cos, sin) * jax.nn.silu(m_gate)
    y_gdn = gdn_mixer(g_q, g_k, g_v, g_z, g_b, g_a, gdn_conv_w, gdn_A_log, gdn_dt_bias, gdn_norm_w)
    y_moba = moba_mixer(c_q, c_k, c_v, t5_table) * jax.nn.silu(c_gate)
    y = jnp.concatenate([y_mla, y_gdn, y_moba], axis=-1)
    return x + y @ w_out

def second_inputs(seed: int = 0) -> dict:
    key = jax.random.key(seed)
    ks = jax.random.split(key, 20)
    nrm = jax.random.normal
    f32 = jnp.float32
    dt = jnp.exp(jax.random.uniform(ks[10], (DEPTH, GDN_HEADS), f32, math.log(1e-3), math.log(1e-1)))
    return {
        "x": nrm(ks[0], (BATCH, SEQ, D_MODEL), f32),
        "norm_w": 1.0 + 0.02 * nrm(ks[1], (DEPTH, D_MODEL), f32),
        "w_in": nrm(ks[2], (DEPTH, D_MODEL, IN_COLS), f32) * D_MODEL ** -0.5,
        "mla_q_norm": 1.0 + 0.02 * nrm(ks[3], (DEPTH, MLA_Q_LORA), f32),
        "mla_w_uq": nrm(ks[4], (DEPTH, MLA_Q_LORA, MLA_HEADS * (MLA_NOPE + MLA_ROPE)), f32) * MLA_Q_LORA ** -0.5,
        "mla_kv_norm": 1.0 + 0.02 * nrm(ks[5], (DEPTH, MLA_KV_LORA), f32),
        "mla_w_ukv": nrm(ks[6], (DEPTH, MLA_KV_LORA, MLA_HEADS * (MLA_NOPE + MLA_V)), f32) * MLA_KV_LORA ** -0.5,
        "gdn_conv_w": nrm(ks[7], (DEPTH, GDN_CONV, 2 * GDN_HEADS * GDN_DK + GDN_WIDTH), f32) * GDN_CONV ** -0.5,
        "gdn_A_log": jnp.log(jax.random.uniform(ks[8], (DEPTH, GDN_HEADS), f32, 1.0, 16.0)),
        "gdn_dt_bias": jnp.log(jnp.expm1(dt)),
        "gdn_norm_w": 1.0 + 0.02 * nrm(ks[9], (DEPTH, GDN_DV), f32),
        "w_out": nrm(ks[11], (DEPTH, MIX_WIDTH, D_MODEL), f32) * (MIX_WIDTH * 2 * DEPTH) ** -0.5,
        "t5_table": 0.5 * nrm(ks[12], (T5_BUCKETS, MOBA_HEADS), f32),
        "final_norm_w": 1.0 + 0.02 * nrm(ks[13], (D_MODEL,), f32),
    }

def second_block(x, norm_w, w_in, mla_q_norm, mla_w_uq, mla_kv_norm, mla_w_ukv,
              gdn_conv_w, gdn_A_log, gdn_dt_bias, gdn_norm_w, w_out, t5_table, final_norm_w):
    S = x.shape[1]
    cos, sin = rope_tables(S, MLA_ROPE)
    for l in range(DEPTH):
        x = hybrid_layer(x, norm_w[l], w_in[l], mla_q_norm[l], mla_w_uq[l], mla_kv_norm[l],
                         mla_w_ukv[l], gdn_conv_w[l], gdn_A_log[l], gdn_dt_bias[l],
                         gdn_norm_w[l], w_out[l], t5_table, cos, sin)
    return rmsnorm(x, final_norm_w)


def setup_inputs(seed=0):
    out = dict(first_inputs(seed))
    for name, value in second_inputs(seed + 1).items():
        if name != "x":
            out[name + "_2"] = value
    return out


def reference(
    x, positions, g_mix, w_in, b_gate, g_qa, g_ka, g_kidx, w_oa, cb_conv_w, cb_conv_b, cb_ln_g,
    cb_ln_b, w_ob, cc_conv_w, w_oc, w_od, w_merge, g_ffn, w_ffn_gate, w_ffn_up, ffn_conv_w,
    w_ffn_down, norm_w_2, w_in_2, mla_q_norm_2, mla_w_uq_2, mla_kv_norm_2, mla_w_ukv_2,
    gdn_conv_w_2, gdn_A_log_2, gdn_dt_bias_2, gdn_norm_w_2, w_out_2, t5_table_2, final_norm_w_2,
):
    x = first_block(
        x, positions, g_mix, w_in, b_gate, g_qa, g_ka, g_kidx, w_oa, cb_conv_w, cb_conv_b,
        cb_ln_g, cb_ln_b, w_ob, cc_conv_w, w_oc, w_od, w_merge, g_ffn, w_ffn_gate, w_ffn_up,
        ffn_conv_w, w_ffn_down,
    )
    return second_block(
        x, norm_w_2, w_in_2, mla_q_norm_2, mla_w_uq_2, mla_kv_norm_2, mla_w_ukv_2, gdn_conv_w_2,
        gdn_A_log_2, gdn_dt_bias_2, gdn_norm_w_2, w_out_2, t5_table_2, final_norm_w_2,
    )


_drawn_inputs = setup_inputs


def setup_inputs(seed=0):
    import zlib

    import numpy as np

    out = dict(_drawn_inputs(seed))
    spreads = {}
    factors = {'g_qa': 6.894,
     'g_ka': 6.419,
     'cb_ln_b': 5.441,
     'norm_w_2': 8.0,
     'mla_q_norm_2': 8.0,
     'mla_w_uq_2': 2.901,
     'mla_kv_norm_2': 8.0,
     'gdn_norm_w_2': 8.0,
     't5_table_2': 4.911,
     'final_norm_w_2': 2.782}
    for name, (base, spread) in spreads.items():
        noise = np.random.default_rng([zlib.crc32(name.encode()), seed]).standard_normal(out[name].shape)
        drawn = base * np.exp(spread * noise) if base else spread * noise
        out[name] = __import__('jax').numpy.asarray(drawn.astype(out[name].dtype))
    for name, factor in factors.items():
        out[name] = (out[name] * factor).astype(out[name].dtype)
    return out
```

```python
from contextlib import ExitStack

import numpy as np
import concourse.bass as bass
from concourse import mybir

F32 = mybir.dt.float32
I32 = mybir.dt.int32
ALU = mybir.AluOpType
ACT = mybir.ActivationFunctionType
AX = mybir.AxisListType

P = 128
S = 256
D = 1024
L = 2
FF = 2816
NIN1 = 10052
NIN2 = 3752
SLOT = 8 * 520
NSLOT = 3
NEG = -1e30
PICKED = -3e38

PL = {}
_at = 0
for _n, _w in (("g_mix", 8), ("b_gate", 32), ("cb_w", 124), ("cb_b", 4), ("ln_g", 4), ("ln_b", 4),
               ("cc_w", 12), ("g_ffn", 8), ("ffn_w", 66), ("norm2", 8), ("qn2", 2), ("kvn2", 1),
               ("gdn_w", 48), ("gdn_n", 1), ("alog", 4), ("dtb", 4)):
    PL[_n] = (_at, _w)
    _at += _w
NPL = _at
ROWS = {"g_q": (0, 128), "g_k": (128, 128), "g_ki": (256, 64)}

CN = {}
_at = 0
for _n, _w in (("ident", 128), ("tri", 128), ("strict", 128), ("lv", 6 * 128),
               ("blk", 128), ("half0", 128), ("half1", 128), ("trirev", 128), ("zero", 128), ("causal", 128),
               ("m0", 256), ("n0", 256), ("invf", 24),
               ("rope2", 64)):
    CN[_n] = (_at, _w)
    _at += _w
NCN = _at


class Queue:

    def __init__(self, sem):
        self.sem, self.n, self.ops, self.seen = sem, 0, [], {}

    def wait(self, *tokens):
        for t in tokens:
            if t is None:
                continue
            if isinstance(t, list):
                self.wait(*t)
            elif self.seen.get(id(t[0]), 0) < t[1]:
                self.seen[id(t[0])] = t[1]
                self.ops.append(lambda e, t=t: e.wait_ge(t[0], t[1]))

    def quiet(self, fn):
        self.ops.append(fn)

    def __call__(self, fn, *after):
        self.wait(*after)
        self.n += 1
        self.ops.append(lambda e: fn(e).then_inc(self.sem, 1))
        return (self.sem, self.n)

    def run(self, e):
        for op in self.ops:
            op(e)


def build(nc, a, out):
    ctx = ExitStack()
    with ctx:
        def sb(name, shape, dt=F32):
            return ctx.enter_context(nc.sbuf_tensor(name, shape, dt))

        def sem(name):
            return ctx.enter_context(nc.semaphore(name))

        banks = [ctx.enter_context(nc.psum_tensor(f"bank{i}", [P, 512], F32)) for i in range(8)]

        ring = sb("ring", [P, NSLOT, SLOT])
        cst = sb("cst", [P, NCN])
        par = sb("par", [P, L * NPL])
        onesb = sb("onesb", [P, 128])
        mhalf = sb("mhalf", [P, 1])
        posi = sb("posi", [P, 2], I32)
        posf = sb("posf", [P, 2])
        x = sb("x", [P, 2, D])
        xn = sb("xn", [P, 2, D])
        hT = sb("hT", [P, 8, S])
        big = sb("big", [P, 32 * S])
        mer = sb("mer", [P, 8, S])
        st = sb("st", [P, 512])
        cs = sb("cs", [P, 2, 48])
        bufA = sb("bufA", [P, 4 * S])
        bufB = sb("bufB", [P, 4 * S])
        bufC = sb("bufC", [P, 4 * S])
        bufD = sb("bufD", [P, 4 * S])
        bufE = sb("bufE", [P, 4 * S])
        bufF = sb("bufF", [P, 4 * S])
        bufG = sb("bufG", [P, 4 * S])
        bufH = sb("bufH", [P, 4 * S])
        bufI = sb("bufI", [P, 4 * S])
        bufJ = sb("bufJ", [P, 4 * S])
        ptb = sb("ptb", [P, 3, 4, 128])
        pt = [[ptb[:, 0], None], [ptb[:, 1], ptb[:, 2]]]
        two = sb("two", [P, 7168])
        glup = two[:, 0:1144].rearrange("p (c s) -> p c s", c=4)
        ccp = two[:, 1144:2176].rearrange("p (c s) -> p c s", c=4)
        gpad = two[:, 2176:3208].rearrange("p (r c s) -> p r c s", r=2, c=2)
        ibuf = two[:, 3208:3856].rearrange("p (t n) -> p t n", t=2)
        iT = two[0:64, 3856:5136].rearrange("p (h s) -> p h s", h=5)
        gx = two[:, 0:4096].rearrange("p (a n) -> p a n", a=8)
        gs = two[:, 4096:4608].rearrange("p (h d) -> p h d", h=4)
        gains = two[:, 5136:5776]
        rt = two[:, 5776:5968].rearrange("p (t n) -> p t n", t=2)
        gm = two[:, 4608:6144]
        bia = two[:, 6144:7168].rearrange("p (h s) -> p h s", h=4)
        gdp = two[:, 0:1036].rearrange("p (r c s) -> p r c s", r=2, c=2)
        wuq = two[:, 1036:1804].rearrange("p (k n) -> p k n", k=2)
        wukv = two[:, 1804:2316]
        mhalf5 = mhalf
        sgb = sb("sgb", [P, 2, 512])
        tab = sb("tab", [32, 4])

        pe, ve, ac, po = (Queue(sem(n)) for n in ("s_pe", "s_dve", "s_act", "s_pool"))
        sp = Queue(sem("s_sp"))
        s_slot = [sem(f"s_slot{i}") for i in range(NSLOT)]
        s_gn, s_fl = sem("s_gn"), sem("s_fl")
        s_c, s_p, s_x, s_pos, s_tab, s_sc, s_bi, s_u, s_out, s_fn = (
            sem(n) for n in ("s_c", "s_p", "s_x", "s_pos", "s_tab", "s_sc", "s_bi", "s_u", "s_out", "s_fn"))

        def con(name, a0=0, a1=None):
            o, w = CN[name]
            return cst[:, o + a0:o + (w if a1 is None else a1)]

        def prm(name, layer, a0=0, a1=None):
            o, w = PL[name]
            o += layer * NPL
            return par[:, o + a0:o + (w if a1 is None else a1)]

        def row(name, layer):
            o, w = ROWS[name]
            return gains[:, layer * 320 + o:layer * 320 + o + w]

        def dma(q, dst, src, s, *after):
            q.wait(*after)
            q.quiet(lambda e: e.dma_start(dst, src).then_inc(s, 16))

        ident = con("ident")

        loads = []

        def load_list():
            for l in range(L):
                w = a["w_in"][l].rearrange("(k p) n -> p k n", p=P)
                for c0, c1 in ([(1536, 1860), (0, 512), (512, 1024), (1024, 1536),
                                (1860, 2372), (2372, 2884),
                                (3396, 3908), (3908, 4420), (2884, 3396),
                                (4420, 4932), (4932, 5444), (5444, 5956)]
                               + [(5956 + 512 * i, 6468 + 512 * i) for i in range(8)]):
                    loads.append((w[:, :, c0:c1], 8, c1 - c0))
                for n in ("w_ob", "w_oc", "w_od", "w_oa"):
                    loads.append((a[n][l].rearrange("(k p) n -> p k n", p=P), 4, D))
                w = a["w_merge"][l].rearrange("(k p) n -> p k n", p=P)
                for i in range(2):
                    loads.append((w[:, 4 * i:4 * i + 4, :], 4, D))
                g = a["w_ffn_gate"][l].rearrange("(k p) n -> p k n", p=P)
                u = a["w_ffn_up"][l].rearrange("(k p) n -> p k n", p=P)
                for i in range(6):
                    e = min(512 * i + 512, FF)
                    loads.append((g[:, :, 512 * i:e], 8, e - 512 * i))
                    loads.append((u[:, :, 512 * i:e], 8, e - 512 * i))
                w = a["w_ffn_down"][l].rearrange("(k p) n -> p k n", p=P)
                for i in range(6):
                    e = min(4 * i + 4, 22)
                    loads.append((w[:, 4 * i:e, :], e - 4 * i, D))
            for l in range(L):
                w = a["w_in_2"][l].rearrange("(k p) n -> p k n", p=P)
                for c0, c1 in [(0, 416), (2208, 2728), (1184, 1696), (672, 1184), (1696, 2208),
                               (2728, 3240), (3240, 3752), (416, 672)]:
                    loads.append((w[:, :, c0:c1], 8, c1 - c0))
                w = a["w_out_2"][l].rearrange("(k p) n -> p k n", p=P)
                for i in range(2):
                    loads.append((w[:, 4 * i:4 * i + 4, :], 4, D))

        load_list()
        used = [0]

        def slot_view(i):
            _, k, n = loads[i]
            return ring[:, i % NSLOT, 0:k * n].rearrange("p (k n) -> p k n", k=k)

        def issue(i, *after):
            if i < len(loads):
                dma(sp, slot_view(i), loads[i][0], s_slot[i % NSLOT], *after)

        def take():
            i = used[0]
            used[0] += 1
            return i, slot_view(i), (s_slot[i % NSLOT], 16 * (i // NSLOT + 1))

        def done(i, token):
            issue(i + NSLOT, token)

        free = [None] * 8
        turn = {"m": 0, "s": 0}

        def bank(kind):
            b = turn[kind] % 4 + (4 if kind == "s" else 0)
            turn[kind] += 1
            return b, banks[b], free[b]

        def group(o, pairs, *after, start=True, stop=True, tr=False):
            pe.wait(*after)
            tok = None
            for i, (l_, r_) in enumerate(pairs):
                last = i == len(pairs) - 1
                f = (lambda e, l_=l_, r_=r_, i=i, last=last:
                     e.matmul(o, l_, r_, start=start and i == 0, stop=stop and last))
                if last:
                    tok = pe(f)
                else:
                    pe.quiet(f)
            return tok

        def turnover(o, i_, *after):
            k = i_.shape[0]
            return pe(lambda e: e.transpose(o, i_, ident[0:k, 0:k]), *after)

        def vtt(o, i0, i1, op, *after, q=None):
            return (q or ve)(lambda e: e.tensor_tensor(o, i0, i1, op), *after)

        def vts(o, i0, s1, s2, o1, o2, *after, q=None):
            if s2 is None:
                return (q or ve)(lambda e: e.tensor_scalar(o, i0, s1, None, o1), *after)
            return (q or ve)(lambda e: e.tensor_scalar(o, i0, s1, s2, o1, o2), *after)

        def vst(o, i0, s_, i1, o1, o2, *after, q=None):
            return (q or ve)(lambda e: e.scalar_tensor_tensor(out=o, in0=i0, scalar=s_, in1=i1, op0=o1, op1=o2), *after)

        def vcp(o, i_, *after, q=None):
            return (q or ve)(lambda e: e.tensor_copy(o, i_), *after)

        def act(o, i_, f, *after, **kw):
            return ac(lambda e: e.activation(o, i_, f, **kw), *after)

        def half(n):
            return mhalf[:, :].to_broadcast([P, n])

        def bc(ap, shape, ax=1):
            return ap.unsqueeze(ax).to_broadcast(shape)

        dma(sp, x[:, :, :], a["x"][0].rearrange("(t p) d -> p t d", p=P), s_x)
        dma(sp, cst[:, :], a["consts"], s_c)
        dma(sp, par[:, :], a["params"], s_p)
        for i in range(NSLOT):
            issue(i)
        dma(ac, posi[:, :], a["pos"], s_pos)
        dma(ac, tab[:, :], a["t5_table_2"], s_tab)
        dma(ac, bufA[0:32, 0:512], a["onehot"], s_tab)
        dma(ac, gains, a["gains"], s_gn)
        GAIN = (s_gn, 16)
        CST, PAR, XIN = (s_c, 16), (s_p, 16), (s_x, 16)
        t_ones = ve(lambda e: e.memset(onesb[:, :], 1.0))
        t_mh = ve(lambda e: e.memset(mhalf[:, :], -0.5))
        z1 = ve(lambda e: e.memset(glup[:, :, 0:30], 0.0))
        z2 = ve(lambda e: e.memset(ccp[:, :, 0:2], 0.0))
        z3 = ve(lambda e: e.memset(gpad[:, :, :, 0:2], 0.0))

        t = vcp(posf[:, :], posi[:, :], (s_pos, 16))
        tt_ = None
        ang, kk, ki, r_ = rt[:, :, 0:24], rt[:, :, 24:48], rt[:, :, 48:72], rt[:, :, 72:96]
        tw = []
        for tb in range(2):
            tw.append(vts(ang[:, tb], con("invf"), posf[:, tb:tb + 1], None, ALU.mult, None, t, CST))
        MAGIC = 12582912.0
        TWO = [6.28125, 0.0019350051879882812, 3.019916050561733e-07, 2.0561020951390433e-14]
        assert abs(sum(TWO) - 2 * np.pi) < 1e-12
        for which in range(2):
            o = cs[:, :, 24 * which:24 * which + 24]
            t = vts(kk, ang, float(1 / (2 * np.pi)), 0.25 if which == 0 else 0.0, ALU.mult, ALU.add, tw, t)
            t = vts(kk, kk, MAGIC, -MAGIC, ALU.add, ALU.add, t)
            t = vts(ki, kk, 1 / 4096.0, MAGIC, ALU.mult, ALU.add, t)
            t = vts(ki, ki, -MAGIC, 4096.0, ALU.add, ALU.mult, t)
            t = vtt(kk, kk, ki, ALU.subtract, t)
            src = ang
            for c in TWO:
                t = vst(r_, ki, -c, src, ALU.mult, ALU.add, t)
                t = vst(r_, kk, -c, r_, ALU.mult, ALU.add, t)
                src = r_
            if which == 0:
                t = vts(r_, r_, float(np.pi / 2), None, ALU.add, None, t)
            t = vts(r_, r_, 3.1415925, -3.1415925, ALU.min, ALU.max, t)
            t = act(o, r_, ACT.Sin, t)
        t_cs = t

        b, bk, _ = bank("s")
        t = group(bk[0:4, 0:512], [(tab[:, :], bufA[0:32, 0:512])], (s_tab, 32))
        t = vcp(two[0:4, 6144:6656], bk[0:4, :], t)
        free[b] = t
        dma(ac, a["scratch"], two[0:4, 6144:6656], s_sc, t)

        def normed_T(layer, gname, t_x):
            ts = []
            for tb in range(2):
                ts.append(act(xn[:, tb], x[:, tb], ACT.Square, t_x, accum_out=st[:, tb:tb + 1]))
            t = vts(st[:, 2:4], st[:, 0:2], 1.0 / D, 1e-6, ALU.mult, ALU.add, ts)
            t = vtt(st[:, 4:6], st[:, 2:4], half(2), ALU.pow, t, t_mh, q=po)
            tn = [vts(xn[:, tb], x[:, tb], st[:, 4 + tb:5 + tb], None, ALU.mult, None, t) for tb in range(2)]
            outs = []
            for c in range(0, 8, 2):
                b, bk, fr = bank("m")
                for j in range(2):
                    for tb in range(2):
                        tk = turnover(bk[:, j * S + tb * P:j * S + tb * P + P],
                                      xn[:, tb, (c + j) * P:(c + j + 1) * P], tn[tb], fr, CST)
                r = []
                for j in range(2):
                    g = prm(gname, layer, c + j, c + j + 1)
                    if c % 4 == 0:
                        r.append(act(hT[:, c + j], bk[:, j * S:j * S + S], ACT.Copy, tk, PAR, scale=g))
                    else:
                        r.append(vts(hT[:, c + j], bk[:, j * S:j * S + S], g, None, ALU.mult, None, tk, PAR))
                free[b] = r
                outs += r
            return outs

        def tok_major(i, w, tw_, tb, n, src, t_src, kk_=8):
            b, bk, fr = bank("m")
            t = group(bk[:, 0:n], [(src[:, k, tb * P:tb * P + P], w[:, k, 0:n]) for k in range(kk_)],
                      tw_, t_src, fr)
            return b, bk, t

        def chan_major(w, tw_, c, n, src, t_src, kk_=8):
            b, bk, fr = bank("m")
            for j in range(n):
                t = group(bk[:, j * S:j * S + S],
                          [(w[:, k, (c + j) * P:(c + j + 1) * P], src[:, k, :]) for k in range(kk_)],
                          tw_, t_src, fr)
            return b, bk, t

        def rope(v, nh, half, cos, sin, tmp, t):
            x1, x2 = v[:, :, 0:half], v[:, :, half:2 * half]
            c, s_ = bc(cos, [P, nh, half]), bc(sin, [P, nh, half])
            ts = [vtt(tmp[:, 0], x1, c, ALU.mult, t), vtt(tmp[:, 1], x2, s_, ALU.mult, t),
                  vtt(tmp[:, 2], x2, c, ALU.mult, t), vtt(tmp[:, 3], x1, s_, ALU.mult, t)]
            vtt(x1, tmp[:, 0], tmp[:, 1], ALU.subtract, ts)
            return vtt(x2, tmp[:, 2], tmp[:, 3], ALU.add, ts)

        war_pt = [None, None]

        def attend(lg, qT, kT, V, t_in, t_v, scale, mask, t_mask, outp, so, rowtiles=False):
            marks = []
            for tb in range(2):
                nk = P * (tb + 1)
                g = lg[tb].rearrange("p (h k) -> p h k", h=4)[:, :, 0:nk]
                tl = []
                for hp in range(2):
                    b, bk, fr = bank("s")
                    for j in range(2):
                        h = hp + 2 * j if rowtiles else 2 * hp + j
                        t = group(bk[:, j * nk:(j + 1) * nk], [(qT(h, tb), kT(h, 0, nk))], t_in, fr)
                    src = bk[:, 0:2 * nk].rearrange("p (h k) -> p h k", h=2)
                    hs = slice(hp, hp + 3, 2) if rowtiles else slice(2 * hp, 2 * hp + 2)
                    t = vst(g[:, hs], src, scale, mask(tb, hp), ALU.mult, ALU.add, t, t_mask)
                    free[b] = t
                    tl.append(t)
                s0 = so + 16 * tb
                t = ve(lambda e, g=g, s0=s0: e.tensor_reduce(st[:, s0:s0 + 4], g, AX.X, ALU.max, negate=True), tl)
                te = [act(g[:, h], g[:, h], ACT.Exp, t, bias=st[:, s0 + h:s0 + h + 1],
                          accum_out=st[:, s0 + 4 + h:s0 + 5 + h]) for h in range(4)]
                t = ve(lambda e, s0=s0: e.reciprocal(st[:, s0 + 8:s0 + 12], st[:, s0 + 4:s0 + 8]), te)
                t = vtt(g, g, bc(st[:, s0 + 8:s0 + 12], [P, 4, nk], 2), ALU.mult, t)
                marks.append(t)
                yield
            tp = [[], []]
            for tb in range(2):
                g = lg[tb].rearrange("p (h k) -> p h k", h=4)
                for kb in range(tb + 1):
                    b, bk, fr = bank("s")
                    for h in range(4):
                        t = turnover(bk[:, h * P:h * P + P], g[:, h, kb * P:kb * P + P], marks[tb], fr)
                    dst = pt[tb][kb].rearrange("p h k -> p (h k)")
                    if kb == 0:
                        t = act(dst, bk[:, :], ACT.Copy, t, war_pt[tb])
                    else:
                        t = vcp(dst, bk[:, :], t, war_pt[tb])
                    free[b] = t
                    tp[tb].append(t)
            yield
            for tb in range(2):
                b, bk, fr = bank("s")
                t = outp(tb, bk, lambda h, kb: (V(h, kb), pt[tb][kb][:, h, :]), tb + 1,
                         [tp[tb], t_v, fr])
                war_pt[tb] = t[0]
                free[b] = t[1]
            yield

        def tick(sides, n=1):
            for _ in range(n):
                if sides:
                    g = sides.pop(0)
                    try:
                        next(g)
                        sides.append(g)
                    except StopIteration:
                        pass

        def drain(sides):
            while sides:
                tick(sides)

        def block1(l, t_x):
            t_h = normed_T(l, "g_mix", t_x)
            res = {}
            sides = []
            gates = big[:, :].rearrange("p (c s) -> p c s", s=S)
            qk = [bufA[:, :].rearrange("p (h d) -> p h d", h=8), bufB[:, :].rearrange("p (h d) -> p h d", h=8)]
            vA = bufC[:, :].rearrange("p (t n) -> p t n", t=2)
            qkT = xn[:, :, :].rearrange("p t n -> p (t n)").rearrange("p (h s) -> p h s", s=S)
            sqT = bufD[:, :].rearrange("p (h s) -> p h s", s=S)
            skT = bufE[:, :].rearrange("p (h s) -> p h s", s=S)
            sv = bufF[:, :].rearrange("p (t n) -> p t n", t=2)
            cacc = bufG[:, :].rearrange("p (c s) -> p c s", s=S)
            gbS = bufH[:, :].rearrange("p (c s) -> p c s", s=S)
            yc = bufI[:, :].rearrange("p (c s) -> p c s", s=S)
            yaT = bufD
            lgs = [bufA[:, :], bufB[:, :]]

            i, w, tw_ = take()
            ti = []
            for tb in range(2):
                b, bk, t = tok_major(i, w, tw_, tb, 324, hT, t_h)
                e_ = act(ibuf[:, tb], bk[:, 0:324], ACT.Copy, t)
                free[b] = e_
                ti.append(e_)
            done(i, t)

            mk = mer[:, 6:8, :]
            wk = mer[:, 4:6, :]
            rl = mer[:, 0:4, :]

            def indexer():
                tr_ = []
                for tb in range(2):
                    kx = ibuf[:, tb, 256:320]
                    s0 = 16 + 2 * tb
                    t = act(sgb[:, tb, 0:64], kx, ACT.Square, ti[tb], accum_out=st[:, s0:s0 + 1])
                    t = vts(st[:, s0:s0 + 1], st[:, s0:s0 + 1], 1.0 / 64, 1e-6, ALU.mult, ALU.add, t)
                    t = vtt(st[:, s0 + 1:s0 + 2], st[:, s0:s0 + 1], half(1), ALU.pow, t, q=po)
                    t = vst(kx, kx, st[:, s0 + 1:s0 + 2], row("g_ki", l), ALU.mult, ALU.mult, t, GAIN)
                    v = ibuf[:, tb, 0:320].rearrange("p (h d) -> p h d", h=5)
                    tmp = sgb[:, tb, 0:160].rearrange("p (a h d) -> p a h d", a=4, h=5)
                    tr_.append(rope(v, 5, 8, cs[:, tb, 16:24], cs[:, tb, 40:48], tmp, [t, t_cs]))
                yield
                te = []
                for tb in range(2):
                    for hh, n in ((0, 4), (4, 1)):
                        b, bk, fr = bank("s")
                        for h in range(hh, hh + n):
                            t = turnover(bk[0:64, (h - hh) * P:(h - hh) * P + P],
                                         ibuf[:, tb, h * 64:h * 64 + 64], tr_[tb], fr)
                        t = act(iT[:, hh:hh + n, tb * P:tb * P + P],
                                bk[0:64, 0:n * P].rearrange("p (h k) -> p h k", h=n), ACT.Copy, t)
                        free[b] = t
                        te.append(t)
                yield
                for tb in range(2):
                    nk = P * (tb + 1)
                    tl = []
                    for hp in range(2):
                        b, bk, fr = bank("s")
                        for j in range(2):
                            h = 2 * hp + j
                            t = group(bk[:, j * nk:(j + 1) * nk],
                                      [(iT[:, h, tb * P:tb * P + P], iT[:, 4, 0:nk])], te, fr)
                        r = []
                        for j in range(2):
                            h = 2 * hp + j
                            r.append(vts(rl[:, h, 0:nk], bk[:, j * nk:(j + 1) * nk], 0.0,
                                         ibuf[:, tb, 320 + h:321 + h], ALU.max, ALU.mult, t))
                        free[b] = r
                        tl += r
                    t = vtt(rl[:, 0, 0:nk], rl[:, 0, 0:nk], rl[:, 1, 0:nk], ALU.add, tl)
                    t = vtt(rl[:, 0, 0:nk], rl[:, 0, 0:nk], rl[:, 2, 0:nk], ALU.add, t)
                    t = vtt(wk[:, tb, 0:nk], rl[:, 0, 0:nk], rl[:, 3, 0:nk], ALU.add, t)
                    t = vtt(wk[:, tb, nk - P:nk], wk[:, tb, nk - P:nk], con("causal"), ALU.add, t)
                    yield
                    for r in range(8):
                        s0 = 32 + 8 * tb
                        src = wk[:, tb, 0:nk]
                        t = ve(lambda e, s0=s0, src=src: e.max(st[:, s0:s0 + 8], src), t)
                        t = ve(lambda e, s0=s0, src=src: e.match_replace(src, st[:, s0:s0 + 8], src, PICKED), t)
                        if r == 3:
                            yield
                    t = vts(mk[:, tb, 0:nk], wk[:, tb, 0:nk], -2e38, NEG, ALU.is_gt, ALU.mult, t)
                    t = vtt(mk[:, tb, nk - P:nk], mk[:, tb, nk - P:nk], con("causal"), ALU.add, t)
                    res["mask", tb] = t
                    yield

            sides.append(indexer())

            tq = [[], []]
            for part in range(2):
                i, w, tw_ = take()
                for tb in range(2):
                    b, bk, t = tok_major(i, w, tw_, tb, 512, hT, t_h)
                    e_ = act(qk[tb][:, 4 * part:4 * part + 4].rearrange("p h d -> p (h d)"), bk[:, :], ACT.Copy, t)
                    free[b] = e_
                    tq[tb].append(e_)
                    tick(sides)
                done(i, t)
            i, w, tw_ = take()
            for tb in range(2):
                b, bk, t = tok_major(i, w, tw_, tb, 512, hT, t_h)
                t_vA = act(vA[:, tb], bk[:, :], ACT.Copy, t)
                free[b] = t_vA
                tick(sides)
            done(i, t)

            def sparse():
                trs = []
                for tb in range(2):
                    v = qk[tb]
                    sq = mer[:, 0:4, :].rearrange("p c s -> p (c s)").rearrange("p (h d) -> p h d", h=8)
                    sq = gpsq = big[:, 24 * S:28 * S].rearrange("p (h d) -> p h d", h=8) if tb == 0 else \
                        big[:, 28 * S:32 * S].rearrange("p (h d) -> p h d", h=8)
                    t = act(sq, v, ACT.Square, tq[tb])
                    s0 = 48 + 24 * tb
                    t = ve(lambda e, s0=s0, sq=sq: e.tensor_reduce(st[:, s0:s0 + 8], sq, AX.X, ALU.add), t)
                    t = vts(st[:, s0:s0 + 8], st[:, s0:s0 + 8], 1.0 / 128, 1e-6, ALU.mult, ALU.add, t)
                    t = vtt(st[:, s0 + 8:s0 + 16], st[:, s0:s0 + 8], half(8), ALU.pow, t, q=po)
                    t = vtt(v, v, bc(st[:, s0 + 8:s0 + 16], [P, 8, P], 2), ALU.mult, t)
                    vtt(v[:, 0:4], v[:, 0:4], bc(row("g_q", l), [P, 4, P]), ALU.mult, t, GAIN)
                    t = vtt(v[:, 4:8], v[:, 4:8], bc(row("g_k", l), [P, 4, P]), ALU.mult, t, GAIN)
                    tmp = sq.rearrange("p h d -> p (h d)")[:, 0:512].rearrange("p (a h d) -> p a h d", a=4, h=8)
                    trs.append(rope(v, 8, 16, cs[:, tb, 0:16], cs[:, tb, 24:40], tmp, [t, t_cs]))
                    yield
                res["squares"] = trs
                te = []
                for tb in range(2):
                    for hh in (0, 4):
                        b, bk, fr = bank("s")
                        for h in range(4):
                            t = turnover(bk[:, h * P:h * P + P], qk[tb][:, hh + h, :], trs[tb], fr)
                        t = act(qkT[:, hh:hh + 4, tb * P:tb * P + P],
                                bk[:, :].rearrange("p (h k) -> p h k", h=4), ACT.Copy, t)
                        free[b] = t
                        te.append(t)
                    yield
                while ("mask", 1) not in res or "sb_done" not in res:
                    yield

                def outp(tb, bk, pr, nkb, aft):
                    for h in range(4):
                        t = group(bk[:, h * P:h * P + P], [pr(h, kb) for kb in range(nkb)], aft)
                    e_ = act(yaT[:, :].rearrange("p (h s) -> p h s", s=S)[:, :, tb * P:tb * P + P],
                             bk[:, :].rearrange("p (h k) -> p h k", h=4), ACT.Copy, t, res["sb_done"])
                    res["ya", tb] = e_
                    return t, e_

                yield from attend(lgs, lambda h, tb: qkT[:, h, tb * P:tb * P + P],
                                  lambda h, k0, k1: qkT[:, 4 + h, k0:k1],
                                  lambda h, kb: vA[:, kb, h * P:h * P + P], te, t_vA, float(P) ** -0.5,
                                  lambda tb, hp: bc(mk[:, tb, 0:P * (tb + 1)], [P, 2, P * (tb + 1)]),
                                  [res["mask", 0], res["mask", 1]], outp, 96)

            sides.append(sparse())

            ia, wa, twa = take()
            ib, wb, twb = take()
            tg = []
            for p_ in range(2):
                bA, bkA, tA = chan_major(wa, twa, 2 * p_, 2, hT, t_h)
                bB, bkB, tB = chan_major(wb, twb, 2 * p_, 2, hT, t_h)
                t = act(sgb[:, p_], bkB[:, :], ACT.Sigmoid, tB, res.get("x"))
                free[bB] = t
                t = vtt(glup[:, 2 * p_:2 * p_ + 2, 30:286], bkA[:, :].rearrange("p (c s) -> p c s", c=2),
                        sgb[:, p_].rearrange("p (c s) -> p c s", c=2), ALU.mult, tA, t)
                free[bA] = t
                tg.append(t)
                tick(sides, 2)
            done(ia, tA)
            done(ib, tB)

            def conv_branch():
                last = [None] * 4
                for j in range(31):
                    for c in range(4):
                        q = ve
                        wv = prm("cb_w", l, c * 31 + j, c * 31 + j + 1)
                        if j == 0:
                            last[c] = vts(cacc[:, c], glup[:, c, 0:S], wv, prm("cb_b", l, c, c + 1),
                                          ALU.mult, ALU.add, tg, PAR, z1, q=q)
                        else:
                            last[c] = vst(cacc[:, c], glup[:, c, j:j + S], wv, cacc[:, c], ALU.mult, ALU.add,
                                          last[c], q=q)
                    if j % 3 == 2:
                        yield
                b, bk, fr = bank("s")
                t = group(bk[:, 0:S], [(onesb[:, :], cacc[:, c]) for c in range(4)], last, fr, t_ones)
                t = vst(cacc, bc(bk[:, 0:S], [P, 4, S]), -1.0 / 512, cacc, ALU.mult, ALU.add, t)
                free[b] = t
                sq = bufJ[:, :].rearrange("p (c s) -> p c s", s=S)
                t = act(sq, cacc, ACT.Square, t)
                yield
                b, bk, fr = bank("s")
                t = group(bk[:, 0:S], [(onesb[:, :], sq[:, c]) for c in range(4)], t, fr)
                t = vts(sgb[:, 0, 0:S], bk[:, 0:S], 1.0 / 512, 1e-6, ALU.mult, ALU.add, t)
                free[b] = t
                t = vtt(sgb[:, 0, S:512], sgb[:, 0, 0:S], half(S), ALU.pow, t, q=po)
                t = vtt(cacc, cacc, bc(sgb[:, 0, S:512], [P, 4, S]), ALU.mult, t)
                yield
                ts = [act(sq[:, c], cacc[:, c], ACT.Sigmoid, t, scale=prm("ln_g", l, c, c + 1),
                          bias=prm("ln_b", l, c, c + 1)) for c in range(4)]
                tz = [vts(cacc[:, c], cacc[:, c], prm("ln_g", l, c, c + 1), prm("ln_b", l, c, c + 1),
                          ALU.mult, ALU.add, ts) for c in range(4)]
                res["yb"] = vtt(cacc, cacc, sq, ALU.mult, tz)
                yield

            sides.append(conv_branch())

            ig, wg, twg = take()
            ix, wx, twx = take()
            tc_ = []
            for p_ in range(2):
                bA, bkA, tA = chan_major(wg, twg, 2 * p_, 2, hT, t_h)
                bB, bkB, tB = chan_major(wx, twx, 2 * p_, 2, hT, t_h)
                tmp = bufI[:, p_ * 512:(p_ + 1) * 512]
                t = act(tmp, bkA[:, :], ACT.Copy, tA)
                free[bA] = t
                t = vtt(ccp[:, 2 * p_:2 * p_ + 2, 2:258], bkB[:, :].rearrange("p (c s) -> p c s", c=2),
                        tmp.rearrange("p (c s) -> p c s", c=2), ALU.mult, tB, t)
                free[bB] = t
                tc_.append(t)
                tick(sides, 2)
            done(ig, tA)
            done(ix, tB)
            ig, wg, twg = take()
            tb_ = []
            for p_ in range(2):
                bA, bkA, tA = chan_major(wg, twg, 2 * p_, 2, hT, t_h)
                t = act(gbS[:, 2 * p_:2 * p_ + 2].rearrange("p c s -> p (c s)"), bkA[:, :], ACT.Copy, tA)
                free[bA] = t
                tb_.append(t)
                tick(sides, 2)
            done(ig, tA)

            def short_branch():
                for j in range(3):
                    for c in range(4):
                        wv = prm("cc_w", l, c * 3 + j, c * 3 + j + 1)
                        if j == 0:
                            t = vts(yc[:, c], ccp[:, c, 0:S], wv, None, ALU.mult, None, tc_, PAR, z2)
                        else:
                            t = vst(yc[:, c], ccp[:, c, j:j + S], wv, yc[:, c], ALU.mult, ALU.add, t)
                    yield
                res["yc"] = vtt(yc, yc, gbS, ALU.mult, t, tb_)
                yield

            sides.append(short_branch())

            i, w, tw_ = take()
            tsq = []
            for p_ in range(2):
                b, bk, t = chan_major(w, tw_, 2 * p_, 2, hT, t_h)
                e_ = act(sqT[:, 2 * p_:2 * p_ + 2].rearrange("p c s -> p (c s)"), bk[:, :], ACT.Copy, t,
                         scale=float(P) ** -0.5)
                free[b] = e_
                tsq.append(e_)
                tick(sides, 2)
            done(i, t)
            i, w, tw_ = take()
            for p_ in range(2):
                b, bk, t = chan_major(w, tw_, 2 * p_, 2, hT, t_h)
                e_ = act(skT[:, 2 * p_:2 * p_ + 2].rearrange("p c s -> p (c s)"), bk[:, :], ACT.Copy, t)
                free[b] = e_
                tsq.append(e_)
                tick(sides, 2)
            done(i, t)
            i, w, tw_ = take()
            for tb in range(2):
                b, bk, t = tok_major(i, w, tw_, tb, 512, hT, t_h)
                e_ = act(sv[:, tb], bk[:, :], ACT.Copy, t)
                free[b] = e_
                tsq.append(e_)
                tick(sides, 2)
            done(i, t)

            lk = mer2 = None
            lkb = [bufH, bufJ]

            def stick():
                while "yc" not in res or "yb" not in res:
                    yield
                lk0 = bufJ[:, :].rearrange("p (h s) -> p h s", s=S)
                lk1 = bufH[:, 0:512].rearrange("p (h s) -> p h s", s=P)
                tls = []
                for g in range(3):
                    b, bk, fr = bank("s")
                    if g < 2:
                        for j in range(2):
                            h = 2 * g + j
                            t = group(bk[:, j * S:j * S + S], [(skT[:, h, 0:P], sqT[:, h, :])], tsq, fr)
                        dst, m = lk0[:, 2 * g:2 * g + 2].rearrange("p c s -> p (c s)"), bc(con("m0"), [P, 2, S])
                        shp = dict(c=2)
                    else:
                        for h in range(4):
                            t = group(bk[:, h * P:h * P + P], [(skT[:, h, P:S], sqT[:, h, P:S])], tsq, fr)
                        dst, m = lk1.rearrange("p c s -> p (c s)"), bc(con("m0", 0, P), [P, 4, P])
                        shp = dict(c=4)
                    t = act(dst, bk[:, :], ACT.Abs, t, res["yb"], res["yc"])
                    t = act(dst, dst, ACT.Exp, t, scale=-1.0)
                    t = act(dst, dst, ACT.Ln, t, bias=1.0)
                    t = vst(dst, bk[:, :], 0.0, dst, ALU.max, ALU.add, t)
                    free[b] = t
                    d3 = dst.rearrange("p (c s) -> p c s", **shp)
                    tls.append(vtt(d3, d3, m, ALU.mult, t))
                    yield
                a0 = bufJ[:, :].rearrange("p (h s) -> p h s", s=S)
                a1 = bufH[:, 0:512].rearrange("p (h s) -> p h s", s=P)
                tas = []
                hold = []
                for g in range(2):
                    b, bk, fr = bank("s")
                    for j in range(2):
                        h = 2 * g + j
                        o = bk[:, j * S:j * S + S]
                        group(o, [(con("trirev"), lk0[:, h]), (skT[:, h, 0:P], sqT[:, h, :])], tls, fr, stop=False)
                        t = group(bk[:, j * S + P:j * S + S], [(onesb[:, :], lk1[:, h])], start=False)
                    hold.append((b, bk, t))
                b, bk, fr = bank("s")
                for h in range(4):
                    t = group(bk[:, h * P:h * P + P], [(con("trirev"), lk1[:, h]),
                                                       (skT[:, h, P:S], sqT[:, h, P:S])], fr)
                hold.append((b, bk, t))
                for g, (b, bk, t1) in enumerate(hold):
                    if g < 2:
                        dst, m, n = a0[:, 2 * g:2 * g + 2], bc(con("n0"), [P, 2, S]), 2
                    else:
                        dst, m, n = a1, bc(con("n0", 0, P), [P, 4, P]), 4
                    t = vst(dst, bk[:, :].rearrange("p (c s) -> p c s", c=n), 0.0, m, ALU.min, ALU.add, t)
                    free[b] = t
                    tas.append(act(dst, dst, ACT.Exp, t))
                yield
                for g in range(2):
                    b, bk, fr = bank("s")
                    for j in range(2):
                        h = 2 * g + j
                        group(bk[:, j * S:j * S + S], [(sv[:, 0, h * P:h * P + P], a0[:, h])], tas, fr, stop=False)
                        t = group(bk[:, j * S + P:j * S + S], [(sv[:, 1, h * P:h * P + P], a1[:, h])], start=False)
                    t = act(skT[:, 2 * g:2 * g + 2].rearrange("p c s -> p (c s)"), bk[:, :], ACT.Copy, t)
                    free[b] = t
                res["yd"] = res["sb_done"] = t
                yield

            sides.append(stick())

            tgt = []
            for gi in range(8):
                i, w, tw_ = take()
                for p_ in range(2):
                    b, bk, t = chan_major(w, tw_, 2 * p_, 2, hT, t_h)
                    for j in range(2):
                        c = 4 * gi + 2 * p_ + j
                        aft = res["squares"] if c >= 24 else None
                        e_ = act(gates[:, c], bk[:, j * S:j * S + S], ACT.Sigmoid, t, PAR, aft, bias=prm("b_gate", l, c, c + 1))
                    free[b] = e_
                    tick(sides, 3)
                done(i, t)
            t_gates = e_
            prev = [None] * 4

            def branch(bi, src, t_src, first):
                i, w, tw_ = take()
                for p_ in range(4):
                    b, bk, t = chan_major(w, tw_, 2 * p_, 2, src, t_src, 4)
                    m2 = mer[:, 2 * p_:2 * p_ + 2].rearrange("p c s -> p (c s)")
                    g2 = gates[:, 8 * bi + 2 * p_:8 * bi + 2 * p_ + 2].rearrange("p c s -> p (c s)")
                    if first:
                        prev[p_] = vtt(m2, bk[:, :], g2, ALU.mult, t, t_gates, res["mask", 1])
                        free[b] = prev[p_]
                    else:
                        tm = vtt(g2, bk[:, :], g2, ALU.mult, t)
                        free[b] = tm
                        prev[p_] = vtt(m2, m2, g2, ALU.add, tm, prev[p_])
                done(i, t)

            drain(sides)
            branch(1, cacc, res["yb"], True)
            branch(2, yc, res["yc"], False)
            branch(3, skT, res["yd"], False)
            branch(0, yaT[:, :].rearrange("p (h s) -> p h s", s=S), [res["ya", 0], res["ya", 1]], False)
            t_x = row_out([mer], prev, 2, [4, 4], t_x)

            t_h = normed_T(l, "g_ffn", t_x)
            ffa = big[:, 0:22 * S].rearrange("p (c s) -> p c s", s=S)
            lastu = [None, None]
            tf = []
            n_ = 0
            for i6 in range(6):
                ig, wg, twg = take()
                iu, wu, twu = take()
                for p_ in range(2 if i6 < 5 else 1):
                    bG, bkG, tG = chan_major(wg, twg, 2 * p_, 2, hT, t_h)
                    bU, bkU, tU = chan_major(wu, twu, 2 * p_, 2, hT, t_h)
                    r = n_ % 2
                    n_ += 1
                    gp = gpad[:, r]
                    t = act(gp[:, :, 2:258], bkG[:, :].rearrange("p (c s) -> p c s", c=2), ACT.Copy, tG,
                            lastu[r], z3)
                    free[bG] = t
                    y = bufA[:, r * 512:r * 512 + 512].rearrange("p (c s) -> p c s", c=2)
                    sg = bufB[:, r * 512:r * 512 + 512].rearrange("p (c s) -> p c s", c=2)
                    tt2 = [t, t]
                    for k3 in range(3):
                        for j in range(2):
                            c = 4 * i6 + 2 * p_ + j
                            wv = prm("ffn_w", l, c * 3 + k3, c * 3 + k3 + 1)
                            if k3 == 0:
                                tt2[j] = vts(y[:, j], gp[:, j, 0:S], wv, None, ALU.mult, None, tt2[j], PAR)
                            else:
                                tt2[j] = vst(y[:, j], gp[:, j, k3:k3 + S], wv, y[:, j], ALU.mult, ALU.add, tt2[j])
                    lastu[r] = list(tt2)
                    t = act(sg, y, ACT.Sigmoid, tt2)
                    t = vtt(y, y, sg, ALU.mult, t)
                    c = 4 * i6 + 2 * p_
                    t = vtt(ffa[:, c:c + 2], y, bkU[:, :].rearrange("p (c s) -> p c s", c=2), ALU.mult, t, tU)
                    free[bU] = t
                    tf.append(t)
                done(ig, tG)
                done(iu, tU)
            return row_out([ffa], tf, 6, [4] * 5 + [2], t_x)

        def row_out(srcs, t_src, nl, ks, t_x):
            src = srcs[0]
            hold = [bank("m") for _ in range(4)]
            k0 = 0
            for n, kc in enumerate(ks):
                i, w, tw_ = take()
                for q_, (b, bk, fr) in enumerate(hold):
                    tb, nh = q_ // 2, q_ % 2
                    t = group(bk[:, :], [(src[:, k0 + k, tb * P:tb * P + P], w[:, k, nh * 512:nh * 512 + 512])
                                         for k in range(kc)], tw_, t_src, fr,
                              start=n == 0, stop=n == nl - 1)
                    if n == nl - 1:
                        hold[q_] = (b, bk, t)
                done(i, t)
                k0 += kc
            for q_, (b, bk, t) in enumerate(hold):
                tb, nh = q_ // 2, q_ % 2
                xs = x[:, tb, nh * 512:nh * 512 + 512]
                t_x = vtt(xs, bk[:, :], xs, ALU.add, t)
                free[b] = t_x
            return t_x

        def bias_tiles(t_x):
            for h in range(4):
                dma(ac, big[:, h * S:(h + 1) * S], a["toep"][h], s_bi, (s_sc, 16), t_x)
            dma(ac, bufA[:, 0:128], a["flip"], s_fl)
            for h in range(4):
                b, bk, fr = bank("s")
                t = group(bk[:, 0:S], [(bufA[:, 0:128], big[:, h * S:(h + 1) * S])], (s_bi, 64), (s_fl, 16), fr)
                t = vcp(bia[:, h, :], bk[:, 0:S], t)
                free[b] = t
                t = vtt(bia[:, h, 128:256], bia[:, h, 128:256], con("causal"), ALU.add, t)
            return t

        t_bias = [None]

        def block2(l, t_x):
            if l == 0:
                t_bias[0] = bias_tiles(t_x)
            z4 = ve(lambda e: e.memset(gdp[:, :, :, 0:3], 0.0), t_x)
            dma(ac, wuq[:, :, :], a["mla_w_uq_2"][l].rearrange("(k p) n -> p k n", p=P), s_u, t_x)
            dma(ac, wukv[:, :], a["mla_w_ukv_2"][l], s_u)
            t_wu = (s_u, 32 * (l + 1))
            t_h = normed_T(l, "norm2", t_x)
            res = {}
            sides = []
            yT = mer
            m0 = xn[:, :, 0:416]
            mtmp = xn[:, :, 416:1024]

            i, w, tw_ = take()
            tm = []
            for tb in range(2):
                b, bk, t = tok_major(i, w, tw_, tb, 416, hT, t_h)
                e_ = act(m0[:, tb], bk[:, 0:416], ACT.Copy, t)
                free[b] = e_
                tm.append(e_)
            done(i, t)

            qm = [bufA[:, 0:384].rearrange("p (h d) -> p h d", h=4), bufB[:, 0:384].rearrange("p (h d) -> p h d", h=4)]
            km = [bufA[:, 384:768].rearrange("p (h d) -> p h d", h=4), bufB[:, 384:768].rearrange("p (h d) -> p h d", h=4)]
            vm = [bufA[:, 768:1024], bufB[:, 768:1024]]
            lgs = [bufC[:, :], bufD[:, :]]
            cqT = bufE[:, 0:512].rearrange("p (k s) -> p k s", k=2)
            ckT = bufE[:, 512:768]
            qmT = bufF[:, :].rearrange("p (h s) -> p h s", s=S)
            kmT = bufG[:, :].rearrange("p (h s) -> p h s", s=S)

            def latent():
                tn = []
                for tb in range(2):
                    s0 = 16 + 8 * tb
                    t1 = act(sgb[:, tb, 0:256], m0[:, tb, 0:256], ACT.Square, tm[tb], accum_out=st[:, s0:s0 + 1])
                    t2 = act(sgb[:, tb, 256:384], m0[:, tb, 256:384], ACT.Square, accum_out=st[:, s0 + 1:s0 + 2])
                    t1 = vts(st[:, s0:s0 + 1], st[:, s0:s0 + 1], 1.0 / 256, 1e-6, ALU.mult, ALU.add, t1)
                    t2 = vts(st[:, s0 + 1:s0 + 2], st[:, s0 + 1:s0 + 2], 1.0 / 128, 1e-6, ALU.mult, ALU.add, t2)
                    t = vtt(st[:, s0 + 2:s0 + 4], st[:, s0:s0 + 2], half(2), ALU.pow, [t1, t2], q=po)
                    vts(m0[:, tb, 0:256], m0[:, tb, 0:256], st[:, s0 + 2:s0 + 3], None, ALU.mult, None, t)
                    t = vts(m0[:, tb, 256:384], m0[:, tb, 256:384], st[:, s0 + 3:s0 + 4], None, ALU.mult, None, t)
                    tn.append(t)
                yield
                b, bk, fr = bank("s")
                for c in range(2):
                    for tb in range(2):
                        t = turnover(bk[:, c * S + tb * P:c * S + tb * P + P], m0[:, tb, c * P:c * P + P], tn[tb], fr)
                tc = [act(cqT[:, c], bk[:, c * S:c * S + S], ACT.Copy, t, scale=prm("qn2", l, c, c + 1))
                      for c in range(2)]
                free[b] = tc
                b, bk, fr = bank("s")
                for tb in range(2):
                    t = turnover(bk[:, tb * P:tb * P + P], m0[:, tb, 256:384], tn[tb], fr)
                tc.append(act(ckT, bk[:, 0:S], ACT.Copy, t, scale=prm("kvn2", l)))
                free[b] = tc[-1]
                yield
                tr_ = []
                for tb in range(2):
                    b, bk, fr = bank("s")
                    t = group(bk[:, 0:384], [(cqT[:, k, tb * P:tb * P + P], wuq[:, k]) for k in range(2)],
                              tc, t_wu, fr)
                    res["wu"] = t
                    t = vts(qm[tb].rearrange("p h d -> p (h d)"), bk[:, 0:384], float(96) ** -0.5, None,
                            ALU.mult, None, t)
                    free[b] = t
                    b, bk, fr = bank("s")
                    t2 = group(bk[:, :], [(ckT[:, tb * P:tb * P + P], wukv[:, :])], tc, fr)
                    res["wu"] = t2
                    kv = bk[:, :].rearrange("p (h d) -> p h d", h=4)
                    t3 = act(km[tb][:, :, 0:64], kv[:, :, 0:64], ACT.Copy, t2)
                    t4 = act(vm[tb].rearrange("p (h d) -> p h d", h=4), kv[:, :, 64:128], ACT.Copy, t2)
                    free[b] = t4
                    cos, sin = con("rope2", 32 * tb, 32 * tb + 16), con("rope2", 32 * tb + 16, 32 * tb + 32)
                    tmp = mtmp[:, tb, 0:256].rearrange("p (a h d) -> p a h d", a=4, h=4)
                    t = rope(qm[tb][:, :, 64:96], 4, 16, cos, sin, tmp, [t])
                    tmp = mtmp[:, tb, 256:320].rearrange("p (a h d) -> p a h d", a=4, h=1)
                    t5 = rope(m0[:, tb, 384:416].unsqueeze(1), 1, 16, cos, sin, tmp, [tm[tb]])
                    t5 = vcp(km[tb][:, :, 64:96], bc(m0[:, tb, 384:416], [P, 4, 32]), t5)
                    tr_.append([t, t3, t5])
                    res["vm"] = t4
                    yield
                te = []
                for tb in range(2):
                    for src, dst in ((qm[tb], qmT), (km[tb], kmT)):
                        b, bk, fr = bank("s")
                        for h in range(4):
                            t = turnover(bk[0:96, h * P:h * P + P], src[:, h, :], tr_[tb], fr)
                        t = act(dst[0:96, :, tb * P:tb * P + P],
                                bk[0:96, :].rearrange("p (h k) -> p h k", h=4), ACT.Copy, t)
                        free[b] = t
                        te.append(t)
                yield

                def mask(tb, hp):
                    return bc(mk0 if tb == 0 else mk1, [P, 2, P * (tb + 1)])

                mk0 = con("causal")
                zo = CN["zero"][0]
                mk1 = cst[:, zo:zo + S]
                yield from attend(lgs, lambda h, tb: qmT[0:96, h, tb * P:tb * P + P],
                                  lambda h, k0, k1: kmT[0:96, h, k0:k1],
                                  lambda h, kb: vm[kb][:, h * 64:h * 64 + 64], te, res["vm"], 1.0,
                                  mask, CST, pair_out("mla", 0, "mg"), 96)
                res["mla_done"] = True
                while "moba_in" not in res:
                    yield

                def mqT(h, tb):
                    return cq[64 * (h % 2):64 * (h % 2) + 64, h // 2, tb * P:tb * P + P]

                def mkT(h, k0, k1):
                    return ck[64 * (h % 2):64 * (h % 2) + 64, h // 2, k0:k1]

                def mask2(tb, hp):
                    return bia[:, hp:hp + 3:2, 128:256] if tb == 0 else bia[:, hp:hp + 3:2, :]

                yield from attend(lgs, mqT, mkT, lambda h, kb: cv[:, kb, h * 64:h * 64 + 64],
                                  res["moba_in"], res["cv"], 1.0, mask2, t_bias[0], pair_out("moba", 6, "cg"), 96,
                                  rowtiles=True)

            mgs = big[:, 0:2 * S].rearrange("p (c s) -> p c s", s=S)
            cgs = big[:, 2 * S:4 * S].rearrange("p (c s) -> p c s", s=S)
            gate_of = {"mg": mgs, "cg": cgs}

            def pair_out(name, c0, gname):
                def outp(tb, bk, pr, nkb, aft):
                    for h in range(4):
                        o = bk[64 * (h % 2):64 * (h % 2) + 64, (h // 2) * P:(h // 2) * P + P]
                        t = group(o, [pr(h, kb) for kb in range(nkb)], aft)
                    e_ = act(yT[:, c0:c0 + 2, tb * P:tb * P + P],
                             bk[:, 0:2 * P].rearrange("p (h k) -> p h k", h=2), ACT.Copy, t)
                    res[name, tb] = e_
                    return t, e_
                return outp

            sides.append(latent())

            zs = big[:, 4 * S:8 * S].rearrange("p (h s) -> p h s", s=S)
            qc = big[:, 8 * S:12 * S].rearrange("p (h s) -> p h s", s=S)
            kc = big[:, 12 * S:16 * S].rearrange("p (h s) -> p h s", s=S)
            vc = big[:, 16 * S:20 * S].rearrange("p (h s) -> p h s", s=S)
            i, w, tw_ = take()
            bg = st[:, 128:144].rearrange("p (t n) -> p t n", t=2)
            tbg = []
            for p_ in range(2):
                b, bk, t = chan_major(w, tw_, 2 * p_, 2, hT, t_h)
                t1 = act(bufI[:, p_ * 512:p_ * 512 + 512], bk[:, :], ACT.Sigmoid, t)
                t1 = vtt(zs[:, 2 * p_:2 * p_ + 2].rearrange("p c s -> p (c s)"), bk[:, :],
                         bufI[:, p_ * 512:p_ * 512 + 512], ALU.mult, t1)
                free[b] = t1
            res["zs"] = t1
            for tb in range(2):
                b, bk, fr = bank("m")
                t = group(bk[:, 0:8], [(hT[:, k, tb * P:tb * P + P], w[:, k, 512:520]) for k in range(8)], fr)
                tbg.append(vcp(bg[:, tb], bk[:, 0:8], t))
                free[b] = tbg[-1]
            done(i, t)
            tick(sides, 2)

            nst = [160]

            def cell(n):
                o = nst[0]
                nst[0] += n
                return st[:, o:o + n]

            beta = cell(8).rearrange("p (t h) -> p t h", t=2)
            gv = cell(8).rearrange("p (t h) -> p t h", t=2)
            gc = cell(8).rearrange("p (t h) -> p t h", t=2)
            ngc = cell(8).rearrange("p (t h) -> p t h", t=2)
            egc = cell(8).rearrange("p (t h) -> p t h", t=2)
            edl = cell(8).rearrange("p (t h) -> p t h", t=2)
            gend = cell(16).rearrange("p (t c h) -> p t c h", t=2, c=2)
            ss = cell(16).rearrange("p (q t h) -> p q t h", q=2, t=2)
            rs = cell(16).rearrange("p (q t h) -> p q t h", q=2, t=2)
            r1 = cell(8).rearrange("p (t h) -> p t h", t=2)
            r3 = cell(8).rearrange("p (t h) -> p t h", t=2)
            cw = cell(8).rearrange("p (t h) -> p t h", t=2)
            ckk = cell(8).rearrange("p (t h) -> p t h", t=2)
            ea = cell(4)
            t4a = cell(8).rearrange("p (t h) -> p t h", t=2)
            t4b = cell(8).rearrange("p (t h) -> p t h", t=2)
            assert nst[0] <= 512

            def decay_prep():
                t = act(beta, bg[:, :, 0:4], ACT.Sigmoid, tbg)
                ta = vtt(t4a, bg[:, :, 4:8], bc(prm("dtb", l), [P, 2, 4]), ALU.add, tbg)
                t1 = act(t4b, t4a, ACT.Abs, ta)
                t1 = act(t4b, t4b, ACT.Exp, t1, scale=-1.0)
                t1 = act(t4b, t4b, ACT.Ln, t1, bias=1.0)
                t2 = act(ea, prm("alog", l), ACT.Exp)
                t1 = vst(t4a, t4a, 0.0, t4b, ALU.max, ALU.add, t1, t2)
                t1 = vst(gv, t4a, -1.0, bc(ea, [P, 2, 4]), ALU.mult, ALU.mult, t1, t)
                yield
                b, bk, fr = bank("s")
                for tb in range(2):
                    t = group(bk[:, 16 * tb:16 * tb + 4], [(con("tri"), gv[:, tb])], t1, fr)
                    t = group(bk[:, 16 * tb + 4:16 * tb + 8], [(con("blk"), gv[:, tb])])
                    t = group(bk[:, 16 * tb + 8:16 * tb + 12], [(con("half0"), gv[:, tb])])
                    t = group(bk[:, 16 * tb + 12:16 * tb + 16], [(con("half1"), gv[:, tb])])
                v = bk[:, 0:32].rearrange("p (t n) -> p t n", t=2)
                t2 = vcp(gc, v[:, :, 0:4], t)
                t3 = vts(ngc, v[:, :, 0:4], -1.0, None, ALU.mult, None, t)
                t4 = vtt(edl, v[:, :, 4:8], gc, ALU.subtract, t2)
                t5 = act(gend.rearrange("p t c h -> p t (c h)"), v[:, :, 8:16], ACT.Exp, t3, t4)
                t6 = act(egc, gc, ACT.Exp, t2)
                t7 = act(edl, edl, ACT.Exp, t4)
                free[b] = [t4, t5]
                res["dec"] = [t3, t7]
                yield

            sides.append(decay_prep())

            nz = [0]
            lastg = [None, None]

            def conv4(dst, ci, tag):
                i, w, tw_ = take()
                for p_ in range(2):
                    b, bk, t = chan_major(w, tw_, 2 * p_, 2, hT, t_h)
                    r = nz[0] % 2
                    nz[0] += 1
                    t = act(gdp[:, r, :, 3:259], bk[:, :].rearrange("p (c s) -> p c s", c=2), ACT.Copy, t,
                            lastg[r], z4)
                    free[b] = t
                    tj = [t, t]
                    for k4 in range(4):
                        for j in range(2):
                            c = 2 * p_ + j
                            wv = prm("gdn_w", l, (ci + c) * 4 + k4, (ci + c) * 4 + k4 + 1)
                            if k4 == 0:
                                tj[j] = vts(dst[:, c], gdp[:, r, j, 0:S], wv, None, ALU.mult, None, tj[j])
                            else:
                                tj[j] = vst(dst[:, c], gdp[:, r, j, k4:k4 + S], wv, dst[:, c],
                                            ALU.mult, ALU.add, tj[j])
                    lastg[r] = list(tj)
                    tmp = bufI[:, p_ * 512:p_ * 512 + 512]
                    d2 = dst[:, 2 * p_:2 * p_ + 2].rearrange("p c s -> p (c s)")
                    t1 = act(tmp, d2, ACT.Sigmoid, tj, res.get("silu"))
                    t1 = vtt(d2, d2, tmp, ALU.mult, t1)
                    res["silu"] = t1
                    res[tag] = t1
                    tick(sides)
                done(i, t)

            conv4(kc, 4, "kc")
            conv4(qc, 0, "qc")
            conv4(vc, 8, "vc")

            ktk = big[:, 20 * S:24 * S].rearrange("p (t n) -> p t n", t=2)
            ke = big[:, 24 * S:28 * S].rearrange("p (t n) -> p t n", t=2)
            vb = big[:, 28 * S:32 * S].rearrange("p (t n) -> p t n", t=2)
            Dm = bufH[:, :].rearrange("p (t n) -> p t n", t=2)
            LT = bufI[:, :].rearrange("p (t n) -> p t n", t=2)
            AT = bufJ[:, :].rearrange("p (t n) -> p t n", t=2)
            qg = vc
            TT = [gx[:, 0], gx[:, 1]]
            T_ = [gx[:, 2], gx[:, 3]]
            BT = [gx[:, 4], gx[:, 5]]
            Mm = [gx[:, 6], gx[:, 7]]
            WT = kc
            U = qc
            Ut = U.rearrange("p h s -> p (h s)").rearrange("p (t n) -> p t n", t=2)
            Sst = gs

            def delta():
                t1 = act(LT.rearrange("p t n -> p (t n)"), kc.rearrange("p h s -> p (h s)"), ACT.Square,
                         res["kc"], res["silu"])
                t2 = act(AT.rearrange("p t n -> p (t n)"), qc.rearrange("p h s -> p (h s)"), ACT.Square, res["qc"])
                b, bk, fr = bank("s")
                for q_, src in ((0, LT), (1, AT)):
                    sv_ = src.rearrange("p t n -> p (t n)").rearrange("p (h s) -> p h s", s=S)
                    for tb in range(2):
                        for h in range(4):
                            c = q_ * 8 + tb * 4 + h
                            t = group(bk[:, c:c + 1], [(sv_[:, h, tb * P:tb * P + P], onesb[:, 0:1])], t1, t2, fr)
                t = vts(ss.rearrange("p q t h -> p (q t h)"), bk[:, 0:16], 1e-6, None, ALU.add, None, t)
                free[b] = t
                t = vtt(rs.rearrange("p q t h -> p (q t h)"), ss.rearrange("p q t h -> p (q t h)"),
                        half(16), ALU.pow, t, q=po)
                tq_ = vts(rs[:, 1], rs[:, 1], float(P) ** -0.5, None, ALU.mult, None, t)
                t1 = vtt(r1, rs[:, 0], beta, ALU.mult, t, res["dec"])
                t3 = vtt(r3, rs[:, 1], egc, ALU.mult, tq_)
                t4 = vst(cw, r1, -1.0, egc, ALU.mult, ALU.mult, t1)
                t5 = vtt(ckk, rs[:, 0], edl, ALU.mult, t)
                yield
                tt3 = []
                for tb in range(2):
                    b, bk, fr = bank("s")
                    for h in range(4):
                        t = turnover(bk[:, h * P:h * P + P], kc[:, h, tb * P:tb * P + P], fr, res["kc"])
                    v3 = bk[:, :].rearrange("p (h d) -> p h d", h=4)
                    ta = vtt(ktk[:, tb].rearrange("p (h d) -> p h d", h=4), v3, bc(cw[:, tb], [P, 4, P], 2),
                             ALU.mult, t, t4)
                    tb_2 = vtt(ke[:, tb].rearrange("p (h d) -> p h d", h=4), v3, bc(ckk[:, tb], [P, 4, P], 2),
                               ALU.mult, t, t5)
                    free[b] = tb_2
                    b, bk, fr = bank("s")
                    for h in range(4):
                        t = turnover(bk[:, h * P:h * P + P], vc[:, h, tb * P:tb * P + P], fr, res["vc"])
                    v3 = bk[:, :].rearrange("p (h d) -> p h d", h=4)
                    tc = vtt(vb[:, tb].rearrange("p (h d) -> p h d", h=4), v3, bc(beta[:, tb], [P, 4, P], 2),
                             ALU.mult, t)
                    free[b] = tc
                    tt3.append(tc)
                    yield
                for tb in range(2):
                    pr_ = []
                    for vec, mat, dst in ((gv, con("tri"), 0), (r1, ident, 1), (rs[:, 1], ident, 2), (r3, ident, 3)):
                        b, bk, fr = bank("s")
                        for h in range(4):
                            t = group(bk[:, h * P:h * P + P], [(vec[:, tb, h:h + 1].to_broadcast([P, P]), mat)],
                                      t1, t3, tq_, fr)
                        if dst == 0:
                            for h in range(4):
                                tt = vts(Dm[:, tb, h * P:h * P + P], bk[:, h * P:h * P + P], ngc[:, tb, h:h + 1], 0.0,
                                         ALU.add, ALU.min, t)
                            free[b] = tt
                            tt = act(Dm[:, tb], Dm[:, tb], ACT.Exp, tt)
                            td = vtt(Dm[:, tb].rearrange("p (h d) -> p h d", h=4),
                                     Dm[:, tb].rearrange("p (h d) -> p h d", h=4),
                                     bc(con("tri"), [P, 4, P]), ALU.mult, tt)
                        elif dst == 1:
                            tD1 = vtt(LT[:, tb], Dm[:, tb], bk[:, :], ALU.mult, t, td)
                            free[b] = tD1
                        elif dst == 2:
                            tD2 = vtt(AT[:, tb], Dm[:, tb], bk[:, :], ALU.mult, t)
                            free[b] = tD2
                        else:
                            tqg = vtt(qg[:, :, tb * P:tb * P + P], qc[:, :, tb * P:tb * P + P],
                                      bk[:, :].rearrange("p (h d) -> p h d", h=4), ALU.mult, t, tt3)
                            free[b] = tqg
                    yield
                    for src, dst in ((kc, LT), (qc, AT)):
                        b, bk, fr = bank("s")
                        for h in range(4):
                            t = group(bk[:, h * P:h * P + P],
                                      [(kc[:, h, tb * P:tb * P + P], src[:, h, tb * P:tb * P + P])], fr)
                        for h in range(4):
                            sl = slice(h * P, h * P + P)
                            tt = vst(dst[:, tb, sl], bk[:, sl], rs[:, 0, tb, h:h + 1], dst[:, tb, sl],
                                     ALU.mult, ALU.mult, t, tD1, tD2)
                        free[b] = tt
                    res["A", tb] = tt
                    l3 = LT[:, tb].rearrange("p (h d) -> p h d", h=4)
                    res["L", tb] = vtt(l3, l3, bc(con("strict"), [P, 4, P]), ALU.mult, tt)
                    yield
                cur = {}
                for lv in range(6):
                    tB = [vtt(BT[tb].rearrange("p (h d) -> p h d", h=4),
                              LT[:, tb].rearrange("p (h d) -> p h d", h=4),
                              bc(con("lv", lv * P, lv * P + P), [P, 4, P]), ALU.mult,
                              res["L", tb], cur.get(("m", tb)), res["wu"], q=po if lv else ve) for tb in range(2)]
                    if lv == 0:
                        id4 = bc(ident, [P, 4, P])
                        for tb in range(2):
                            b, bk, fr = bank("s")
                            for h in range(4):
                                t = group(bk[:, h * P:h * P + P], [(BT[tb][:, h * P:h * P + P], ident)], tB[tb], fr)
                            cur["m", tb] = t
                            cur["T", tb] = vtt(T_[tb].rearrange("p (h d) -> p h d", h=4), id4,
                                               bk[:, :].rearrange("p (h d) -> p h d", h=4), ALU.subtract, t)
                            free[b] = cur["T", tb]
                            cur["TT", tb] = vtt(TT[tb].rearrange("p (h d) -> p h d", h=4), id4,
                                                BT[tb].rearrange("p (h d) -> p h d", h=4), ALU.subtract, tB[tb])
                            cur["m", tb] = [t, cur["TT", tb]]
                        yield
                        continue
                    tM = []
                    for tb in range(2):
                        b, bk, fr = bank("s")
                        for h in range(4):
                            sl = slice(h * P, h * P + P)
                            t = group(bk[:, sl], [(BT[tb][:, sl], T_[tb][:, sl])], tB[tb], cur["T", tb], fr)
                        cur["m", tb] = t
                        t = act(Mm[tb], bk[:, :], ACT.Copy, t, cur.get(("u", tb)))
                        free[b] = t
                        tM.append(t)
                    yield
                    for tb in range(2):
                        b, bk, fr = bank("s")
                        for h in range(4):
                            sl = slice(h * P, h * P + P)
                            t = group(bk[:, sl], [(Mm[tb][:, sl], TT[tb][:, sl])], tM[tb], cur["TT", tb], fr)
                        if lv < 5:
                            b2, bk2, fr2 = bank("s")
                            for h in range(4):
                                sl = slice(h * P, h * P + P)
                                t_2 = group(bk2[:, sl], [(TT[tb][:, sl], Mm[tb][:, sl])], fr2)
                            cur["u", tb] = t_2
                            cur["T", tb] = vtt(T_[tb], T_[tb], bk2[:, :], ALU.subtract, t_2)
                            free[b2] = cur["T", tb]
                        else:
                            t_2 = t
                        cur["TT", tb] = vtt(TT[tb], TT[tb], bk[:, :], ALU.subtract, t_2)
                        free[b] = cur["TT", tb]
                    yield
                tW = []
                for tb in range(2):
                    b, bk, fr = bank("s")
                    for h in range(4):
                        sl = slice(h * P, h * P + P)
                        t = group(bk[:, sl], [(ktk[:, tb, sl], TT[tb][:, sl])], cur["TT", tb], fr)
                    t = act(WT[:, :, tb * P:tb * P + P], bk[:, :].rearrange("p (h d) -> p h d", h=4), ACT.Copy, t,
                            res["A", 1])
                    free[b] = t
                    tW.append(t)
                yield
                tS = None
                for c in range(4):
                    tb, hf = c // 2, c % 2
                    rows = slice(64 * hf, 64 * hf + 64)
                    cols = slice(tb * P + 64 * hf, tb * P + 64 * hf + 64)
                    b, bk, fr = bank("s")
                    for h in range(4):
                        sl = slice(h * P, h * P + P)
                        pairs = [(TT[tb][:, sl], vb[:, tb, sl])]
                        if c:
                            pairs.append((WT[:, h, tb * P:tb * P + P], Sst[:, h]))
                        t = group(bk[:, sl], pairs, tW, tS, fr)
                    tU = vcp(Ut[rows, tb], bk[rows, :], t, res["A", 1])
                    free[b] = tU
                    bo, bko, fr = bank("s")
                    for h in range(4):
                        o = bko[:, h * 64:h * 64 + 64]
                        pairs = [(Ut[rows, tb, h * P:h * P + P], AT[rows, tb, h * P + 64 * hf:h * P + 64 * hf + 64])]
                        if c:
                            group(o, [(Sst[:, h], qg[:, h, cols])], tU, tqg, fr, stop=False)
                            t = group(o, pairs, start=False)
                        else:
                            t = group(o, pairs, tU, fr)
                    to = act(yT[:, 2:6, cols], bko[:, 0:256].rearrange("p (h d) -> p h d", h=4), ACT.Copy, t)
                    free[bo] = to
                    if c < 3:
                        b, bk, fr = bank("s")
                        for h in range(4):
                            t = group(bk[:, h * P:h * P + P],
                                      [(ke[rows, tb, h * P:h * P + P], Ut[rows, tb, h * P:h * P + P])], fr, tU)
                        if c == 0:
                            tS = vcp(Sst.rearrange("p h d -> p (h d)"), bk[:, :], t)
                        else:
                            for h in range(4):
                                tS = vst(Sst[:, h], Sst[:, h], gend[:, tb, hf, h:h + 1], bk[:, h * P:h * P + P],
                                         ALU.mult, ALU.add, t)
                        free[b] = tS
                    yield
                o4 = yT[:, 2:6]
                sq = LT.rearrange("p t n -> p (t n)").rearrange("p (h s) -> p h s", s=S)
                t = act(sq, o4, ACT.Square, to)
                yield
                rr = Dm.rearrange("p t n -> p (t n)").rearrange("p (h s) -> p h s", s=S)
                for p_ in range(2):
                    b, bk, fr = bank("s")
                    for j in range(2):
                        t1 = group(bk[:, j * S:j * S + S], [(onesb[:, :], sq[:, 2 * p_ + j])], t, fr)
                    r2 = rr[:, 2 * p_:2 * p_ + 2].rearrange("p c s -> p (c s)")
                    t1 = vts(r2, bk[:, :], 1.0 / P, 1e-6, ALU.mult, ALU.add, t1)
                    free[b] = t1
                    t1 = vtt(r2, r2, half(512), ALU.pow, t1, t_m5, q=po)
                    y2 = o4[:, 2 * p_:2 * p_ + 2]
                    t1 = vst(y2, y2, prm("gdn_n", l), rr[:, 2 * p_:2 * p_ + 2], ALU.mult, ALU.mult, t1, to)
                    res["gdn", p_] = vtt(y2, y2, zs[:, 2 * p_:2 * p_ + 2], ALU.mult, t1)
                yield

            sides.append(delta())

            cq = gm[:, 0:512].rearrange("p (c s) -> p c s", s=S)
            ck = gm[:, 512:1024].rearrange("p (c s) -> p c s", s=S)
            cv = gm[:, 1024:1536].rearrange("p (t n) -> p t n", t=2)
            i, w, tw_ = take()
            ins = []
            for p_ in range(2):
                b, bk, t = chan_major(w, tw_, 2 * p_, 2, hT, t_h)
                dst = (cq if p_ == 0 else ck).rearrange("p c s -> p (c s)")
                e_ = act(dst, bk[:, :], ACT.Copy, t, scale=0.125 if p_ == 0 else 1.0)
                free[b] = e_
                ins.append(e_)
                tick(sides, 3)
            done(i, t)
            i, w, tw_ = take()
            for tb in range(2):
                b, bk, t = tok_major(i, w, tw_, tb, 256, hT, t_h)
                e_ = act(cv[:, tb], bk[:, 0:256], ACT.Copy, t)
                free[b] = e_
                tick(sides, 3)
            res["cv"] = e_
            res["moba_in"] = ins

            def silu_gate(w, tw_, c, dst):
                b, bk, t = chan_major(w, tw_, c, 2, hT, t_h)
                d2 = dst.rearrange("p c s -> p (c s)")
                t1 = act(sgb[:, 0], bk[:, :], ACT.Sigmoid, t, res.get("sgb"))
                t1 = vtt(d2, bk[:, :], sgb[:, 0], ALU.mult, t1)
                res["sgb"] = t1
                free[b] = t1
                return t, t1

            t, tcg = silu_gate(w, tw_, 2, cgs)
            done(i, t)
            tick(sides, 3)
            i, w, tw_ = take()
            t, tmg = silu_gate(w, tw_, 0, mgs)
            done(i, t)
            drain(sides)
            tfin = [res["gdn", 0], res["gdn", 1]]
            for name, c0, g, tg_ in (("mla", 0, mgs, tmg), ("moba", 6, cgs, tcg)):
                tfin.append(vtt(yT[:, c0:c0 + 2], yT[:, c0:c0 + 2], g, ALU.mult, tg_, res[name, 0], res[name, 1]))
            return row_out([yT], tfin, 2, [4, 4], t_x)

        t_m5 = t_mh
        fnw = mer[:, 0:4].rearrange("p c s -> p (c s)")

        t_x = XIN
        for l in range(L):
            t_x = block1(l, t_x)
        for l in range(L):
            t_x = block2(l, t_x)
        dma(ac, fnw, a["final_w"], s_fn, t_x)
        ts = [act(xn[:, tb], x[:, tb], ACT.Square, t_x, accum_out=st[:, tb:tb + 1]) for tb in range(2)]
        t = vts(st[:, 2:4], st[:, 0:2], 1.0 / D, 1e-6, ALU.mult, ALU.add, ts)
        t = vtt(st[:, 4:6], st[:, 2:4], half(2), ALU.pow, t, q=po)
        for tb in range(2):
            t2 = vst(xn[:, tb], x[:, tb], st[:, 4 + tb:5 + tb], fnw, ALU.mult, ALU.mult, t, (s_fn, 16))
            dma(sp, out[0, tb * P:tb * P + P, :], xn[:, tb], s_out, t2)
        sp.wait((s_out, 32))
        sp.wait((s_sc, 16))
        assert used[0] == len(loads)

        block = ctx.enter_context(nc.Block())

        @block.sync
        def _(e):
            sp.run(e)

        @block.gpsimd
        def _(e):
            po.run(e)

        @block.scalar
        def _(e):
            ac.run(e)

        @block.vector
        def _(e):
            ve.run(e)

        @block.tensor
        def _(e):
            pe.run(e)


def shape_constants():
    c = np.zeros((P, NCN), np.float32)

    def put(name, m):
        o, w = CN[name]
        c[0:m.shape[0], o:o + w] = m

    i = np.arange(P)
    r, q = i[:, None], i[None, :]
    same = (r // 64) == (q // 64)
    put("ident", np.eye(P))
    put("tri", same & (r <= q))
    put("strict", same & (r < q))
    lv = []
    for s in (1, 2, 4, 8, 16, 32):
        lv.append((r // (2 * s) == q // (2 * s)) & (q % (2 * s) >= s) & (r % (2 * s) < s))
    put("lv", np.concatenate(lv, 1))
    put("blk", same)
    put("half0", (r < 64) & (q >= 0))
    put("half1", (r >= 64) & (q >= 0))
    put("trirev", r >= q)
    put("causal", np.where(q <= r, 0.0, NEG))
    strict = (r < q).astype(np.float32)
    put("m0", np.concatenate([-strict, -np.ones((P, P))], 1))
    put("n0", np.concatenate([np.where(r < q, 0.0, NEG), np.zeros((P, P))], 1))
    n = np.maximum(255 - np.arange(512), 0)
    nf = np.maximum(n, 1).astype(np.float32)
    large = 16 + (np.log(nf / np.float32(16)) / np.float32(np.log(2048 / 16)) * np.float32(16)).astype(np.int32)
    bucket = np.where(n < 16, n, np.minimum(large, 31))
    oh = np.zeros((32, 512), np.float32)
    oh[bucket, np.arange(512)] = 1.0
    inv = [np.float32(500000.0) ** (-(np.arange(h, dtype=np.float32) * np.float32(2.0)) / np.float32(2 * h))
           for h in (16, 8)]
    put("invf", np.broadcast_to(np.concatenate(inv).astype(np.float32), (P, 24)))
    inv2 = (1.0 / (np.float32(10000.0) ** (np.arange(0, 32, 2, dtype=np.float32) / np.float32(32)))).astype(np.float32)
    ang = np.arange(S, dtype=np.float32)[:, None] * inv2[None, :]
    cc, ss = np.cos(ang.astype(np.float32)), np.sin(ang.astype(np.float32))
    put("rope2", np.concatenate([cc[:P], ss[:P], cc[P:], ss[P:]], 1))
    return c, oh, np.ascontiguousarray(np.eye(P, dtype=np.float32)[::-1])


def pack_params(a):
    cols = []
    for l in range(L):
        def ch(v):
            v = v.reshape(-1, v.shape[-1] // P, P)
            return v.transpose(2, 1, 0).reshape(P, -1)

        def rows(v):
            return np.broadcast_to(v[None, :], (P, v.shape[0]))

        part = {
            "g_mix": ch(a["g_mix"][l]), "b_gate": ch(a["b_gate"][l]), "cb_w": ch(a["cb_conv_w"][l]),
            "cb_b": ch(a["cb_conv_b"][l]), "ln_g": ch(a["cb_ln_g"][l]), "ln_b": ch(a["cb_ln_b"][l]),
            "cc_w": ch(a["cc_conv_w"][l]), "g_ffn": ch(a["g_ffn"][l]), "ffn_w": ch(a["ffn_conv_w"][l]),
            "norm2": ch(a["norm_w_2"][l]), "qn2": ch(a["mla_q_norm_2"][l]), "kvn2": ch(a["mla_kv_norm_2"][l]),
            "gdn_w": ch(a["gdn_conv_w_2"][l]), "gdn_n": ch(a["gdn_norm_w_2"][l]),
            "alog": rows(a["gdn_A_log_2"][l]), "dtb": rows(a["gdn_dt_bias_2"][l]),
        }
        for n in PL:
            cols.append(part[n])
    gains = [rows(a[n][l]) for l in range(L) for n in ("g_qa", "g_ka", "g_kidx")]
    return np.ascontiguousarray(np.concatenate(cols, 1)), np.ascontiguousarray(np.concatenate(gains, 1))


BIGS = ["x", "w_in", "w_oa", "w_ob", "w_oc", "w_od", "w_merge", "w_ffn_gate", "w_ffn_up", "w_ffn_down",
        "w_in_2", "mla_w_uq_2", "mla_w_ukv_2", "w_out_2", "t5_table_2"]


def kernel(**inputs):
    import concourse.bacc as bacc
    from concourse.bass_utils import run_bass_kernel_spmd

    h = {k: np.asarray(v) for k, v in inputs.items()}
    feed = {n: np.ascontiguousarray(h[n]) for n in BIGS}
    feed["pos"] = np.ascontiguousarray(h["positions"][0].reshape(2, P).T)
    feed["final_w"] = np.ascontiguousarray(np.broadcast_to(h["final_norm_w_2"][None, :], (P, D)))
    feed["params"], feed["gains"] = pack_params(h)
    feed["consts"], feed["onehot"], feed["flip"] = shape_constants()
    nc = bacc.Bacc("TRN2", target_bir_lowering=False, num_devices=1)
    a, arrays = {}, {}
    for n, v in feed.items():
        arrays[f"in_{n}"] = v
        a[n] = nc.dram_tensor(f"in_{n}", v.shape, mybir.dt.from_np(v.dtype), kind="ExternalInput").ap()
    out = nc.dram_tensor("out_x", (1, S, D), F32, kind="ExternalOutput").ap()
    scratch = nc.dram_tensor("toeplitz", (4, 512), F32, kind="Internal")
    sa = scratch.ap()
    a["scratch"] = sa
    a["toep"] = [bass.AP(tensor=sa.tensor, offset=h_ * 512, ap=[[1, P], [1, S]]) for h_ in range(4)]
    build(nc, a, out)
    r = run_bass_kernel_spmd(nc, [arrays], core_ids=[0])
    return r.results[0]["out_x"]
```

```python
from contextlib import ExitStack

import numpy as np
import concourse.bass as bass
from concourse import mybir

F32 = mybir.dt.float32
I32 = mybir.dt.int32
ALU = mybir.AluOpType
ACT = mybir.ActivationFunctionType
AX = mybir.AxisListType

P = 128
S = 256
D = 1024
L = 2
FF = 2816
NIN1 = 10052
NIN2 = 3752
SLOT = 4 * 512
NSLOT = 3
PART = 2 * 512
NPART = 4
F32R = mybir.dt.float32r
NEG = -1e30
PICKED = -3e38

PL = {}
_at = 0
for _n, _w in (("g_mix", 8), ("b_gate", 32), ("cb_w", 124), ("cb_b", 4), ("ln_g", 4), ("ln_b", 4),
               ("cc_w", 12), ("g_ffn", 8), ("ffn_w", 66), ("norm2", 8), ("qn2", 2), ("kvn2", 1),
               ("gdn_w", 48), ("gdn_n", 1), ("alog", 4), ("dtb", 4)):
    PL[_n] = (_at, _w)
    _at += _w
NPL = _at
ROWS = {"g_q": (0, 128), "g_k": (128, 128), "g_ki": (256, 64)}

CN = {}
_at = 0
for _n, _w in (("ident", 128), ("tri", 128), ("strict", 128), ("lv", 6 * 128),
               ("blk", 128), ("half0", 128), ("half1", 128), ("trirev", 128), ("zero", 128), ("causal", 128),
               ("m0", 256), ("n0", 256), ("invf", 24),
               ("rope2", 64)):
    CN[_n] = (_at, _w)
    _at += _w
NCN = _at


class Pairs(list):
    pass


class Queue:

    def __init__(self, sem):
        self.sem, self.n, self.ops, self.seen = sem, 0, [], {}

    def wait(self, *tokens):
        for t in tokens:
            if t is None:
                continue
            if isinstance(t, list):
                self.wait(*t)
            elif self.seen.get(id(t[0]), 0) < t[1]:
                self.seen[id(t[0])] = t[1]
                self.ops.append(lambda e, t=t: e.wait_ge(t[0], t[1]))

    def quiet(self, fn):
        self.ops.append(fn)

    def __call__(self, fn, *after):
        self.wait(*after)
        self.n += 1
        self.ops.append(lambda e: fn(e).then_inc(self.sem, 1))
        return (self.sem, self.n)

    def run(self, e):
        for op in self.ops:
            op(e)


def build(nc, a, out):
    ctx = ExitStack()
    with ctx:
        def sb(name, shape, dt=F32):
            return ctx.enter_context(nc.sbuf_tensor(name, shape, dt))

        def sem(name):
            return ctx.enter_context(nc.semaphore(name))

        banks = [ctx.enter_context(nc.psum_tensor(f"bank{i}", [P, 512], F32)) for i in range(8)]

        ring = sb("ring", [P, NSLOT, SLOT])
        whi = sb("whi", [P, NPART, PART], F32R)
        wlo = sb("wlo", [P, NPART, PART], F32R)
        hhi = sb("hhi", [P, 8, S], F32R)
        hlo = sb("hlo", [P, 8, S], F32R)
        cst = sb("cst", [P, NCN])
        par = sb("par", [P, L * NPL])
        onesb = sb("onesb", [P, 128])
        mhalf = sb("mhalf", [P, 1])
        posi = sb("posi", [P, 2], I32)
        posf = sb("posf", [P, 2])
        x = sb("x", [P, 2, D])
        xn = sb("xn", [P, 2, D])
        st = sb("st", [P, 512])
        cs = sb("cs", [P, 2, 48])
        sgb = sb("sgb", [P, 4, S])
        tab = sb("tab", [32, 4])
        ptb = sb("ptb", [P, 3, 4, 128])
        pt = [[ptb[:, 0], None], [ptb[:, 1], ptb[:, 2]]]

        first = ExitStack()
        fhi = first.enter_context(nc.sbuf_tensor("fhi", [P, 2, 4, S], F32R))
        flo = first.enter_context(nc.sbuf_tensor("flo", [P, 2, 4, S], F32R))
        w1 = first.enter_context(nc.sbuf_tensor("w1", [P, 18568], F32))
        first.close()
        w2 = sb("w2", [P, 24064])

        def part1(o, n):
            assert o + n <= 18568
            return w1[:, o:o + n]

        def c4(ap):
            return ap.rearrange("p (c s) -> p c s", s=S)

        A1, B1, vAf = part1(0, 1024), part1(1024, 1024), part1(2048, 1024)
        ibuf = part1(3072, 648).rearrange("p (t n) -> p t n", t=2)
        iT = part1(3720, 1280)[0:64].rearrange("p (h s) -> p h s", h=5)
        mk = c4(part1(5000, 512))
        sqT, skT = c4(part1(5512, 1024)), c4(part1(6536, 1024))
        gpad = part1(5512, 1032).rearrange("p (r c s) -> p r c s", r=2, c=2)
        sv = part1(7560, 1024).rearrange("p (t n) -> p t n", t=2)
        lk0 = c4(part1(8584, 1024))
        lk1 = part1(9608, 512).rearrange("p (h s) -> p h s", s=P)
        glup = part1(10120, 1144).rearrange("p (c s) -> p c s", c=4)
        cacc = c4(part1(11264, 1024))
        ccp = part1(12288, 1032).rearrange("p (c s) -> p c s", c=4)
        gbS, yc = c4(part1(13320, 1024)), c4(part1(14344, 1024))
        rt = part1(14344, 192).rearrange("p (t n) -> p t n", t=2)
        gains = part1(15368, 640)
        mer1 = c4(part1(16008, 2048))
        tap = part1(18056, 512).rearrange("p (r s) -> p r s", r=2)

        def part2(o, n):
            return w2[:, o:o + n]

        big = part2(0, 8192)
        bufA, bufB, bufC, bufD, bufE, bufF, bufG, bufH, bufI, bufJ = (
            part2(8192 + 1024 * i, 1024) for i in range(10))
        mer = c4(part2(18432, 2048))
        gm = part2(20480, 1536)
        bia = c4(part2(22016, 1024))
        gdp = part2(8192 + 9216, 1036).rearrange("p (r c s) -> p r c s", r=2, c=2)
        wuq = bufD[:, 0:768].rearrange("p (k n) -> p k n", k=2)
        wukv = bufC[:, 0:512]
        gs = xn[:, :, 736:992].rearrange("p t (a d) -> p t a d", a=2)
        halves = lambda b: [b[:, 0:512], b[:, 512:1024]]

        pe, ve, ac, po = (Queue(sem(n)) for n in ("s_pe", "s_dve", "s_act", "s_pool"))
        sp = Queue(sem("s_sp"))
        s_slot = [sem(f"s_slot{i}") for i in range(NSLOT)]
        s_gn, s_fl = sem("s_gn"), sem("s_fl")
        s_c, s_p, s_x, s_pos, s_tab, s_sc, s_bi, s_u, s_out, s_fn = (
            sem(n) for n in ("s_c", "s_p", "s_x", "s_pos", "s_tab", "s_sc", "s_bi", "s_u", "s_out", "s_fn"))

        def con(name, a0=0, a1=None):
            o, w = CN[name]
            return cst[:, o + a0:o + (w if a1 is None else a1)]

        def prm(name, layer, a0=0, a1=None):
            o, w = PL[name]
            o += layer * NPL
            return par[:, o + a0:o + (w if a1 is None else a1)]

        def row(name, layer):
            o, w = ROWS[name]
            return gains[:, layer * 320 + o:layer * 320 + o + w]

        def dma(q, dst, src, s, *after):
            q.wait(*after)
            q.quiet(lambda e: e.dma_start(dst, src).then_inc(s, 16))

        ident = con("ident")

        loads, parts = [], []

        def load(src, cuts):
            k, n = src.shape[1], src.shape[2]
            assert k * n <= SLOT
            for c in cuts:
                parts.append((len(loads),) + c)
            loads.append((src, k, n))

        def load_k8(w, c0, c1):
            for k in (0, 4):
                load(w[:, k:k + 4, c0:c1], [(0, 2, 0, c1 - c0), (2, 4, 0, c1 - c0)])

        def load_list():
            for l in range(L):
                w = a["w_in"][l].rearrange("(k p) n -> p k n", p=P)
                for c0, c1 in [(2372, 2884), (1860, 2372), (1536, 1860), (0, 512), (512, 1024), (1024, 1536),
                               (4420, 4932), (4932, 5444), (5444, 5956),
                               (3396, 3908), (3908, 4420), (2884, 3396)]:
                    load_k8(w, c0, c1)
                for n, bi in (("w_ob", 1), ("w_oc", 2), ("w_od", 3), ("w_oa", 0)):
                    wo = a[n][l].rearrange("(k p) n -> p k n", p=P)
                    for hf in range(2):
                        load_k8(w, 5956 + 1024 * bi + 512 * hf, 6468 + 1024 * bi + 512 * hf)
                        load(wo[:, :, 512 * hf:512 * hf + 512], [(0, 2, 0, 512), (2, 4, 0, 512)])
                w = a["w_merge"][l].rearrange("(k p) n -> p k n", p=P)
                for i in range(4):
                    load(w[:, 2 * i:2 * i + 2, :], [(0, 2, 0, 512), (0, 2, 512, 1024)])
                g = a["w_ffn_gate"][l].rearrange("(k p) n -> p k n", p=P)
                u = a["w_ffn_up"][l].rearrange("(k p) n -> p k n", p=P)
                w = a["w_ffn_down"][l].rearrange("(k p) n -> p k n", p=P)

                def down(i):
                    for k in range(4 * i, min(4 * i + 4, 22), 2):
                        load(w[:, k:k + 2, :], [(0, 2, 0, 512), (0, 2, 512, 1024)])

                for i in range(6):
                    e = min(512 * i + 512, FF)
                    load_k8(g, 512 * i, e)
                    load_k8(u, 512 * i, e)
                    if i:
                        down(i - 1)
                down(5)
            for l in range(L):
                w = a["w_in_2"][l].rearrange("(k p) n -> p k n", p=P)
                load(w[:, :, 2720:2728], [(0, 8, 0, 8)])
                for c0, c1 in [(1184, 1696), (672, 1184), (1696, 2208), (0, 416), (2728, 3240), (3240, 3752),
                               (2208, 2720), (416, 672)]:
                    load_k8(w, c0, c1)
                w = a["w_out_2"][l].rearrange("(k p) n -> p k n", p=P)
                for i in (0, 3, 1, 2):
                    load(w[:, 2 * i:2 * i + 2, :], [(0, 2, 0, 512), (0, 2, 512, 1024)])

        load_list()
        last_part = [max(j for j, p_ in enumerate(parts) if p_[0] == i) for i in range(len(loads))]
        used = [0]
        cutq = [0]
        landed = {}
        hi_done, lo_done, low_made = {}, {}, {}

        def issue(i, *after):
            if i < len(loads):
                src, k, n = loads[i]
                dma(sp, ring[:, i % NSLOT, 0:k * n].rearrange("p (k n) -> p k n", k=k), src,
                    s_slot[i % NSLOT], *after)

        def split_part(j):
            i, k0, k1, c0, c1 = parts[j]
            _, k, n = loads[i]
            src = ring[:, i % NSLOT, 0:k * n].rearrange("p (k n) -> p k n", k=k)[:, k0:k1, c0:c1]
            size = (k1 - k0) * (c1 - c0)
            h_, l_ = (w_[:, j % NPART, 0:size].rearrange("p (k n) -> p k n", k=k1 - k0) for w_ in (whi, wlo))
            th = act(h_, src, ACT.Copy, (s_slot[i % NSLOT], 16 * (i // NSLOT + 1)), hi_done.get(j - NPART),
                     low_made.get(j - NPART))
            tl = vtt(l_, src, h_, ALU.subtract, th, lo_done.get(j - NPART), q=po if j % 3 == 1 else ve)
            landed[j] = (h_, l_, th, tl)
            low_made[j] = tl
            if j == last_part[i]:
                issue(i + NSLOT, [low_made[j_] for j_, p_ in enumerate(parts[:j + 1]) if p_[0] == i])

        def take():
            j = used[0]
            used[0] += 1
            while cutq[0] <= min(j + NPART - 1, len(parts) - 1) and cutq[0] - NPART < j:
                split_part(cutq[0])
                cutq[0] += 1
            return (j,) + landed.pop(j)

        def done(j, th, tl):
            hi_done[j], lo_done[j] = th, tl
            while cutq[0] <= min(j + NPART, len(parts) - 1):
                split_part(cutq[0])
                cutq[0] += 1

        free = [None] * 8
        turn = {"m": 0, "s": 0}

        def bank(kind):
            b = turn[kind] % 4 + (4 if kind == "s" else 0)
            turn[kind] += 1
            return b, banks[b], free[b]

        def group(o, pairs, *after, start=True, stop=True, tr=False):
            pe.wait(*after)
            tok = None
            for i, (l_, r_) in enumerate(pairs):
                last = i == len(pairs) - 1
                f = (lambda e, l_=l_, r_=r_, i=i, last=last:
                     e.matmul(o, l_, r_, start=start and i == 0, stop=stop and last))
                if last:
                    tok = pe(f)
                else:
                    pe.quiet(f)
            return tok

        def turnover(o, i_, *after):
            k = i_.shape[0]
            return pe(lambda e: e.transpose(o, i_, ident[0:k, 0:k]), *after)

        def vtt(o, i0, i1, op, *after, q=None):
            return (q or ve)(lambda e: e.tensor_tensor(o, i0, i1, op), *after)

        def vts(o, i0, s1, s2, o1, o2, *after, q=None):
            if s2 is None:
                return (q or ve)(lambda e: e.tensor_scalar(o, i0, s1, None, o1), *after)
            return (q or ve)(lambda e: e.tensor_scalar(o, i0, s1, s2, o1, o2), *after)

        def vst(o, i0, s_, i1, o1, o2, *after, q=None):
            return (q or ve)(lambda e: e.scalar_tensor_tensor(out=o, in0=i0, scalar=s_, in1=i1, op0=o1, op1=o2), *after)

        def vcp(o, i_, *after, q=None):
            return (q or ve)(lambda e: e.tensor_copy(o, i_), *after)

        def act(o, i_, f, *after, **kw):
            return ac(lambda e: e.activation(o, i_, f, **kw), *after)

        def half(n):
            return mhalf[:, :].to_broadcast([P, n])

        def bc(ap, shape, ax=1):
            return ap.unsqueeze(ax).to_broadcast(shape)

        def split(h_, l_, src, *after):
            th = act(h_, src, ACT.Copy, *after)
            return [th, vtt(l_, src, h_, ALU.subtract, th)]

        def streamed(nparts, src, t_src, chans=None, toks=None, held=None, k0=0, first_=True, final=True,
                     on=None):
            sh, sl = src
            nb = 2 if toks else (chans + 1) // 2
            if held is None:
                held = [bank("m") for _ in range(nb)]
            for q_ in range(nparts):
                j, wh, wl, th, tl = take()
                kn = wh.shape[1]
                if q_ == 0:
                    pe.wait([h_[2] for h_ in held])
                pe.wait([t_src[c] for c in range(k0 // 2, (k0 + kn + 1) // 2)] if isinstance(t_src, Pairs)
                        else t_src)
                ends = []
                for half_, tok in ((0, th), (1, tl)):
                    pe.wait(tok)
                    w_ = (wh, wl)[half_]
                    todo = []
                    for u in range(2 if toks else chans):
                        for k in range(kn):
                            for s_ in ((sh, sl) if half_ == 0 else (sh,)):
                                if toks:
                                    o = held[u][1][:, 0:toks]
                                    pr = (s_[:, k0 + k, u * P:u * P + P], w_[:, k, 0:toks])
                                    opens = k == 0 and s_ is sh
                                else:
                                    o = held[u // 2][1][:, (u % 2) * S:(u % 2) * S + S]
                                    pr = (w_[:, k, u * P:u * P + P], s_[:, k0 + k, :])
                                    opens = k == 0 and s_ is sh and u % 2 == 0
                                todo.append((o, pr, first_ and q_ == 0 and half_ == 0 and opens,
                                             final and q_ == nparts - 1 and half_ == 1))
                    for n_, (o, pr, st_, sp_) in enumerate(todo):
                        f = (lambda e, o=o, pr=pr, st_=st_, sp_=sp_:
                             e.matmul(o, pr[0], pr[1], start=st_, stop=sp_, skip_group_check=True))
                        if n_ == len(todo) - 1:
                            ends.append(pe(f))
                        else:
                            pe.quiet(f)
                done(j, ends[0], ends[1])
                k0 += kn
                if on:
                    on()
            return held, ends[1]

        dma(sp, x[:, :, :], a["x"][0].rearrange("(t p) d -> p t d", p=P), s_x)
        dma(sp, cst[:, :], a["consts"], s_c)
        dma(sp, par[:, :], a["params"], s_p)
        for i in range(NSLOT):
            issue(i)
        dma(ac, posi[:, :], a["pos"], s_pos)
        dma(ac, tab[:, :], a["t5_table_2"], s_tab)
        dma(ac, A1[0:32, 0:512], a["onehot"], s_tab)
        dma(ac, gains, a["gains"], s_gn)
        GAIN = (s_gn, 16)
        CST, PAR, XIN = (s_c, 16), (s_p, 16), (s_x, 16)
        t_ones = ve(lambda e: e.memset(onesb[:, :], 1.0))
        t_mh = ve(lambda e: e.memset(mhalf[:, :], -0.5))
        z1 = ve(lambda e: e.memset(glup[:, :, 0:30], 0.0))
        z2 = ve(lambda e: e.memset(ccp[:, :, 0:2], 0.0))

        t = vcp(posf[:, :], posi[:, :], (s_pos, 16))
        tt_ = None
        ang, kk, ki, r_ = rt[:, :, 0:24], rt[:, :, 24:48], rt[:, :, 48:72], rt[:, :, 72:96]
        tw = []
        for tb in range(2):
            tw.append(vts(ang[:, tb], con("invf"), posf[:, tb:tb + 1], None, ALU.mult, None, t, CST))
        MAGIC = 12582912.0
        TWO = [6.28125, 0.0019350051879882812, 3.019916050561733e-07, 2.0561020951390433e-14]
        assert abs(sum(TWO) - 2 * np.pi) < 1e-12
        for which in range(2):
            o = cs[:, :, 24 * which:24 * which + 24]
            t = vts(kk, ang, float(1 / (2 * np.pi)), 0.25 if which == 0 else 0.0, ALU.mult, ALU.add, tw, t)
            t = vts(kk, kk, MAGIC, -MAGIC, ALU.add, ALU.add, t)
            t = vts(ki, kk, 1 / 4096.0, MAGIC, ALU.mult, ALU.add, t)
            t = vts(ki, ki, -MAGIC, 4096.0, ALU.add, ALU.mult, t)
            t = vtt(kk, kk, ki, ALU.subtract, t)
            src = ang
            for c in TWO:
                t = vst(r_, ki, -c, src, ALU.mult, ALU.add, t)
                t = vst(r_, kk, -c, r_, ALU.mult, ALU.add, t)
                src = r_
            if which == 0:
                t = vts(r_, r_, float(np.pi / 2), None, ALU.add, None, t)
            t = vts(r_, r_, 3.1415925, -3.1415925, ALU.min, ALU.max, t)
            t = act(o, r_, ACT.Sin, t)
        t_cs = t

        b, bk, _ = bank("s")
        t = group(bk[0:4, 0:512], [(tab[:, :], A1[0:32, 0:512])], (s_tab, 32))
        t = vcp(part1(13320, 512)[0:4], bk[0:4, :], t)
        free[b] = t
        dma(ac, a["scratch"], part1(13320, 512)[0:4], s_sc, t)

        def normed_T(layer, gname, t_x):
            ts = []
            for tb, nh in ((0, 0), (1, 0), (0, 1), (1, 1)):
                cols = slice(512 * nh, 512 * nh + 512)
                q_ = 2 * tb + nh
                ts.append(act(xn[:, tb, cols], x[:, tb, cols], ACT.Square, t_x[q_], scale=1.0 / 32,
                              accum_out=st[:, q_:q_ + 1]))
            t = vst(st[:, 4:6], st[:, 0:4:2], 1e-6, st[:, 1:4:2], ALU.add, ALU.add, ts)
            t = vtt(st[:, 6:8], st[:, 4:6], half(2), ALU.pow, t, t_mh, q=po)
            tn = {}
            for nh in range(2):
                cols = slice(512 * nh, 512 * nh + 512)
                tn[nh, 0] = vts(xn[:, 0, cols], x[:, 0, cols], st[:, 6:7], None, ALU.mult, None, t)
                tn[nh, 1] = act(xn[:, 1, cols], x[:, 1, cols], ACT.Copy, t, scale=st[:, 7:8])
            outs = Pairs()
            for c in range(0, 8, 2):
                b, bk, fr = bank("m")
                for j in range(2):
                    for tb in range(2):
                        tk = turnover(bk[:, j * S + tb * P:j * S + tb * P + P],
                                      xn[:, tb, (c + j) * P:(c + j + 1) * P], tn[c // 4, tb], fr, CST)
                for j in range(2):
                    g = prm(gname, layer, c + j, c + j + 1)
                    th = act(hhi[:, c + j], bk[:, j * S:j * S + S], ACT.Copy, tk, PAR, scale=g)
                for j in range(2):
                    g = prm(gname, layer, c + j, c + j + 1)
                    tl = vst(hlo[:, c + j], bk[:, j * S:j * S + S], g, hhi[:, c + j],
                             ALU.mult, ALU.subtract, th, PAR)
                free[b] = tl
                outs.append(tl)
            return outs

        def rope(v, nh, half, cos, sin, tmp, t):
            x1, x2 = v[:, :, 0:half], v[:, :, half:2 * half]
            c, s_ = bc(cos, [P, nh, half]), bc(sin, [P, nh, half])
            ts = [vtt(tmp[:, 0], x1, c, ALU.mult, t), vtt(tmp[:, 1], x2, s_, ALU.mult, t),
                  vtt(tmp[:, 2], x2, c, ALU.mult, t), vtt(tmp[:, 3], x1, s_, ALU.mult, t)]
            vtt(x1, tmp[:, 0], tmp[:, 1], ALU.subtract, ts)
            return vtt(x2, tmp[:, 2], tmp[:, 3], ALU.add, ts)

        war_pt = [None, None]

        def attend(lg, qT, kT, V, t_in, t_v, scale, mask, t_mask, outp, so, rowtiles=False):
            marks = []
            for tb in range(2):
                nk = P * (tb + 1)
                g = lg[tb].rearrange("p (h k) -> p h k", h=4)[:, :, 0:nk]
                tl = []
                for hp in range(2):
                    b, bk, fr = bank("s")
                    for j in range(2):
                        h = hp + 2 * j if rowtiles else 2 * hp + j
                        t = group(bk[:, j * nk:(j + 1) * nk], [(qT(h, tb), kT(h, 0, nk))], t_in, fr)
                    src = bk[:, 0:2 * nk].rearrange("p (h k) -> p h k", h=2)
                    hs = slice(hp, hp + 3, 2) if rowtiles else slice(2 * hp, 2 * hp + 2)
                    t = vst(g[:, hs], src, scale, mask(tb, hp), ALU.mult, ALU.add, t, t_mask)
                    free[b] = t
                    tl.append(t)
                s0 = so + 16 * tb
                t = ve(lambda e, g=g, s0=s0: e.tensor_reduce(st[:, s0:s0 + 4], g, AX.X, ALU.max, negate=True), tl)
                te = [act(g[:, h], g[:, h], ACT.Exp, t, bias=st[:, s0 + h:s0 + h + 1],
                          accum_out=st[:, s0 + 4 + h:s0 + 5 + h]) for h in range(4)]
                t = ve(lambda e, s0=s0: e.reciprocal(st[:, s0 + 8:s0 + 12], st[:, s0 + 4:s0 + 8]), te)
                t = vtt(g, g, bc(st[:, s0 + 8:s0 + 12], [P, 4, nk], 2), ALU.mult, t)
                marks.append(t)
                yield
            tp = [[], []]
            for tb in range(2):
                g = lg[tb].rearrange("p (h k) -> p h k", h=4)
                for kb in range(tb + 1):
                    b, bk, fr = bank("s")
                    for h in range(4):
                        t = turnover(bk[:, h * P:h * P + P], g[:, h, kb * P:kb * P + P], marks[tb], fr)
                    dst = pt[tb][kb].rearrange("p h k -> p (h k)")
                    if kb == 0:
                        t = act(dst, bk[:, :], ACT.Copy, t, war_pt[tb])
                    else:
                        t = vcp(dst, bk[:, :], t, war_pt[tb])
                    free[b] = t
                    tp[tb].append(t)
            yield
            for tb in range(2):
                b, bk, fr = bank("s")
                t = outp(tb, bk, lambda h, kb: (V(h, kb), pt[tb][kb][:, h, :]), tb + 1,
                         [tp[tb], t_v, fr])
                war_pt[tb] = t[0]
                free[b] = t[1]
            yield

        def tick(sides):
            ahead, rest = sides
            again = 1 if ahead else 2
            if ahead:
                try:
                    next(ahead[0])
                except StopIteration:
                    ahead.pop(0)
            for _ in range(again):
                if rest:
                    g = rest.pop(0)
                    try:
                        next(g)
                        rest.append(g)
                    except StopIteration:
                        pass

        def drain(sides):
            while sides[0] or sides[1]:
                tick(sides)

        def block1(l, t_x):
            t_h = normed_T(l, "g_mix", t_x)
            res = {}
            sides = ([], [])
            hh = (hhi, hlo)
            qk = [A1.rearrange("p (h d) -> p h d", h=8), B1.rearrange("p (h d) -> p h d", h=8)]
            vA = vAf.rearrange("p (t n) -> p t n", t=2)
            xnf = xn[:, :, :].rearrange("p t n -> p (t n)")
            qkT = xnf.rearrange("p (h s) -> p h s", s=S)
            wk = mer1[:, 4:6, :]
            rl = mer1[:, 0:4, :]
            lgs = [A1, B1]
            F = [(fhi[:, r], flo[:, r]) for r in range(2)]

            def go():
                tick(sides)

            held, t = streamed(4, hh, t_h, chans=4, on=go)
            for p_, (b, bk, _) in enumerate(held):
                tsg = act(sgb[:, 2 * p_:2 * p_ + 2].rearrange("p c s -> p (c s)"), bk[:, :], ACT.Sigmoid, t,
                          res.get("sgb"))
                free[b] = tsg
            held, t = streamed(4, hh, t_h, chans=4, on=go)
            tg = []
            for p_, (b, bk, _) in enumerate(held):
                free[b] = vtt(glup[:, 2 * p_:2 * p_ + 2, 30:286], bk[:, :].rearrange("p (c s) -> p c s", c=2),
                              sgb[:, 2 * p_:2 * p_ + 2], ALU.mult, t, tsg)
                tg.append(free[b])
            res["sgb"] = free[b]

            def conv_branch():
                last = [None] * 4
                taps = [None, None]
                for j in range(31):
                    for c in range(4):
                        wv = prm("cb_w", l, c * 31 + j, c * 31 + j + 1)
                        if c == 3:
                            if j == 0:
                                last[3] = act(cacc[:, 3], glup[:, 3, 0:S], ACT.Identity, tg, PAR, z1, scale=wv,
                                              bias=prm("cb_b", l, 3, 4))
                            else:
                                t = act(tap[:, j % 2], glup[:, 3, j:j + S], ACT.Copy, taps[j % 2], scale=wv)
                                last[3] = vtt(cacc[:, 3], cacc[:, 3], tap[:, j % 2], ALU.add, t, last[3], q=po)
                                taps[j % 2] = last[3]
                        elif j == 0:
                            last[c] = vts(cacc[:, c], glup[:, c, 0:S], wv, prm("cb_b", l, c, c + 1),
                                          ALU.mult, ALU.add, tg, PAR, z1)
                        else:
                            last[c] = vst(cacc[:, c], glup[:, c, j:j + S], wv, cacc[:, c], ALU.mult, ALU.add,
                                          last[c])
                    yield
                b, bk, fr = bank("s")
                t = group(bk[:, 0:S], [(onesb[:, :], cacc[:, c]) for c in range(4)], last, fr, t_ones)
                t = vst(cacc, bc(bk[:, 0:S], [P, 4, S]), -1.0 / 512, cacc, ALU.mult, ALU.add, t)
                free[b] = t
                sq = lk0
                t = act(sq, cacc, ACT.Square, t)
                yield
                b, bk, fr = bank("s")
                for tb in range(2):
                    t1 = group(bk[:, tb:tb + 1], [(sq[:, c, tb * P:tb * P + P], onesb[:, 0:1]) for c in range(4)],
                               t, fr)
                t = vts(st[:, 12:14], bk[:, 0:2], 1.0 / 512, 1e-6, ALU.mult, ALU.add, t1)
                free[b] = t
                t = vtt(st[:, 14:16], st[:, 12:14], half(2), ALU.pow, t, q=po)
                yield
                b, bk, fr = bank("s")
                for tb in range(2):
                    t1 = group(bk[:, tb * P:tb * P + P], [(st[:, 14 + tb:15 + tb].to_broadcast([P, P]), ident)],
                               t, fr)
                t = vtt(cacc, cacc, bc(bk[:, 0:S], [P, 4, S]), ALU.mult, t1)
                free[b] = t
                yield
                ts = [act(sq[:, c], cacc[:, c], ACT.Sigmoid, t, scale=prm("ln_g", l, c, c + 1),
                          bias=prm("ln_b", l, c, c + 1)) for c in range(4)]
                tz = [vts(cacc[:, c], cacc[:, c], prm("ln_g", l, c, c + 1), prm("ln_b", l, c, c + 1),
                          ALU.mult, ALU.add, ts) for c in range(4)]
                t = vtt(cacc, cacc, sq, ALU.mult, tz)
                yield
                res["yb"] = split(F[0][0], F[0][1], cacc, t)
                yield

            sides[0].append(conv_branch())

            held, t = streamed(4, hh, t_h, toks=324, on=go)
            ti = []
            for tb, (b, bk, _) in enumerate(held):
                free[b] = act(ibuf[:, tb], bk[:, 0:324], ACT.Copy, t)
                ti.append(free[b])

            def indexer():
                tr_ = []
                for tb in range(2):
                    kx = ibuf[:, tb, 256:320]
                    s0 = 16 + 2 * tb
                    t = act(mk[:, tb, 0:64], kx, ACT.Square, ti[tb], accum_out=st[:, s0:s0 + 1])
                    t = vts(st[:, s0:s0 + 1], st[:, s0:s0 + 1], 1.0 / 64, 1e-6, ALU.mult, ALU.add, t)
                    t = vtt(st[:, s0 + 1:s0 + 2], st[:, s0:s0 + 1], half(1), ALU.pow, t, q=po)
                    t = vst(kx, kx, st[:, s0 + 1:s0 + 2], row("g_ki", l), ALU.mult, ALU.mult, t, GAIN)
                    v = ibuf[:, tb, 0:320].rearrange("p (h d) -> p h d", h=5)
                    tmp = mk[:, tb, 0:160].rearrange("p (a h d) -> p a h d", a=4, h=5)
                    tr_.append(rope(v, 5, 8, cs[:, tb, 16:24], cs[:, tb, 40:48], tmp, [t, t_cs]))
                yield
                te = []
                for tb in range(2):
                    for hh, n in ((0, 4), (4, 1)):
                        b, bk, fr = bank("s")
                        for h in range(hh, hh + n):
                            t = turnover(bk[0:64, (h - hh) * P:(h - hh) * P + P],
                                         ibuf[:, tb, h * 64:h * 64 + 64], tr_[tb], fr)
                        t = act(iT[:, hh:hh + n, tb * P:tb * P + P],
                                bk[0:64, 0:n * P].rearrange("p (h k) -> p h k", h=n), ACT.Copy, t)
                        free[b] = t
                        te.append(t)
                yield
                for tb in range(2):
                    nk = P * (tb + 1)
                    tl = []
                    for hp in range(2):
                        b, bk, fr = bank("s")
                        for j in range(2):
                            h = 2 * hp + j
                            t = group(bk[:, j * nk:(j + 1) * nk],
                                      [(iT[:, h, tb * P:tb * P + P], iT[:, 4, 0:nk])], te, fr)
                        r = []
                        for j in range(2):
                            h = 2 * hp + j
                            r.append(vts(rl[:, h, 0:nk], bk[:, j * nk:(j + 1) * nk], 0.0,
                                         ibuf[:, tb, 320 + h:321 + h], ALU.max, ALU.mult, t))
                        free[b] = r
                        tl += r
                    t = vtt(rl[:, 0, 0:nk], rl[:, 0, 0:nk], rl[:, 1, 0:nk], ALU.add, tl)
                    t = vtt(rl[:, 0, 0:nk], rl[:, 0, 0:nk], rl[:, 2, 0:nk], ALU.add, t)
                    t = vtt(wk[:, tb, 0:nk], rl[:, 0, 0:nk], rl[:, 3, 0:nk], ALU.add, t)
                    t = vtt(wk[:, tb, nk - P:nk], wk[:, tb, nk - P:nk], con("causal"), ALU.add, t)
                    yield
                    for r in range(8):
                        if r:
                            yield
                        s0 = 32 + 8 * tb
                        src = wk[:, tb, 0:nk]
                        t = ve(lambda e, s0=s0, src=src: e.max(st[:, s0:s0 + 8], src), t)
                        t = ve(lambda e, s0=s0, src=src: e.match_replace(src, st[:, s0:s0 + 8], src, PICKED), t)
                    t = vts(mk[:, tb, 0:nk], wk[:, tb, 0:nk], -2e38, NEG, ALU.is_gt, ALU.mult, t)
                    t = vtt(mk[:, tb, nk - P:nk], mk[:, tb, nk - P:nk], con("causal"), ALU.add, t)
                    res["mask", tb] = t
                    yield

            sides[1].append(indexer())

            tq = [[], []]
            for part in range(2):
                held, t = streamed(4, hh, t_h, toks=512, on=go)
                for tb, (b, bk, _) in enumerate(held):
                    free[b] = act(qk[tb][:, 4 * part:4 * part + 4].rearrange("p h d -> p (h d)"), bk[:, :],
                                  ACT.Copy, t)
                    tq[tb].append(free[b])
            held, t = streamed(4, hh, t_h, toks=512, on=go)
            for tb, (b, bk, _) in enumerate(held):
                free[b] = t_vA = act(vA[:, tb], bk[:, :], ACT.Copy, t)

            def sparse():
                trs = []
                for tb in range(2):
                    v = qk[tb]
                    sq = xnf[:, 1024 * tb:1024 * tb + 1024].rearrange("p (h d) -> p h d", h=8)
                    t = act(sq, v, ACT.Square, tq[tb])
                    s0 = 48 + 24 * tb
                    t = ve(lambda e, s0=s0, sq=sq: e.tensor_reduce(st[:, s0:s0 + 8], sq, AX.X, ALU.add), t)
                    t = vts(st[:, s0:s0 + 8], st[:, s0:s0 + 8], 1.0 / 128, 1e-6, ALU.mult, ALU.add, t)
                    t = vtt(st[:, s0 + 8:s0 + 16], st[:, s0:s0 + 8], half(8), ALU.pow, t, q=po)
                    t = vtt(v, v, bc(st[:, s0 + 8:s0 + 16], [P, 8, P], 2), ALU.mult, t)
                    yield
                    vtt(v[:, 0:4], v[:, 0:4], bc(row("g_q", l), [P, 4, P]), ALU.mult, t, GAIN)
                    t = vtt(v[:, 4:8], v[:, 4:8], bc(row("g_k", l), [P, 4, P]), ALU.mult, t, GAIN)
                    tmp = sq.rearrange("p h d -> p (h d)")[:, 0:512].rearrange("p (a h d) -> p a h d", a=4, h=8)
                    trs.append(rope(v, 8, 16, cs[:, tb, 0:16], cs[:, tb, 24:40], tmp, [t, t_cs]))
                    yield
                te = []
                for tb in range(2):
                    for hh in (0, 4):
                        b, bk, fr = bank("s")
                        for h in range(4):
                            t = turnover(bk[:, h * P:h * P + P], qk[tb][:, hh + h, :], trs[tb], fr)
                        t = act(qkT[:, hh:hh + 4, tb * P:tb * P + P],
                                bk[:, :].rearrange("p (h k) -> p h k", h=4), ACT.Copy, t, trs)
                        free[b] = t
                        te.append(t)
                    yield
                while ("mask", 1) not in res or "wo_c" not in res:
                    yield

                def outp(tb, bk, pr, nkb, aft):
                    for h in range(4):
                        t = group(bk[:, h * P:h * P + P], [pr(h, kb) for kb in range(nkb)], aft)
                    e_ = split(F[1][0][:, :, tb * P:tb * P + P], F[1][1][:, :, tb * P:tb * P + P],
                               bk[:, :].rearrange("p (h k) -> p h k", h=4), t, res["wo_c"])
                    res["ya", tb] = e_
                    return t, e_

                yield from attend(lgs, lambda h, tb: qkT[:, h, tb * P:tb * P + P],
                                  lambda h, k0, k1: qkT[:, 4 + h, k0:k1],
                                  lambda h, kb: vA[:, kb, h * P:h * P + P], te, t_vA, float(P) ** -0.5,
                                  lambda tb, hp: bc(mk[:, tb, 0:P * (tb + 1)], [P, 2, P * (tb + 1)]),
                                  [res["mask", 0], res["mask", 1]], outp, 96)

            sides[1].append(sparse())
            tsq = []
            for dst, sc_ in ((sqT, float(P) ** -0.5), (skT, 1.0)):
                held, t = streamed(4, hh, t_h, chans=4, on=go)
                for p_, (b, bk, _) in enumerate(held):
                    free[b] = act(dst[:, 2 * p_:2 * p_ + 2].rearrange("p c s -> p (c s)"), bk[:, :], ACT.Copy, t,
                                  scale=sc_)
                    tsq.append(free[b])
            held, t = streamed(4, hh, t_h, toks=512, on=go)
            for tb, (b, bk, _) in enumerate(held):
                free[b] = act(sv[:, tb], bk[:, :], ACT.Copy, t)
                tsq.append(free[b])

            def stick():
                while "yb" not in res:
                    yield
                tls = []
                for g in range(3):
                    b, bk, fr = bank("s")
                    if g < 2:
                        for j in range(2):
                            h = 2 * g + j
                            t = group(bk[:, j * S:j * S + S], [(skT[:, h, 0:P], sqT[:, h, :])], tsq, fr)
                        dst, m = lk0[:, 2 * g:2 * g + 2].rearrange("p c s -> p (c s)"), bc(con("m0"), [P, 2, S])
                        shp = dict(c=2)
                    else:
                        for h in range(4):
                            t = group(bk[:, h * P:h * P + P], [(skT[:, h, P:S], sqT[:, h, P:S])], tsq, fr)
                        dst, m = lk1.rearrange("p c s -> p (c s)"), bc(con("m0", 0, P), [P, 4, P])
                        shp = dict(c=4)
                    t = act(dst, bk[:, :], ACT.Abs, t, res["yb"])
                    t = act(dst, dst, ACT.Exp, t, scale=-1.0)
                    t = act(dst, dst, ACT.Ln, t, bias=1.0)
                    t = vst(dst, bk[:, :], 0.0, dst, ALU.max, ALU.add, t)
                    free[b] = t
                    d3 = dst.rearrange("p (c s) -> p c s", **shp)
                    tls.append(vtt(d3, d3, m, ALU.mult, t))
                    yield
                a0, a1 = lk0, lk1
                tas = []
                hold = []
                for g in range(2):
                    b, bk, fr = bank("s")
                    for j in range(2):
                        h = 2 * g + j
                        o = bk[:, j * S:j * S + S]
                        group(o, [(con("trirev"), lk0[:, h]), (skT[:, h, 0:P], sqT[:, h, :])], tls, fr, stop=False)
                        t = group(bk[:, j * S + P:j * S + S], [(onesb[:, :], lk1[:, h])], start=False)
                    hold.append((b, bk, t))
                b, bk, fr = bank("s")
                for h in range(4):
                    t = group(bk[:, h * P:h * P + P], [(con("trirev"), lk1[:, h]),
                                                       (skT[:, h, P:S], sqT[:, h, P:S])], fr)
                hold.append((b, bk, t))
                for g, (b, bk, t1) in enumerate(hold):
                    if g < 2:
                        dst, m, n = a0[:, 2 * g:2 * g + 2], bc(con("n0"), [P, 2, S]), 2
                    else:
                        dst, m, n = a1, bc(con("n0", 0, P), [P, 4, P]), 4
                    t = vst(dst, bk[:, :].rearrange("p (c s) -> p c s", c=n), 0.0, m, ALU.min, ALU.add, t)
                    free[b] = t
                    tas.append(act(dst, dst, ACT.Exp, t))
                while "wo_b" not in res:
                    yield
                yd = []
                for g in range(2):
                    b, bk, fr = bank("s")
                    for j in range(2):
                        h = 2 * g + j
                        group(bk[:, j * S:j * S + S], [(sv[:, 0, h * P:h * P + P], a0[:, h])], tas, fr, stop=False)
                        t = group(bk[:, j * S + P:j * S + S], [(sv[:, 1, h * P:h * P + P], a1[:, h])], start=False)
                    yd += split(F[0][0][:, 2 * g:2 * g + 2], F[0][1][:, 2 * g:2 * g + 2],
                                bk[:, :].rearrange("p (c s) -> p c s", c=2), t, res["wo_b"])
                    free[b] = yd[-1]
                res["yd"] = yd
                yield

            sides[1].append(stick())

            held, t = streamed(4, hh, t_h, chans=4, on=go)
            for p_, (b, bk, _) in enumerate(held):
                free[b] = tgc = act(yc[:, 2 * p_:2 * p_ + 2].rearrange("p c s -> p (c s)"), bk[:, :], ACT.Copy, t)
            held, t = streamed(4, hh, t_h, chans=4, on=go)
            tc_ = []
            for p_, (b, bk, _) in enumerate(held):
                free[b] = vtt(ccp[:, 2 * p_:2 * p_ + 2, 2:258], bk[:, :].rearrange("p (c s) -> p c s", c=2),
                              yc[:, 2 * p_:2 * p_ + 2], ALU.mult, t, tgc)
                tc_.append(free[b])
            held, t = streamed(4, hh, t_h, chans=4, on=go)
            tb_ = []
            for p_, (b, bk, _) in enumerate(held):
                free[b] = act(gbS[:, 2 * p_:2 * p_ + 2].rearrange("p c s -> p (c s)"), bk[:, :], ACT.Copy, t,
                              (s_sc, 16))
                tb_.append(free[b])

            def short_branch():
                for j in range(3):
                    for c in range(4):
                        wv = prm("cc_w", l, c * 3 + j, c * 3 + j + 1)
                        if j == 0:
                            t = vts(yc[:, c], ccp[:, c, 0:S], wv, None, ALU.mult, None, tc_, PAR, z2)
                        else:
                            t = vst(yc[:, c], ccp[:, c, j:j + S], wv, yc[:, c], ALU.mult, ALU.add, t)
                    yield
                t = vtt(yc, yc, gbS, ALU.mult, t, tb_)
                res["yc"] = split(F[1][0], F[1][1], yc, t)
                yield

            sides[1].append(short_branch())

            mprev = [None] * 4
            for n_b, (bi, key, r) in enumerate(((1, "yb", 0), (2, "yc", 1), (3, "yd", 0), (0, "ya", 1))):
                for hf in range(2):
                    held, t = streamed(4, hh, t_h, chans=4, on=go)
                    tsg = []
                    for p_, (b, bk, _) in enumerate(held):
                        for j in range(2):
                            c = 8 * bi + 4 * hf + 2 * p_ + j
                            free[b] = act(sgb[:, 2 * p_ + j], bk[:, j * S:j * S + S], ACT.Sigmoid, t, PAR,
                                          res["sgb"], bias=prm("b_gate", l, c, c + 1))
                            tsg.append(free[b])
                    t_gate = t
                    if n_b == 3 and hf == 1:
                        for q_ in range(2):
                            mprev[q_] = split(hhi[:, 2 * q_:2 * q_ + 2], hlo[:, 2 * q_:2 * q_ + 2],
                                              mer1[:, 2 * q_:2 * q_ + 2], mprev[q_], t_gate)
                    keys = [("ya", 0), ("ya", 1)] if key == "ya" else [key]
                    while any(k_ not in res for k_ in keys):
                        tick(sides)
                    held, t = streamed(2, F[r], [res[k_] for k_ in keys], chans=4, on=go)
                    for p_, (b, bk, _) in enumerate(held):
                        q_ = 2 * hf + p_
                        m2 = mer1[:, 2 * q_:2 * q_ + 2]
                        g2 = sgb[:, 2 * p_:2 * p_ + 2]
                        b3 = bk[:, :].rearrange("p (c s) -> p c s", c=2)
                        if n_b == 0:
                            while ("mask", 1) not in res:
                                tick(sides)
                            mprev[q_] = free[b] = res["sgb"] = vtt(m2, b3, g2, ALU.mult, t, tsg, res["mask", 1])
                        else:
                            free[b] = vtt(g2, b3, g2, ALU.mult, t, tsg)
                            mprev[q_] = res["sgb"] = vtt(m2, m2, g2, ALU.add, free[b], mprev[q_],
                                                         q=ve if n_b == 3 else po)
                        if n_b == 3 and hf == 1:
                            mprev[q_] = split(hhi[:, 2 * q_:2 * q_ + 2], hlo[:, 2 * q_:2 * q_ + 2], m2,
                                              mprev[q_], t_gate)
                res["wo_" + "abcd"[bi]] = t
            drain(sides)
            t_x = row_out((hhi, hlo), mprev, t_x)

            t_h = normed_T(l, "g_ffn", t_x)
            z3 = ve(lambda e: e.memset(gpad[:, :, :, 0:2], 0.0), t_x)
            acc = [bank("s") for _ in range(4)]
            fre = [None, None]
            pend = None
            y = A1.rearrange("p (c s) -> p c s", c=4)
            sg = B1.rearrange("p (c s) -> p c s", c=4)
            lastg = [z3, z3]

            def down(i6, kn, tf):
                t_nh = [None, None]
                for k in range(0, kn, 2):
                    for nh in range(2):
                        _, t_nh[nh] = streamed(1, F[i6 % 2], tf, toks=512, held=[acc[nh], acc[2 + nh]], k0=k,
                                         first_=i6 == 0 and k == 0, final=i6 == 5 and k == kn - 2)
                fre[i6 % 2] = t_nh[1]
                return t_nh

            for i6 in range(6):
                n = 4 if i6 < 5 else 2
                held, t = streamed(4, hh, t_h, chans=n)
                ty = [None] * 4
                for p_, (b, bk, _) in enumerate(held):
                    free[b] = t1 = act(gpad[:, p_, :, 2:258],
                                       bk[:, :].rearrange("p (c s) -> p c s", c=2), ACT.Copy, t, lastg[p_])
                    for k3 in range(3):
                        for j in range(2):
                            c = 4 * i6 + 2 * p_ + j
                            wv = prm("ffn_w", l, c * 3 + k3, c * 3 + k3 + 1)
                            yy = y[:, 2 * p_ + j]
                            if k3 == 0:
                                ty[2 * p_ + j] = vts(yy, gpad[:, p_, j, 0:S], wv, None, ALU.mult, None, t1, PAR)
                            else:
                                ty[2 * p_ + j] = vst(yy, gpad[:, p_, j, k3:k3 + S], wv, yy, ALU.mult, ALU.add,
                                                     ty[2 * p_ + j])
                    lastg[p_] = ty[2 * p_ + 1]
                held, t = streamed(4, hh, t_h, chans=n)
                t1 = act(sg[:, 0:n], y[:, 0:n], ACT.Sigmoid, ty[0:n])
                t1 = vtt(y[:, 0:n], y[:, 0:n], sg[:, 0:n], ALU.mult, t1)
                tf = Pairs()
                for p_, (b, bk, _) in enumerate(held):
                    y2 = y[:, 2 * p_:2 * p_ + 2]
                    free[b] = vtt(y2, y2, bk[:, :].rearrange("p (c s) -> p c s", c=2), ALU.mult, t1, t)
                    fh, fl = F[i6 % 2]
                    tf.append(split(fh[:, 2 * p_:2 * p_ + 2], fl[:, 2 * p_:2 * p_ + 2], y2, free[b], fre[i6 % 2]))
                if pend:
                    down(*pend)
                pend = (i6, n, tf)
            return row_add(acc, down(*pend))

        def row_add(acc, t_nh):
            t_x = [None] * 4
            for tb, nh in ((0, 0), (1, 0), (0, 1), (1, 1)):
                b, bk = acc[2 * tb + nh][0:2]
                xs = x[:, tb, nh * 512:nh * 512 + 512]
                free[b] = t_x[2 * tb + nh] = vtt(xs, bk[:, :], xs, ALU.add, t_nh[nh])
            return t_x

        def row_out(src, t_src, t_x, order=(0, 1, 2, 3)):
            acc = [bank("m") for _ in range(4)]
            t_nh = [None, None]
            for n, c in enumerate(order):
                for nh in range(2):
                    _, t_nh[nh] = streamed(1, src, t_src[c], toks=512, held=[acc[nh], acc[2 + nh]], k0=2 * c,
                                    first_=n == 0, final=n == 3)
            return row_add(acc, t_nh)

        def bias_tiles(t_x):
            for h in range(4):
                dma(ac, big[:, h * S:(h + 1) * S], a["toep"][h], s_bi, (s_sc, 16), t_x)
            dma(ac, bufA[:, 0:128], a["flip"], s_fl)
            for h in range(4):
                b, bk, fr = bank("s")
                t = group(bk[:, 0:S], [(bufA[:, 0:128], big[:, h * S:(h + 1) * S])], (s_bi, 64), (s_fl, 16), fr)
                t = vcp(bia[:, h, :], bk[:, 0:S], t)
                free[b] = t
                t = vtt(bia[:, h, 128:256], bia[:, h, 128:256], con("causal"), ALU.add, t)
            return t

        t_bias = [None]

        def block2(l, t_x):
            if l == 0:
                t_bias[0] = bias_tiles(t_x)
            z4 = ve(lambda e: e.memset(gdp[:, :, :, 0:3], 0.0), t_x)
            dma(ac, wuq[:, :, :], a["mla_w_uq_2"][l].rearrange("(k p) n -> p k n", p=P), s_u, t_x)
            dma(ac, wukv[:, :], a["mla_w_ukv_2"][l], s_u)
            t_wu = (s_u, 32 * (l + 1))
            t_h = normed_T(l, "norm2", t_x)
            res = {}
            sides = ([], [])
            yT = mer
            m0 = xn[:, :, 0:416]
            mtmp = xn[:, :, 416:1024]
            hh = (hhi, hlo)

            def go():
                tick(sides)

            qm = [bufA[:, 0:384].rearrange("p (h d) -> p h d", h=4), bufB[:, 0:384].rearrange("p (h d) -> p h d", h=4)]
            km = [bufA[:, 384:768].rearrange("p (h d) -> p h d", h=4), bufB[:, 384:768].rearrange("p (h d) -> p h d", h=4)]
            vm = [bufA[:, 768:1024], bufB[:, 768:1024]]
            lgs = [bufC[:, :], bufD[:, :]]
            cqT = bufE[:, 0:512].rearrange("p (k s) -> p k s", k=2)
            ckT = bufE[:, 512:768]
            qmT = bufF[:, :].rearrange("p (h s) -> p h s", s=S)
            kmT = bufG[:, :].rearrange("p (h s) -> p h s", s=S)

            def latent():
                tn = []
                for tb in range(2):
                    s0 = 16 + 8 * tb
                    t1 = act(mtmp[:, tb, 0:256], m0[:, tb, 0:256], ACT.Square, tm[tb], accum_out=st[:, s0:s0 + 1])
                    t2 = act(bufC[:, 512 + 128 * tb:640 + 128 * tb], m0[:, tb, 256:384], ACT.Square, accum_out=st[:, s0 + 1:s0 + 2])
                    t1 = vts(st[:, s0:s0 + 1], st[:, s0:s0 + 1], 1.0 / 256, 1e-6, ALU.mult, ALU.add, t1)
                    t2 = vts(st[:, s0 + 1:s0 + 2], st[:, s0 + 1:s0 + 2], 1.0 / 128, 1e-6, ALU.mult, ALU.add, t2)
                    t = vtt(st[:, s0 + 2:s0 + 4], st[:, s0:s0 + 2], half(2), ALU.pow, [t1, t2], q=po)
                    vts(m0[:, tb, 0:256], m0[:, tb, 0:256], st[:, s0 + 2:s0 + 3], None, ALU.mult, None, t)
                    t = vts(m0[:, tb, 256:384], m0[:, tb, 256:384], st[:, s0 + 3:s0 + 4], None, ALU.mult, None, t)
                    tn.append(t)
                yield
                b, bk, fr = bank("s")
                for c in range(2):
                    for tb in range(2):
                        t = turnover(bk[:, c * S + tb * P:c * S + tb * P + P], m0[:, tb, c * P:c * P + P], tn[tb], fr)
                tc = [act(cqT[:, c], bk[:, c * S:c * S + S], ACT.Copy, t, scale=prm("qn2", l, c, c + 1))
                      for c in range(2)]
                free[b] = tc
                b, bk, fr = bank("s")
                for tb in range(2):
                    t = turnover(bk[:, tb * P:tb * P + P], m0[:, tb, 256:384], tn[tb], fr)
                tc.append(act(ckT, bk[:, 0:S], ACT.Copy, t, scale=prm("kvn2", l)))
                free[b] = tc[-1]
                yield
                tr_ = []
                for tb in range(2):
                    b, bk, fr = bank("s")
                    t = group(bk[:, 0:384], [(cqT[:, k, tb * P:tb * P + P], wuq[:, k]) for k in range(2)],
                              tc, t_wu, fr)
                    res["wu"] = t
                    t = vts(qm[tb].rearrange("p h d -> p (h d)"), bk[:, 0:384], float(96) ** -0.5, None,
                            ALU.mult, None, t)
                    free[b] = t
                    b, bk, fr = bank("s")
                    t2 = group(bk[:, :], [(ckT[:, tb * P:tb * P + P], wukv[:, :])], tc, fr)
                    res["wu"] = t2
                    kv = bk[:, :].rearrange("p (h d) -> p h d", h=4)
                    t3 = act(km[tb][:, :, 0:64], kv[:, :, 0:64], ACT.Copy, t2)
                    t4 = act(vm[tb].rearrange("p (h d) -> p h d", h=4), kv[:, :, 64:128], ACT.Copy, t2)
                    free[b] = t4
                    cos, sin = con("rope2", 32 * tb, 32 * tb + 16), con("rope2", 32 * tb + 16, 32 * tb + 32)
                    tmp = mtmp[:, tb, 0:256].rearrange("p (a h d) -> p a h d", a=4, h=4)
                    t = rope(qm[tb][:, :, 64:96], 4, 16, cos, sin, tmp, [t])
                    tmp = mtmp[:, tb, 256:320].rearrange("p (a h d) -> p a h d", a=4, h=1)
                    t5 = rope(m0[:, tb, 384:416].unsqueeze(1), 1, 16, cos, sin, tmp, [tm[tb]])
                    t5 = vcp(km[tb][:, :, 64:96], bc(m0[:, tb, 384:416], [P, 4, 32]), t5)
                    tr_.append([t, t3, t5])
                    res["vm"] = t4
                    yield
                te = []
                for tb in range(2):
                    for src, dst in ((qm[tb], qmT), (km[tb], kmT)):
                        b, bk, fr = bank("s")
                        for h in range(4):
                            t = turnover(bk[0:96, h * P:h * P + P], src[:, h, :], tr_[tb], fr)
                        t = act(dst[0:96, :, tb * P:tb * P + P],
                                bk[0:96, :].rearrange("p (h k) -> p h k", h=4), ACT.Copy, t)
                        free[b] = t
                        te.append(t)
                yield

                def mask(tb, hp):
                    return bc(mk0 if tb == 0 else mk1, [P, 2, P * (tb + 1)])

                mk0 = con("causal")
                zo = CN["zero"][0]
                mk1 = cst[:, zo:zo + S]
                yield from attend(lgs, lambda h, tb: qmT[0:96, h, tb * P:tb * P + P],
                                  lambda h, k0, k1: kmT[0:96, h, k0:k1],
                                  lambda h, kb: vm[kb][:, h * 64:h * 64 + 64], te, res["vm"], 1.0,
                                  mask, CST, pair_out("mla", 0, "mg"), 96)
                while "moba_in" not in res:
                    yield

                def mqT(h, tb):
                    return cq[64 * (h % 2):64 * (h % 2) + 64, h // 2, tb * P:tb * P + P]

                def mkT(h, k0, k1):
                    return ck[64 * (h % 2):64 * (h % 2) + 64, h // 2, k0:k1]

                def mask2(tb, hp):
                    return bia[:, hp:hp + 3:2, 128:256] if tb == 0 else bia[:, hp:hp + 3:2, :]

                yield from attend(lgs, mqT, mkT, lambda h, kb: cv[:, kb, h * 64:h * 64 + 64],
                                  res["moba_in"], res["cv"], 1.0, mask2, t_bias[0], pair_out("moba", 6, "cg"), 96,
                                  rowtiles=True)

            mgs = big[:, 0:2 * S].rearrange("p (c s) -> p c s", s=S)
            cgs = big[:, 2 * S:4 * S].rearrange("p (c s) -> p c s", s=S)
            gate_of = {"mg": mgs, "cg": cgs}

            def pair_out(name, c0, gname):
                def outp(tb, bk, pr, nkb, aft):
                    for h in range(4):
                        o = bk[64 * (h % 2):64 * (h % 2) + 64, (h // 2) * P:(h // 2) * P + P]
                        t = group(o, [pr(h, kb) for kb in range(nkb)], aft)
                    e_ = act(yT[:, c0:c0 + 2, tb * P:tb * P + P],
                             bk[:, 0:2 * P].rearrange("p (h k) -> p h k", h=2), ACT.Copy, t)
                    res[name, tb] = e_
                    return t, e_
                return outp

            zs = big[:, 4 * S:8 * S].rearrange("p (h s) -> p h s", s=S)
            qc = big[:, 8 * S:12 * S].rearrange("p (h s) -> p h s", s=S)
            kc = big[:, 12 * S:16 * S].rearrange("p (h s) -> p h s", s=S)
            vc = big[:, 16 * S:20 * S].rearrange("p (h s) -> p h s", s=S)
            bg = st[:, 128:144].rearrange("p (t n) -> p t n", t=2)
            held, t = streamed(1, hh, t_h, toks=8)
            tbg = []
            for tb, (b, bk, _) in enumerate(held):
                free[b] = vcp(bg[:, tb], bk[:, 0:8], t)
                tbg.append(free[b])

            nst = [160]

            def cell(n):
                o = nst[0]
                nst[0] += n
                return st[:, o:o + n]

            beta = cell(8).rearrange("p (t h) -> p t h", t=2)
            gv = cell(8).rearrange("p (t h) -> p t h", t=2)
            gc = cell(8).rearrange("p (t h) -> p t h", t=2)
            ngc = cell(8).rearrange("p (t h) -> p t h", t=2)
            egc = cell(8).rearrange("p (t h) -> p t h", t=2)
            edl = cell(8).rearrange("p (t h) -> p t h", t=2)
            gend = cell(16).rearrange("p (t c h) -> p t c h", t=2, c=2)
            ss = cell(16).rearrange("p (q t h) -> p q t h", q=2, t=2)
            rs = cell(16).rearrange("p (q t h) -> p q t h", q=2, t=2)
            r1 = cell(8).rearrange("p (t h) -> p t h", t=2)
            r3 = cell(8).rearrange("p (t h) -> p t h", t=2)
            cw = cell(8).rearrange("p (t h) -> p t h", t=2)
            ckk = cell(8).rearrange("p (t h) -> p t h", t=2)
            ea = cell(4)
            t4a = cell(8).rearrange("p (t h) -> p t h", t=2)
            t4b = cell(8).rearrange("p (t h) -> p t h", t=2)
            assert nst[0] <= 512

            def decay_prep():
                t = act(beta, bg[:, :, 0:4], ACT.Sigmoid, tbg)
                ta = vtt(t4a, bg[:, :, 4:8], bc(prm("dtb", l), [P, 2, 4]), ALU.add, tbg)
                t1 = act(t4b, t4a, ACT.Abs, ta)
                t1 = act(t4b, t4b, ACT.Exp, t1, scale=-1.0)
                t1 = act(t4b, t4b, ACT.Ln, t1, bias=1.0)
                t2 = act(ea, prm("alog", l), ACT.Exp)
                t1 = vst(t4a, t4a, 0.0, t4b, ALU.max, ALU.add, t1, t2)
                t1 = vst(gv, t4a, -1.0, bc(ea, [P, 2, 4]), ALU.mult, ALU.mult, t1, t)
                yield
                b, bk, fr = bank("s")
                for tb in range(2):
                    t = group(bk[:, 16 * tb:16 * tb + 4], [(con("tri"), gv[:, tb])], t1, fr)
                    t = group(bk[:, 16 * tb + 4:16 * tb + 8], [(con("blk"), gv[:, tb])])
                    t = group(bk[:, 16 * tb + 8:16 * tb + 12], [(con("half0"), gv[:, tb])])
                    t = group(bk[:, 16 * tb + 12:16 * tb + 16], [(con("half1"), gv[:, tb])])
                v = bk[:, 0:32].rearrange("p (t n) -> p t n", t=2)
                t2 = vcp(gc, v[:, :, 0:4], t)
                t3 = vts(ngc, v[:, :, 0:4], -1.0, None, ALU.mult, None, t)
                t4 = vtt(edl, v[:, :, 4:8], gc, ALU.subtract, t2)
                t5 = act(gend.rearrange("p t c h -> p t (c h)"), v[:, :, 8:16], ACT.Exp, t3, t4)
                t6 = act(egc, gc, ACT.Exp, t2)
                t7 = act(edl, edl, ACT.Exp, t4)
                free[b] = [t4, t5]
                res["dec"] = [t3, t7]
                yield

            sides[0].append(decay_prep())

            nz = [0]
            lastg = [None, None]

            def conv4(dst, ci, tag):
                held, t = streamed(4, hh, t_h, chans=4, on=go)
                for p_, (b, bk, _) in enumerate(held):
                    r = p_
                    free[b] = t1 = act(gdp[:, r, :, 3:259], bk[:, :].rearrange("p (c s) -> p c s", c=2), ACT.Copy,
                                       t, lastg[r], z4)
                    tj = [t1, t1]
                    for k4 in range(4):
                        for j in range(2):
                            c = 2 * p_ + j
                            wv = prm("gdn_w", l, (ci + c) * 4 + k4, (ci + c) * 4 + k4 + 1)
                            if k4 == 0:
                                tj[j] = vts(dst[:, c], gdp[:, r, j, 0:S], wv, None, ALU.mult, None, tj[j])
                            else:
                                tj[j] = vst(dst[:, c], gdp[:, r, j, k4:k4 + S], wv, dst[:, c],
                                            ALU.mult, ALU.add, tj[j])
                    lastg[r] = list(tj)
                    tmp = bufI[:, p_ * 512:p_ * 512 + 512]
                    d2 = dst[:, 2 * p_:2 * p_ + 2].rearrange("p c s -> p (c s)")
                    t1 = act(tmp, d2, ACT.Sigmoid, tj, res.get("silu"))
                    t1 = vtt(d2, d2, tmp, ALU.mult, t1)
                    res["silu"] = t1
                    res[tag] = t1

            ktk = big[:, 20 * S:24 * S].rearrange("p (t n) -> p t n", t=2)
            ke = big[:, 24 * S:28 * S].rearrange("p (t n) -> p t n", t=2)
            vb = big[:, 28 * S:32 * S].rearrange("p (t n) -> p t n", t=2)
            Dm = bufH[:, :].rearrange("p (t n) -> p t n", t=2)
            LT = bufI[:, :].rearrange("p (t n) -> p t n", t=2)
            AT = bufJ[:, :].rearrange("p (t n) -> p t n", t=2)
            qg = vc
            TT, Mm = halves(part2(23040, 1024)), halves(bufH)
            T_ = halves(big[:, 4 * S:8 * S])
            BT = halves(yT[:, 2:6].rearrange("p c s -> p (c s)"))
            WT = kc
            U = qc
            Ut = U.rearrange("p h s -> p (h s)").rearrange("p (t n) -> p t n", t=2)
            Sst = [gs[:, h // 2, h % 2] for h in range(4)]

            def delta():
                while "qc" not in res:
                    yield
                sqk, sqq = bufH, part2(23040, 1024)
                t1 = act(sqk, kc.rearrange("p h s -> p (h s)"), ACT.Square,
                         res["kc"], res["silu"])
                t2 = act(sqq, qc.rearrange("p h s -> p (h s)"), ACT.Square, res["qc"])
                b, bk, fr = bank("s")
                for q_, src in ((0, sqk), (1, sqq)):
                    sv_ = src.rearrange("p (h s) -> p h s", s=S)
                    for tb in range(2):
                        for h in range(4):
                            c = q_ * 8 + tb * 4 + h
                            t = group(bk[:, c:c + 1], [(sv_[:, h, tb * P:tb * P + P], onesb[:, 0:1])], t1, t2, fr)
                t = vts(ss.rearrange("p q t h -> p (q t h)"), bk[:, 0:16], 1e-6, None, ALU.add, None, t)
                free[b] = t
                t = vtt(rs.rearrange("p q t h -> p (q t h)"), ss.rearrange("p q t h -> p (q t h)"),
                        half(16), ALU.pow, t, q=po)
                tq_ = vts(rs[:, 1], rs[:, 1], float(P) ** -0.5, None, ALU.mult, None, t)
                t1 = vtt(r1, rs[:, 0], beta, ALU.mult, t, res["dec"])
                t3 = vtt(r3, rs[:, 1], egc, ALU.mult, tq_)
                t4 = vst(cw, r1, -1.0, egc, ALU.mult, ALU.mult, t1)
                t5 = vtt(ckk, rs[:, 0], edl, ALU.mult, t)
                yield
                tt3 = []
                for tb in range(2):
                    b, bk, fr = bank("s")
                    for h in range(4):
                        t = turnover(bk[:, h * P:h * P + P], kc[:, h, tb * P:tb * P + P], fr, res["kc"])
                    v3 = bk[:, :].rearrange("p (h d) -> p h d", h=4)
                    ta = vtt(ktk[:, tb].rearrange("p (h d) -> p h d", h=4), v3, bc(cw[:, tb], [P, 4, P], 2),
                             ALU.mult, t, t4)
                    tb_2 = vtt(ke[:, tb].rearrange("p (h d) -> p h d", h=4), v3, bc(ckk[:, tb], [P, 4, P], 2),
                               ALU.mult, t, t5)
                    free[b] = tb_2
                    yield
                    while "vc" not in res:
                        yield
                    b, bk, fr = bank("s")
                    for h in range(4):
                        t = turnover(bk[:, h * P:h * P + P], vc[:, h, tb * P:tb * P + P], fr, res["vc"])
                    v3 = bk[:, :].rearrange("p (h d) -> p h d", h=4)
                    tc = vtt(vb[:, tb].rearrange("p (h d) -> p h d", h=4), v3, bc(beta[:, tb], [P, 4, P], 2),
                             ALU.mult, t)
                    free[b] = tc
                    tt3.append(tc)
                    yield
                for tb in range(2):
                    pr_ = []
                    for vec, mat, dst in ((gv, con("tri"), 0), (r1, ident, 1), (rs[:, 1], ident, 2), (r3, ident, 3)):
                        b, bk, fr = bank("s")
                        for h in range(4):
                            t = group(bk[:, h * P:h * P + P], [(vec[:, tb, h:h + 1].to_broadcast([P, P]), mat)],
                                      t1, t3, tq_, fr)
                        if dst == 0:
                            for h in range(4):
                                tt = vts(Dm[:, tb, h * P:h * P + P], bk[:, h * P:h * P + P], ngc[:, tb, h:h + 1], 0.0,
                                         ALU.add, ALU.min, t)
                            free[b] = tt
                            tt = act(Dm[:, tb], Dm[:, tb], ACT.Exp, tt)
                            td = vtt(Dm[:, tb].rearrange("p (h d) -> p h d", h=4),
                                     Dm[:, tb].rearrange("p (h d) -> p h d", h=4),
                                     bc(con("tri"), [P, 4, P]), ALU.mult, tt)
                        elif dst == 1:
                            tD1 = vtt(LT[:, tb], Dm[:, tb], bk[:, :], ALU.mult, t, td)
                            free[b] = tD1
                        elif dst == 2:
                            tD2 = vtt(AT[:, tb], Dm[:, tb], bk[:, :], ALU.mult, t)
                            free[b] = tD2
                        else:
                            tqg = vtt(qg[:, :, tb * P:tb * P + P], qc[:, :, tb * P:tb * P + P],
                                      bk[:, :].rearrange("p (h d) -> p h d", h=4), ALU.mult, t, tt3)
                            free[b] = tqg
                    yield
                    for src, dst in ((kc, LT), (qc, AT)):
                        b, bk, fr = bank("s")
                        for h in range(4):
                            t = group(bk[:, h * P:h * P + P],
                                      [(kc[:, h, tb * P:tb * P + P], src[:, h, tb * P:tb * P + P])], fr)
                        for h in range(4):
                            sl = slice(h * P, h * P + P)
                            tt = vst(dst[:, tb, sl], bk[:, sl], rs[:, 0, tb, h:h + 1], dst[:, tb, sl],
                                     ALU.mult, ALU.mult, t, tD1, tD2)
                        free[b] = tt
                    res["A", tb] = tt
                    l3 = LT[:, tb].rearrange("p (h d) -> p h d", h=4)
                    res["L", tb] = vtt(l3, l3, bc(con("strict"), [P, 4, P]), ALU.mult, tt)
                    yield
                cur = {}
                for lv in range(6):
                    tB = [vtt(BT[tb].rearrange("p (h d) -> p h d", h=4),
                              LT[:, tb].rearrange("p (h d) -> p h d", h=4),
                              bc(con("lv", lv * P, lv * P + P), [P, 4, P]), ALU.mult,
                              res["L", tb], cur.get(("m", tb)), q=po if lv else ve) for tb in range(2)]
                    if lv == 0:
                        id4 = bc(ident, [P, 4, P])
                        for tb in range(2):
                            b, bk, fr = bank("s")
                            for h in range(4):
                                t = group(bk[:, h * P:h * P + P], [(BT[tb][:, h * P:h * P + P], ident)], tB[tb], fr)
                            cur["m", tb] = t
                            cur["T", tb] = vtt(T_[tb].rearrange("p (h d) -> p h d", h=4), id4,
                                               bk[:, :].rearrange("p (h d) -> p h d", h=4), ALU.subtract, t)
                            free[b] = cur["T", tb]
                            cur["TT", tb] = vtt(TT[tb].rearrange("p (h d) -> p h d", h=4), id4,
                                                BT[tb].rearrange("p (h d) -> p h d", h=4), ALU.subtract, tB[tb])
                            cur["m", tb] = [t, cur["TT", tb]]
                        yield
                        continue
                    tM = []
                    for tb in range(2):
                        b, bk, fr = bank("s")
                        for h in range(4):
                            sl = slice(h * P, h * P + P)
                            t = group(bk[:, sl], [(BT[tb][:, sl], T_[tb][:, sl])], tB[tb], cur["T", tb], fr)
                        cur["m", tb] = t
                        t = act(Mm[tb], bk[:, :], ACT.Copy, t, cur.get(("u", tb)))
                        free[b] = t
                        tM.append(t)
                    yield
                    for tb in range(2):
                        b, bk, fr = bank("s")
                        for h in range(4):
                            sl = slice(h * P, h * P + P)
                            t = group(bk[:, sl], [(Mm[tb][:, sl], TT[tb][:, sl])], tM[tb], cur["TT", tb], fr)
                        if lv < 5:
                            b2, bk2, fr2 = bank("s")
                            for h in range(4):
                                sl = slice(h * P, h * P + P)
                                t_2 = group(bk2[:, sl], [(TT[tb][:, sl], Mm[tb][:, sl])], fr2)
                            cur["u", tb] = t_2
                            cur["T", tb] = vtt(T_[tb], T_[tb], bk2[:, :], ALU.subtract, t_2)
                            free[b2] = cur["T", tb]
                        else:
                            t_2 = t
                        cur["TT", tb] = vtt(TT[tb], TT[tb], bk[:, :], ALU.subtract, t_2)
                        free[b] = cur["TT", tb]
                    if lv == 5:
                        res["T_free"] = [cur["m", 0], cur["m", 1]]
                    yield
                tW = []
                for tb in range(2):
                    b, bk, fr = bank("s")
                    for h in range(4):
                        sl = slice(h * P, h * P + P)
                        t = group(bk[:, sl], [(ktk[:, tb, sl], TT[tb][:, sl])], cur["TT", tb], fr)
                    t = act(WT[:, :, tb * P:tb * P + P], bk[:, :].rearrange("p (h d) -> p h d", h=4), ACT.Copy, t,
                            res["A", 1])
                    free[b] = t
                    tW.append(t)
                yield
                tS = None
                for c in range(4):
                    tb, hf = c // 2, c % 2
                    rows = slice(64 * hf, 64 * hf + 64)
                    cols = slice(tb * P + 64 * hf, tb * P + 64 * hf + 64)
                    b, bk, fr = bank("s")
                    for h in range(4):
                        sl = slice(h * P, h * P + P)
                        pairs = [(TT[tb][:, sl], vb[:, tb, sl])]
                        if c:
                            pairs.append((WT[:, h, tb * P:tb * P + P], Sst[h]))
                        t = group(bk[:, sl], pairs, tW, tS, fr)
                    tU = vcp(Ut[rows, tb], bk[rows, :], t, res["A", 1])
                    free[b] = tU

                    def one(o, pr, *after, start=False, stop=False):
                        return pe(lambda e: e.matmul(o, pr[0], pr[1], start=start, stop=stop,
                                                     skip_group_check=True), *after)

                    bo, bko, fro = bank("s")
                    if c:
                        for h in range(4):
                            one(bko[:, h * 64:h * 64 + 64], (Sst[h], qg[:, h, cols]), tqg, fro, start=h == 0)
                    if c < 3:
                        b, bk, fr = bank("s")
                        for h in range(4):
                            t = group(bk[:, h * P:h * P + P],
                                      [(ke[rows, tb, h * P:h * P + P], Ut[rows, tb, h * P:h * P + P])], fr, tU)
                        if c == 0:
                            tS = vcp(gs, bk[:, :].rearrange("p (t a d) -> p t a d", t=2, a=2), t, tW)
                        else:
                            for h in range(4):
                                tS = vst(Sst[h], Sst[h], gend[:, tb, hf, h:h + 1], bk[:, h * P:h * P + P],
                                         ALU.mult, ALU.add, t)
                        free[b] = tS
                    for h in range(4):
                        t = one(bko[:, h * 64:h * 64 + 64],
                                (Ut[rows, tb, h * P:h * P + P], AT[rows, tb, h * P + 64 * hf:h * P + 64 * hf + 64]),
                                tU, fro, start=c == 0, stop=True)
                    to = act(yT[:, 2:6, cols], bko[:, 0:256].rearrange("p (h d) -> p h d", h=4), ACT.Copy, t)
                    free[bo] = to
                    yield
                o4 = yT[:, 2:6]
                sq = LT.rearrange("p t n -> p (t n)").rearrange("p (h s) -> p h s", s=S)
                t = act(sq, o4, ACT.Square, to)
                yield
                b, bk, fr = bank("s")
                for tb in range(2):
                    for h in range(4):
                        t1 = group(bk[:, tb * 4 + h:tb * 4 + h + 1],
                                   [(sq[:, h, tb * P:tb * P + P], onesb[:, 0:1])], t, fr)
                t = vts(ss[:, 0].rearrange("p t h -> p (t h)"), bk[:, 0:8], 1.0 / P, 1e-6, ALU.mult, ALU.add, t1)
                free[b] = t
                t = vtt(rs[:, 0].rearrange("p t h -> p (t h)"), ss[:, 0].rearrange("p t h -> p (t h)"), half(8),
                        ALU.pow, t, q=po)
                yield
                for p_ in range(2):
                    b, bk, fr = bank("s")
                    for j in range(2):
                        for tb in range(2):
                            t1 = group(bk[:, j * S + tb * P:j * S + tb * P + P],
                                       [(rs[:, 0, tb, 2 * p_ + j:2 * p_ + j + 1].to_broadcast([P, P]), ident)],
                                       t, fr)
                    y2 = o4[:, 2 * p_:2 * p_ + 2]
                    t1 = vst(y2, y2, prm("gdn_n", l), bk[:, :].rearrange("p (c s) -> p c s", c=2),
                             ALU.mult, ALU.mult, t1, to)
                    free[b] = t1
                    while "zs" not in res:
                        yield
                    res["gdn", p_] = vtt(y2, y2, zs[:, 2 * p_:2 * p_ + 2], ALU.mult, t1, res["zs"])
                yield


            conv4(kc, 4, "kc")
            conv4(qc, 0, "qc")
            sides[0].append(delta())
            conv4(vc, 8, "vc")
            held, t = streamed(4, hh, t_h, toks=416, on=go)
            tm = []
            for tb, (b, bk, _) in enumerate(held):
                free[b] = act(m0[:, tb], bk[:, 0:416], ACT.Copy, t)
                tm.append(free[b])
            sides[1].append(latent())

            cq = gm[:, 0:512].rearrange("p (c s) -> p c s", s=S)
            ck = gm[:, 512:1024].rearrange("p (c s) -> p c s", s=S)
            cv = gm[:, 1024:1536].rearrange("p (t n) -> p t n", t=2)
            held, t = streamed(4, hh, t_h, chans=4, on=go)
            ins = []
            for p_, (b, bk, _) in enumerate(held):
                dst = (cq if p_ == 0 else ck).rearrange("p c s -> p (c s)")
                free[b] = act(dst, bk[:, :], ACT.Copy, t, scale=0.125 if p_ == 0 else 1.0)
                ins.append(free[b])

            def silu_of(b, bk, dst, tmp, *after):
                d2 = dst.rearrange("p c s -> p (c s)")
                t1 = act(tmp, bk[:, :], ACT.Sigmoid, *after)
                free[b] = vtt(d2, bk[:, :], tmp, ALU.mult, t1)
                return free[b]

            heldv, heldg = [bank("m") for _ in range(2)], [bank("m")]
            t, tv = both(heldv, heldg, t_h, go)
            for tb, (b, bk, _) in enumerate(heldv):
                free[b] = res["cv"] = act(cv[:, tb], bk[:, 0:256], ACT.Copy, t)
            res["moba_in"] = ins
            tcg = silu_of(heldg[0][0], heldg[0][1], cgs, sgb[:, 0:2].rearrange("p c s -> p (c s)"), t)
            held, t = streamed(4, hh, t_h, chans=4, on=go)
            while "T_free" not in res:
                tick(sides)
            ve.wait(res["T_free"])
            for p_, (b, bk, _) in enumerate(held):
                res["zs"] = silu_of(b, bk, zs[:, 2 * p_:2 * p_ + 2],
                                    sgb[:, 2 * p_:2 * p_ + 2].rearrange("p c s -> p (c s)"), t, tcg)
            held, t = streamed(4, hh, t_h, chans=2, on=go)
            tmg = silu_of(held[0][0], held[0][1], mgs, sgb[:, 0:2].rearrange("p c s -> p (c s)"), t, res["zs"])
            t_last = t
            drain(sides)
            tfin = [None] * 4
            for name, c0, g, tg_ in (("mla", 0, mgs, tmg), ("moba", 6, cgs, tcg)):
                tfin[c0 // 2] = vtt(yT[:, c0:c0 + 2], yT[:, c0:c0 + 2], g, ALU.mult, tg_, res[name, 0],
                                    res[name, 1])
            tfin[1], tfin[2] = res["gdn", 0], res["gdn", 1]
            for c in (0, 3, 1, 2):
                tfin[c] = split(hhi[:, 2 * c:2 * c + 2], hlo[:, 2 * c:2 * c + 2], yT[:, 2 * c:2 * c + 2],
                                tfin[c], t_last)
            return row_out(hh, tfin, t_x, (0, 3, 1, 2))

        def both(hv, hg, t_h, go):
            pe.wait([h_[2] for h_ in hv + hg], list(t_h))
            k0 = 0
            for q_ in range(4):
                j, wh, wl, th, tl = take()
                ends = []
                for half_, tok in ((0, th), (1, tl)):
                    pe.wait(tok)
                    w_ = (wh, wl)[half_]
                    for u in range(4):
                        for k in range(2):
                            for s_ in ((hhi, hlo) if half_ == 0 else (hhi,)):
                                opens = q_ == 0 and half_ == 0 and k == 0 and s_ is hhi and u != 3
                                if u < 2:
                                    o = hv[u][1][:, 0:256]
                                    l_, r_ = s_[:, k0 + k, u * P:u * P + P], w_[:, k, 0:256]
                                else:
                                    o = hg[0][1][:, (u - 2) * S:(u - 2) * S + S]
                                    l_, r_ = w_[:, k, u * P:u * P + P], s_[:, k0 + k, :]
                                stp = q_ == 3 and half_ == 1
                                f = (lambda e, o=o, l_=l_, r_=r_, opens=opens, stp=stp:
                                     e.matmul(o, l_, r_, start=opens, stop=stp, skip_group_check=True))
                                if u == 3 and k == 1 and (half_ == 1 or s_ is hlo):
                                    ends.append(pe(f))
                                else:
                                    pe.quiet(f)
                done(j, ends[0], ends[1])
                k0 += 2
                go()
            return ends[1], None

        t_m5 = t_mh
        fnw = mer[:, 0:4].rearrange("p c s -> p (c s)")
        t_x = [XIN] * 4
        for l in range(L):
            t_x = block1(l, t_x)
        for l in range(L):
            t_x = block2(l, t_x)
        dma(ac, fnw, a["final_w"], s_fn, t_x)
        ts = [act(xn[:, tb], x[:, tb], ACT.Square, t_x, accum_out=st[:, tb:tb + 1]) for tb in range(2)]
        t = vts(st[:, 2:4], st[:, 0:2], 1.0 / D, 1e-6, ALU.mult, ALU.add, ts)
        t = vtt(st[:, 4:6], st[:, 2:4], half(2), ALU.pow, t, q=po)
        for tb in range(2):
            t2 = vst(xn[:, tb], x[:, tb], st[:, 4 + tb:5 + tb], fnw, ALU.mult, ALU.mult, t, (s_fn, 16))
            dma(sp, out[0, tb * P:tb * P + P, :], xn[:, tb], s_out, t2)
        sp.wait((s_out, 32))
        sp.wait((s_sc, 16))
        assert used[0] == len(parts)

        block = ctx.enter_context(nc.Block())

        @block.sync
        def _(e):
            sp.run(e)

        @block.gpsimd
        def _(e):
            po.run(e)

        @block.scalar
        def _(e):
            ac.run(e)

        @block.vector
        def _(e):
            ve.run(e)

        @block.tensor
        def _(e):
            pe.run(e)


def shape_constants():
    c = np.zeros((P, NCN), np.float32)

    def put(name, m):
        o, w = CN[name]
        c[0:m.shape[0], o:o + w] = m

    i = np.arange(P)
    r, q = i[:, None], i[None, :]
    same = (r // 64) == (q // 64)
    put("ident", np.eye(P))
    put("tri", same & (r <= q))
    put("strict", same & (r < q))
    lv = []
    for s in (1, 2, 4, 8, 16, 32):
        lv.append((r // (2 * s) == q // (2 * s)) & (q % (2 * s) >= s) & (r % (2 * s) < s))
    put("lv", np.concatenate(lv, 1))
    put("blk", same)
    put("half0", (r < 64) & (q >= 0))
    put("half1", (r >= 64) & (q >= 0))
    put("trirev", r >= q)
    put("causal", np.where(q <= r, 0.0, NEG))
    strict = (r < q).astype(np.float32)
    put("m0", np.concatenate([-strict, -np.ones((P, P))], 1))
    put("n0", np.concatenate([np.where(r < q, 0.0, NEG), np.zeros((P, P))], 1))
    n = np.maximum(255 - np.arange(512), 0)
    nf = np.maximum(n, 1).astype(np.float32)
    large = 16 + (np.log(nf / np.float32(16)) / np.float32(np.log(2048 / 16)) * np.float32(16)).astype(np.int32)
    bucket = np.where(n < 16, n, np.minimum(large, 31))
    oh = np.zeros((32, 512), np.float32)
    oh[bucket, np.arange(512)] = 1.0
    inv = [np.float32(500000.0) ** (-(np.arange(h, dtype=np.float32) * np.float32(2.0)) / np.float32(2 * h))
           for h in (16, 8)]
    put("invf", np.broadcast_to(np.concatenate(inv).astype(np.float32), (P, 24)))
    inv2 = (1.0 / (np.float32(10000.0) ** (np.arange(0, 32, 2, dtype=np.float32) / np.float32(32)))).astype(np.float32)
    ang = np.arange(S, dtype=np.float32)[:, None] * inv2[None, :]
    cc, ss = np.cos(ang.astype(np.float32)), np.sin(ang.astype(np.float32))
    put("rope2", np.concatenate([cc[:P], ss[:P], cc[P:], ss[P:]], 1))
    return c, oh, np.ascontiguousarray(np.eye(P, dtype=np.float32)[::-1])


def pack_params(a):
    cols = []
    for l in range(L):
        def ch(v):
            v = v.reshape(-1, v.shape[-1] // P, P)
            return v.transpose(2, 1, 0).reshape(P, -1)

        def rows(v):
            return np.broadcast_to(v[None, :], (P, v.shape[0]))

        part = {
            "g_mix": ch(a["g_mix"][l]), "b_gate": ch(a["b_gate"][l]), "cb_w": ch(a["cb_conv_w"][l]),
            "cb_b": ch(a["cb_conv_b"][l]), "ln_g": ch(a["cb_ln_g"][l]), "ln_b": ch(a["cb_ln_b"][l]),
            "cc_w": ch(a["cc_conv_w"][l]), "g_ffn": ch(a["g_ffn"][l]), "ffn_w": ch(a["ffn_conv_w"][l]),
            "norm2": ch(a["norm_w_2"][l]), "qn2": ch(a["mla_q_norm_2"][l]), "kvn2": ch(a["mla_kv_norm_2"][l]),
            "gdn_w": ch(a["gdn_conv_w_2"][l]), "gdn_n": ch(a["gdn_norm_w_2"][l]),
            "alog": rows(a["gdn_A_log_2"][l]), "dtb": rows(a["gdn_dt_bias_2"][l]),
        }
        for n in PL:
            cols.append(part[n])
    gains = [rows(a[n][l]) for l in range(L) for n in ("g_qa", "g_ka", "g_kidx")]
    return np.ascontiguousarray(np.concatenate(cols, 1)), np.ascontiguousarray(np.concatenate(gains, 1))


BIGS = ["x", "w_in", "w_oa", "w_ob", "w_oc", "w_od", "w_merge", "w_ffn_gate", "w_ffn_up", "w_ffn_down",
        "w_in_2", "mla_w_uq_2", "mla_w_ukv_2", "w_out_2", "t5_table_2"]


def kernel(**inputs):
    import concourse.bacc as bacc
    from concourse.bass_utils import run_bass_kernel_spmd

    h = {k: np.asarray(v) for k, v in inputs.items()}
    feed = {n: np.ascontiguousarray(h[n]) for n in BIGS}
    feed["pos"] = np.ascontiguousarray(h["positions"][0].reshape(2, P).T)
    feed["final_w"] = np.ascontiguousarray(np.broadcast_to(h["final_norm_w_2"][None, :], (P, D)))
    feed["params"], feed["gains"] = pack_params(h)
    feed["consts"], feed["onehot"], feed["flip"] = shape_constants()
    nc = bacc.Bacc("TRN2", target_bir_lowering=False, num_devices=1)
    a, arrays = {}, {}
    for n, v in feed.items():
        arrays[f"in_{n}"] = v
        a[n] = nc.dram_tensor(f"in_{n}", v.shape, mybir.dt.from_np(v.dtype), kind="ExternalInput").ap()
    out = nc.dram_tensor("out_x", (1, S, D), F32, kind="ExternalOutput").ap()
    scratch = nc.dram_tensor("toeplitz", (4, 512), F32, kind="Internal")
    sa = scratch.ap()
    a["scratch"] = sa
    a["toep"] = [bass.AP(tensor=sa.tensor, offset=h_ * 512, ap=[[1, P], [1, S]]) for h_ in range(4)]
    build(nc, a, out)
    r = run_bass_kernel_spmd(nc, [arrays], core_ids=[0])
    return r.results[0]["out_x"]
```

```python
from contextlib import ExitStack

import numpy as np
import concourse.bass as bass
from concourse import mybir

F32 = mybir.dt.float32
I32 = mybir.dt.int32
ALU = mybir.AluOpType
ACT = mybir.ActivationFunctionType
AX = mybir.AxisListType

P = 128
S = 256
D = 1024
L = 2
FF = 2816
NIN1 = 10052
NIN2 = 3752
SLOT = 4 * 512
NSLOT = 3
PART = 2 * 512
NPART = 4
F32R = mybir.dt.float32r
NEG = -1e30
PICKED = -3e38

PL = {}
_at = 0
for _n, _w in (("g_mix", 8), ("b_gate", 32), ("cb_w", 124), ("cb_b", 4), ("ln_g", 4), ("ln_b", 4),
               ("cc_w", 12), ("g_ffn", 8), ("ffn_w", 66), ("norm2", 8), ("qn2", 2), ("kvn2", 1),
               ("gdn_w", 48), ("gdn_n", 1), ("alog", 4), ("dtb", 4)):
    PL[_n] = (_at, _w)
    _at += _w
NPL = _at
ROWS = {"g_q": (0, 128), "g_k": (128, 128), "g_ki": (256, 64)}

CN = {}
_at = 0
for _n, _w in (("ident", 128), ("tri", 128), ("strict", 128), ("lv", 6 * 128),
               ("blk", 128), ("half0", 128), ("half1", 128), ("trirev", 128), ("zero", 128), ("causal", 128),
               ("m0", 256), ("n0", 256), ("invf", 24),
               ("rope2", 64)):
    CN[_n] = (_at, _w)
    _at += _w
NCN = _at


class Pairs(list):
    pass


class Queue:

    def __init__(self, sem):
        self.sem, self.n, self.ops, self.seen = sem, 0, [], {}

    def wait(self, *tokens):
        for t in tokens:
            if t is None:
                continue
            if isinstance(t, list):
                self.wait(*t)
            elif self.seen.get(id(t[0]), 0) < t[1]:
                self.seen[id(t[0])] = t[1]
                self.ops.append(lambda e, t=t: e.wait_ge(t[0], t[1]))

    def quiet(self, fn):
        self.ops.append(fn)

    def __call__(self, fn, *after):
        self.wait(*after)
        self.n += 1
        self.ops.append(lambda e: fn(e).then_inc(self.sem, 1))
        return (self.sem, self.n)

    def run(self, e):
        for op in self.ops:
            op(e)


def build(nc, a, out):
    ctx = ExitStack()
    with ctx:
        def sb(name, shape, dt=F32):
            return ctx.enter_context(nc.sbuf_tensor(name, shape, dt))

        def sem(name):
            return ctx.enter_context(nc.semaphore(name))

        banks = [ctx.enter_context(nc.psum_tensor(f"bank{i}", [P, 512], F32)) for i in range(8)]

        ring = sb("ring", [P, NSLOT, SLOT])
        whi = sb("whi", [P, NPART, PART], F32R)
        wlo = sb("wlo", [P, NPART, PART], F32R)
        hhi = sb("hhi", [P, 8, S], F32R)
        hlo = sb("hlo", [P, 8, S], F32R)
        cst = sb("cst", [P, NCN])
        par = sb("par", [P, L * NPL])
        onesb = sb("onesb", [P, 128])
        mhalf = sb("mhalf", [P, 1])
        posi = sb("posi", [P, 2], I32)
        posf = sb("posf", [P, 2])
        x = sb("x", [P, 2, D])
        xn = sb("xn", [P, 2, D])
        st = sb("st", [P, 512])
        cs = sb("cs", [P, 2, 48])
        sgb = sb("sgb", [P, 4, S])
        tab = sb("tab", [32, 4])
        ptb = sb("ptb", [P, 3, 4, 128])
        pt = [[ptb[:, 0], None], [ptb[:, 1], ptb[:, 2]]]

        first = ExitStack()
        fhi = first.enter_context(nc.sbuf_tensor("fhi", [P, 2, 4, S], F32R))
        flo = first.enter_context(nc.sbuf_tensor("flo", [P, 2, 4, S], F32R))
        w1 = first.enter_context(nc.sbuf_tensor("w1", [P, 18568], F32))
        first.close()
        w2 = sb("w2", [P, 24064])

        def part1(o, n):
            assert o + n <= 18568
            return w1[:, o:o + n]

        def c4(ap):
            return ap.rearrange("p (c s) -> p c s", s=S)

        A1, B1, vAf = part1(0, 1024), part1(1024, 1024), part1(2048, 1024)
        ibuf = part1(3072, 648).rearrange("p (t n) -> p t n", t=2)
        iT = part1(3720, 1280)[0:64].rearrange("p (h s) -> p h s", h=5)
        mk = c4(part1(5000, 512))
        sqT, skT = c4(part1(5512, 1024)), c4(part1(6536, 1024))
        gpad = part1(5512, 1032).rearrange("p (r c s) -> p r c s", r=2, c=2)
        sv = part1(7560, 1024).rearrange("p (t n) -> p t n", t=2)
        lk0 = c4(part1(8584, 1024))
        lk1 = part1(9608, 512).rearrange("p (h s) -> p h s", s=P)
        glup = part1(10120, 1144).rearrange("p (c s) -> p c s", c=4)
        cacc = c4(part1(11264, 1024))
        ccp = part1(12288, 1032).rearrange("p (c s) -> p c s", c=4)
        gbS, yc = c4(part1(13320, 1024)), c4(part1(14344, 1024))
        rt = part1(14344, 192).rearrange("p (t n) -> p t n", t=2)
        gains = part1(15368, 640)
        mer1 = c4(part1(16008, 2048))
        tap = part1(18056, 512).rearrange("p (r s) -> p r s", r=2)

        def part2(o, n):
            return w2[:, o:o + n]

        big = part2(0, 8192)
        bufA, bufB, bufC, bufD, bufE, bufF, bufG, bufH, bufI, bufJ = (
            part2(8192 + 1024 * i, 1024) for i in range(10))
        mer = c4(part2(18432, 2048))
        gm = part2(20480, 1536)
        bia = c4(part2(22016, 1024))
        gdp = part2(8192 + 5120, 1036).rearrange("p (r c s) -> p r c s", r=2, c=2)
        wuq = bufD[:, 0:768].rearrange("p (k n) -> p k n", k=2)
        wukv = bufC[:, 0:512]
        gs = xn[:, :, 736:992].rearrange("p t (a d) -> p t a d", a=2)
        halves = lambda b: [b[:, 0:512], b[:, 512:1024]]

        pe, ve, ac, po = (Queue(sem(n)) for n in ("s_pe", "s_dve", "s_act", "s_pool"))
        sp = Queue(sem("s_sp"))
        s_slot = [sem(f"s_slot{i}") for i in range(NSLOT)]
        s_gn, s_fl = sem("s_gn"), sem("s_fl")
        s_c, s_p, s_x, s_pos, s_tab, s_sc, s_bi, s_u, s_out, s_fn, s_id = (
            sem(n) for n in ("s_c", "s_p", "s_x", "s_pos", "s_tab", "s_sc", "s_bi", "s_u", "s_out", "s_fn", "s_id"))

        def con(name, a0=0, a1=None):
            o, w = CN[name]
            return cst[:, o + a0:o + (w if a1 is None else a1)]

        def prm(name, layer, a0=0, a1=None):
            o, w = PL[name]
            o += layer * NPL
            return par[:, o + a0:o + (w if a1 is None else a1)]

        def row(name, layer):
            o, w = ROWS[name]
            return gains[:, layer * 320 + o:layer * 320 + o + w]

        def dma(q, dst, src, s, *after):
            q.wait(*after)
            q.quiet(lambda e: e.dma_start(dst, src).then_inc(s, 16))

        ident = con("ident")

        loads, parts = [], []

        def load(src, cuts):
            k, n = src.shape[1], src.shape[2]
            assert k * n <= SLOT
            for c in cuts:
                parts.append((len(loads),) + c)
            loads.append((src, k, n))

        def load_k8(w, c0, c1):
            for k in (0, 4):
                load(w[:, k:k + 4, c0:c1], [(0, 2, 0, c1 - c0), (2, 4, 0, c1 - c0)])

        def load_list():
            for l in range(L):
                w = a["w_in"][l].rearrange("(k p) n -> p k n", p=P)
                for c0, c1 in [(2372, 2884), (1860, 2372), (1536, 1860), (0, 512), (512, 1024), (1024, 1536),
                               (4420, 4932), (4932, 5444), (5444, 5956),
                               (3396, 3908), (3908, 4420), (2884, 3396)]:
                    load_k8(w, c0, c1)
                for n, bi in (("w_ob", 1), ("w_oc", 2), ("w_od", 3), ("w_oa", 0)):
                    wo = a[n][l].rearrange("(k p) n -> p k n", p=P)
                    for hf in range(2):
                        load_k8(w, 5956 + 1024 * bi + 512 * hf, 6468 + 1024 * bi + 512 * hf)
                        load(wo[:, :, 512 * hf:512 * hf + 512], [(0, 2, 0, 512), (2, 4, 0, 512)])
                w = a["w_merge"][l].rearrange("(k p) n -> p k n", p=P)
                for i in range(4):
                    load(w[:, 2 * i:2 * i + 2, :], [(0, 2, 0, 512), (0, 2, 512, 1024)])
                g = a["w_ffn_gate"][l].rearrange("(k p) n -> p k n", p=P)
                u = a["w_ffn_up"][l].rearrange("(k p) n -> p k n", p=P)
                w = a["w_ffn_down"][l].rearrange("(k p) n -> p k n", p=P)

                def down(i):
                    for k in range(4 * i, min(4 * i + 4, 22), 2):
                        load(w[:, k:k + 2, :], [(0, 2, 0, 512), (0, 2, 512, 1024)])

                for i in range(6):
                    e = min(512 * i + 512, FF)
                    load_k8(g, 512 * i, e)
                    load_k8(u, 512 * i, e)
                    if i:
                        down(i - 1)
                down(5)
            for l in range(L):
                w = a["w_in_2"][l].rearrange("(k p) n -> p k n", p=P)
                load_k8(w, 1184, 1696)
                load(w[:, :, 2720:2728], [(0, 8, 0, 8)])
                for c0, c1 in [(672, 1184), (0, 416), (1696, 2208), (2728, 3240), (3240, 3752),
                               (416, 672), (2208, 2720)]:
                    load_k8(w, c0, c1)
                w = a["w_out_2"][l].rearrange("(k p) n -> p k n", p=P)
                for i in (0, 3, 1, 2):
                    load(w[:, 2 * i:2 * i + 2, :], [(0, 2, 0, 512), (0, 2, 512, 1024)])

        load_list()
        last_part = [max(j for j, p_ in enumerate(parts) if p_[0] == i) for i in range(len(loads))]
        used = [0]
        cutq = [0]
        landed = {}
        hi_done, lo_done, low_made = {}, {}, {}
        calm = [False]

        def issue(i, *after):
            if i < len(loads):
                src, k, n = loads[i]
                dma(sp, ring[:, i % NSLOT, 0:k * n].rearrange("p (k n) -> p k n", k=k), src,
                    s_slot[i % NSLOT], *after)

        def split_part(j):
            i, k0, k1, c0, c1 = parts[j]
            _, k, n = loads[i]
            src = ring[:, i % NSLOT, 0:k * n].rearrange("p (k n) -> p k n", k=k)[:, k0:k1, c0:c1]
            size = (k1 - k0) * (c1 - c0)
            h_, l_ = (w_[:, j % NPART, 0:size].rearrange("p (k n) -> p k n", k=k1 - k0) for w_ in (whi, wlo))
            th = act(h_, src, ACT.Copy, (s_slot[i % NSLOT], 16 * (i // NSLOT + 1)), hi_done.get(j - NPART),
                     low_made.get(j - NPART))
            tl = vtt(l_, src, h_, ALU.subtract, th, lo_done.get(j - NPART), q=po if calm[0] or j % 3 == 1 else ve)
            landed[j] = (h_, l_, th, tl)
            low_made[j] = tl
            if j == last_part[i]:
                issue(i + NSLOT, [low_made[j_] for j_, p_ in enumerate(parts[:j + 1]) if p_[0] == i])

        def take():
            j = used[0]
            used[0] += 1
            while cutq[0] <= min(j + NPART - 1, len(parts) - 1) and cutq[0] - NPART < j:
                split_part(cutq[0])
                cutq[0] += 1
            return (j,) + landed.pop(j)

        def done(j, th, tl):
            hi_done[j], lo_done[j] = th, tl
            while cutq[0] <= min(j + NPART, len(parts) - 1):
                split_part(cutq[0])
                cutq[0] += 1

        free = [None] * 8
        turn = {"m": 0, "s": 0}

        def bank(kind):
            b = turn[kind] % 4 + (4 if kind == "s" else 0)
            turn[kind] += 1
            return b, banks[b], free[b]

        def group(o, pairs, *after, start=True, stop=True, tr=False):
            pe.wait(*after)
            tok = None
            for i, (l_, r_) in enumerate(pairs):
                last = i == len(pairs) - 1
                f = (lambda e, l_=l_, r_=r_, i=i, last=last:
                     e.matmul(o, l_, r_, start=start and i == 0, stop=stop and last))
                if last:
                    tok = pe(f)
                else:
                    pe.quiet(f)
            return tok

        def turnover(o, i_, *after):
            k = i_.shape[0]
            return pe(lambda e: e.transpose(o, i_, ident[0:k, 0:k]), *after)

        def vtt(o, i0, i1, op, *after, q=None):
            return (q or ve)(lambda e: e.tensor_tensor(o, i0, i1, op), *after)

        def vts(o, i0, s1, s2, o1, o2, *after, q=None):
            if s2 is None:
                return (q or ve)(lambda e: e.tensor_scalar(o, i0, s1, None, o1), *after)
            return (q or ve)(lambda e: e.tensor_scalar(o, i0, s1, s2, o1, o2), *after)

        def vst(o, i0, s_, i1, o1, o2, *after, q=None):
            return (q or ve)(lambda e: e.scalar_tensor_tensor(out=o, in0=i0, scalar=s_, in1=i1, op0=o1, op1=o2), *after)

        def vcp(o, i_, *after, q=None):
            return (q or ve)(lambda e: e.tensor_copy(o, i_), *after)

        def act(o, i_, f, *after, **kw):
            return ac(lambda e: e.activation(o, i_, f, **kw), *after)

        def half(n):
            return mhalf[:, :].to_broadcast([P, n])

        def bc(ap, shape, ax=1):
            return ap.unsqueeze(ax).to_broadcast(shape)

        def split(h_, l_, src, *after):
            th = act(h_, src, ACT.Copy, *after)
            return [th, vtt(l_, src, h_, ALU.subtract, th)]

        def streamed(nparts, src, t_src, chans=None, toks=None, held=None, k0=0, first_=True, final=True,
                     on=None, mid=None):
            sh, sl = src
            nb = 2 if toks else (chans + 1) // 2
            if held is None:
                held = [bank("m") for _ in range(nb)]
            for q_ in range(nparts):
                j, wh, wl, th, tl = take()
                kn = wh.shape[1]
                if q_ == 0:
                    pe.wait([h_[2] for h_ in held])
                pe.wait([t_src[c] for c in range(k0 // 2, (k0 + kn + 1) // 2)] if isinstance(t_src, Pairs)
                        else t_src)
                ends = []
                for half_, tok in ((0, th), (1, tl)):
                    pe.wait(tok)
                    w_ = (wh, wl)[half_]
                    todo = []
                    for u in range(2 if toks else chans):
                        for k in range(kn):
                            for s_ in ((sh, sl) if half_ == 0 else (sh,)):
                                if toks:
                                    o = held[u][1][:, 0:toks]
                                    pr = (s_[:, k0 + k, u * P:u * P + P], w_[:, k, 0:toks])
                                    opens = k == 0 and s_ is sh
                                else:
                                    o = held[u // 2][1][:, (u % 2) * S:(u % 2) * S + S]
                                    pr = (w_[:, k, u * P:u * P + P], s_[:, k0 + k, :])
                                    opens = k == 0 and s_ is sh and u % 2 == 0
                                todo.append((o, pr, first_ and q_ == 0 and half_ == 0 and opens,
                                             final and q_ == nparts - 1 and half_ == 1))
                    for n_, (o, pr, st_, sp_) in enumerate(todo):
                        f = (lambda e, o=o, pr=pr, st_=st_, sp_=sp_:
                             e.matmul(o, pr[0], pr[1], start=st_, stop=sp_, skip_group_check=True))
                        if n_ == len(todo) - 1:
                            ends.append(pe(f))
                        else:
                            pe.quiet(f)
                    if mid and half_ == 0:
                        mid()
                done(j, ends[0], ends[1])
                k0 += kn
                if on:
                    on()
            return held, ends[1]

        assert CN["ident"] == (0, 128)
        dma(sp, x[:, :, :], a["x"][0].rearrange("(t p) d -> p t d", p=P), s_x)
        dma(sp, cst[:, 0:128], a["consts"][:, 0:128], s_id)
        for i in range(NSLOT):
            if i == 1:
                dma(sp, par[:, :], a["params"], s_p)
            issue(i)
        dma(sp, cst[:, 128:NCN], a["consts"][:, 128:NCN], s_c)
        dma(ac, posi[:, :], a["pos"], s_pos)
        dma(ac, tab[:, :], a["t5_table_2"], s_tab)
        dma(ac, A1[0:32, 0:512], a["onehot"], s_tab)
        dma(ac, gains, a["gains"], s_gn)
        GAIN = (s_gn, 16)
        CST, PAR, XIN, IDN = (s_c, 16), (s_p, 16), (s_x, 16), (s_id, 16)
        t_ones = ve(lambda e: e.memset(onesb[:, :], 1.0))
        t_mh = ve(lambda e: e.memset(mhalf[:, :], -0.5))
        z1 = ve(lambda e: e.memset(glup[:, :, 0:30], 0.0))
        z2 = ve(lambda e: e.memset(ccp[:, :, 0:2], 0.0))

        def inv_rms(t_x):
            ts = []
            for tb, nh in ((0, 0), (1, 0), (0, 1), (1, 1)):
                cols = slice(512 * nh, 512 * nh + 512)
                q_ = 2 * tb + nh
                ts.append(act(xn[:, tb, cols], x[:, tb, cols], ACT.Square, t_x[q_], scale=1.0 / 32,
                              accum_out=st[:, q_:q_ + 1]))
            t = vst(st[:, 4:6], st[:, 0:4:2], 1e-6, st[:, 1:4:2], ALU.add, ALU.add, ts)
            return vtt(st[:, 6:8], st[:, 4:6], half(2), ALU.pow, t, t_mh, q=po)

        def normed_T(layer, gname, t_x):
            t = inv_rms(t_x)
            tn = {}
            for nh in range(2):
                cols = slice(512 * nh, 512 * nh + 512)
                tn[nh, 0] = vts(xn[:, 0, cols], x[:, 0, cols], st[:, 6:7], None, ALU.mult, None, t)
                tn[nh, 1] = act(xn[:, 1, cols], x[:, 1, cols], ACT.Copy, t, scale=st[:, 7:8])
            outs = Pairs()
            for c in range(0, 8, 2):
                b, bk, fr = bank("m")
                for j in range(2):
                    for tb in range(2):
                        tk = turnover(bk[:, j * S + tb * P:j * S + tb * P + P],
                                      xn[:, tb, (c + j) * P:(c + j + 1) * P], tn[c // 4, tb], fr, IDN)
                for j in range(2):
                    g = prm(gname, layer, c + j, c + j + 1)
                    th = act(hhi[:, c + j], bk[:, j * S:j * S + S], ACT.Copy, tk, PAR, scale=g)
                for j in range(2):
                    g = prm(gname, layer, c + j, c + j + 1)
                    tl = vst(hlo[:, c + j], bk[:, j * S:j * S + S], g, hhi[:, c + j],
                             ALU.mult, ALU.subtract, th, PAR)
                free[b] = tl
                outs.append(tl)
            return outs

        def rope(v, nh, half, cos, sin, tmp, t):
            x1, x2 = v[:, :, 0:half], v[:, :, half:2 * half]
            c, s_ = bc(cos, [P, nh, half]), bc(sin, [P, nh, half])
            ts = [vtt(tmp[:, 0], x1, c, ALU.mult, t), vtt(tmp[:, 1], x2, s_, ALU.mult, t),
                  vtt(tmp[:, 2], x2, c, ALU.mult, t), vtt(tmp[:, 3], x1, s_, ALU.mult, t)]
            vtt(x1, tmp[:, 0], tmp[:, 1], ALU.subtract, ts)
            return vtt(x2, tmp[:, 2], tmp[:, 3], ALU.add, ts)

        war_pt = [None, None]

        def attend(lg, qT, kT, V, t_in, t_v, scale, mask, t_mask, outp, so, rowtiles=False, pause=0):
            marks = []
            for tb in range(2):
                nk = P * (tb + 1)
                g = lg[tb].rearrange("p (h k) -> p h k", h=4)[:, :, 0:nk]
                tl = []
                for hp in range(2):
                    b, bk, fr = bank("s")
                    for j in range(2):
                        h = hp + 2 * j if rowtiles else 2 * hp + j
                        t = group(bk[:, j * nk:(j + 1) * nk], [(qT(h, tb), kT(h, 0, nk))], t_in, fr)
                    src = bk[:, 0:2 * nk].rearrange("p (h k) -> p h k", h=2)
                    hs = slice(hp, hp + 3, 2) if rowtiles else slice(2 * hp, 2 * hp + 2)
                    t = vst(g[:, hs], src, scale, mask(tb, hp), ALU.mult, ALU.add, t, t_mask)
                    free[b] = t
                    tl.append(t)
                s0 = so + 16 * tb
                t = ve(lambda e, g=g, s0=s0: e.tensor_reduce(st[:, s0:s0 + 4], g, AX.X, ALU.max, negate=True), tl)
                te = [act(g[:, h], g[:, h], ACT.Exp, t, bias=st[:, s0 + h:s0 + h + 1],
                          accum_out=st[:, s0 + 4 + h:s0 + 5 + h]) for h in range(4)]
                t = ve(lambda e, s0=s0: e.reciprocal(st[:, s0 + 8:s0 + 12], st[:, s0 + 4:s0 + 8]), te)
                t = vtt(g, g, bc(st[:, s0 + 8:s0 + 12], [P, 4, nk], 2), ALU.mult, t)
                marks.append(t)
                yield
            for _ in range(pause):
                yield
            tp = [[], []]
            for tb in range(2):
                g = lg[tb].rearrange("p (h k) -> p h k", h=4)
                for kb in range(tb + 1):
                    b, bk, fr = bank("s")
                    for h in range(4):
                        t = turnover(bk[:, h * P:h * P + P], g[:, h, kb * P:kb * P + P], marks[tb], fr)
                    dst = pt[tb][kb].rearrange("p h k -> p (h k)")
                    if kb == 0:
                        t = act(dst, bk[:, :], ACT.Copy, t, war_pt[tb])
                    else:
                        t = vcp(dst, bk[:, :], t, war_pt[tb])
                    free[b] = t
                    tp[tb].append(t)
            yield
            if pause:
                yield
            for tb in range(2):
                b, bk, fr = bank("s")
                t = outp(tb, bk, lambda h, kb: (V(h, kb), pt[tb][kb][:, h, :]), tb + 1,
                         [tp[tb], t_v, fr])
                war_pt[tb] = t[0]
                free[b] = t[1]
            yield

        beside = []

        def tick_ahead(ahead):
            if ahead:
                try:
                    next(ahead[0])
                except StopIteration:
                    ahead.pop(0)

        def tick(sides):
            ahead, rest = sides
            for g in list(beside):
                try:
                    next(g)
                except StopIteration:
                    beside.remove(g)
            again = 1 if ahead else 2
            tick_ahead(ahead)
            for _ in range(again):
                if rest:
                    g = rest.pop(0)
                    try:
                        next(g)
                        rest.append(g)
                    except StopIteration:
                        pass

        def drain(sides):
            while sides[0] or sides[1] or beside:
                tick(sides)

        def tables(res):
            t = vcp(posf[:, :], posi[:, :], (s_pos, 16))
            ang, kk, ki, r_ = rt[:, :, 0:24], rt[:, :, 24:48], rt[:, :, 48:72], rt[:, :, 72:96]
            tw = []
            for tb in range(2):
                tw.append(vts(ang[:, tb], con("invf"), posf[:, tb:tb + 1], None, ALU.mult, None, t, CST))
            MAGIC = 12582912.0
            TWO = [6.28125, 0.0019350051879882812, 3.019916050561733e-07, 2.0561020951390433e-14]
            assert abs(sum(TWO) - 2 * np.pi) < 1e-12
            for which in range(2):
                o = cs[:, :, 24 * which:24 * which + 24]
                t = vts(kk, ang, float(1 / (2 * np.pi)), 0.25 if which == 0 else 0.0, ALU.mult, ALU.add, tw, t)
                t = vts(kk, kk, MAGIC, -MAGIC, ALU.add, ALU.add, t)
                t = vts(ki, kk, 1 / 4096.0, MAGIC, ALU.mult, ALU.add, t)
                t = vts(ki, ki, -MAGIC, 4096.0, ALU.add, ALU.mult, t)
                t = vtt(kk, kk, ki, ALU.subtract, t)
                yield
                src = ang
                for c in TWO:
                    t = vst(r_, ki, -c, src, ALU.mult, ALU.add, t)
                    t = vst(r_, kk, -c, r_, ALU.mult, ALU.add, t)
                    src = r_
                if which == 0:
                    t = vts(r_, r_, float(np.pi / 2), None, ALU.add, None, t)
                t = vts(r_, r_, 3.1415925, -3.1415925, ALU.min, ALU.max, t)
                yield
                t = act(o, r_, ACT.Sin, t)
            res["cs"] = t
            yield

            b, bk, _ = bank("s")
            t = group(bk[0:4, 0:512], [(tab[:, :], A1[0:32, 0:512])], (s_tab, 32))
            t = vcp(part1(13320, 512)[0:4], bk[0:4, :], t)
            free[b] = t
            yield
            dma(ac, a["scratch"], part1(13320, 512)[0:4], s_sc, t)

        at_start = {}

        def block1(l, t_x):
            t_h = normed_T(l, "g_mix", t_x)
            res = {}
            sides = ([], [])
            hh = (hhi, hlo)
            qk = [A1.rearrange("p (h d) -> p h d", h=8), B1.rearrange("p (h d) -> p h d", h=8)]
            vA = vAf.rearrange("p (t n) -> p t n", t=2)
            xnf = xn[:, :, :].rearrange("p t n -> p (t n)")
            qkT = xnf.rearrange("p (h s) -> p h s", s=S)
            wk = mer1[:, 4:6, :]
            rl = mer1[:, 0:4, :]
            lgs = [A1, B1]
            F = [(fhi[:, r], flo[:, r]) for r in range(2)]

            def go():
                tick(sides)

            if l == 0:
                sides[0].append(tables(at_start))

            held, t = streamed(4, hh, t_h, chans=4, on=go)
            for p_, (b, bk, _) in enumerate(held):
                tsg = act(sgb[:, 2 * p_:2 * p_ + 2].rearrange("p c s -> p (c s)"), bk[:, :], ACT.Sigmoid, t,
                          res.get("sgb"))
                free[b] = tsg
            held, t = streamed(4, hh, t_h, chans=4, on=go)
            tg = []
            for p_, (b, bk, _) in enumerate(held):
                free[b] = vtt(glup[:, 2 * p_:2 * p_ + 2, 30:286], bk[:, :].rearrange("p (c s) -> p c s", c=2),
                              sgb[:, 2 * p_:2 * p_ + 2], ALU.mult, t, tsg)
                tg.append(free[b])
            res["sgb"] = free[b]

            def conv_branch():
                last = [None] * 4
                taps = [None, None]
                made = None

                def add_tap(j, t):
                    last[3] = vtt(cacc[:, 3], cacc[:, 3], tap[:, j % 2], ALU.add, t, last[3], q=po)
                    taps[j % 2] = last[3]

                for j in range(31):
                    for c in range(4):
                        wv = prm("cb_w", l, c * 31 + j, c * 31 + j + 1)
                        if c == 3:
                            if j == 0:
                                last[3] = act(cacc[:, 3], glup[:, 3, 0:S], ACT.Identity, tg, PAR, z1, scale=wv,
                                              bias=prm("cb_b", l, 3, 4))
                            else:
                                t = act(tap[:, j % 2], glup[:, 3, j:j + S], ACT.Copy, taps[j % 2], scale=wv)
                                if made:
                                    add_tap(*made)
                                made = (j, t)
                        elif j == 0:
                            last[c] = vts(cacc[:, c], glup[:, c, 0:S], wv, prm("cb_b", l, c, c + 1),
                                          ALU.mult, ALU.add, tg, PAR, z1)
                        else:
                            last[c] = vst(cacc[:, c], glup[:, c, j:j + S], wv, cacc[:, c], ALU.mult, ALU.add,
                                          last[c])
                    if j % 6 != 5:
                        yield
                add_tap(*made)
                yield
                t = vtt(lk0[:, 0:2], cacc[:, 0:2], cacc[:, 2:4], ALU.add, last)
                t = vtt(lk0[:, 0], lk0[:, 0], lk0[:, 1], ALU.add, t)
                yield
                yield
                b, bk, fr = bank("s")
                t = group(bk[:, 0:S], [(onesb[:, :], lk0[:, 0])], t, fr, t_ones)
                t = vst(cacc, bc(bk[:, 0:S], [P, 4, S]), -1.0 / 512, cacc, ALU.mult, ALU.add, t)
                free[b] = t
                sq = lk0
                t = act(sq, cacc, ACT.Square, t)
                t = vtt(sq[:, 0:2], sq[:, 0:2], sq[:, 2:4], ALU.add, t, q=po)
                t = vtt(sq[:, 0], sq[:, 0], sq[:, 1], ALU.add, t, q=po)
                yield
                yield
                b, bk, fr = bank("s")
                for tb in range(2):
                    t1 = group(bk[:, tb:tb + 1], [(sq[:, 0, tb * P:tb * P + P], onesb[:, 0:1])], t, fr)
                t = vts(st[:, 12:14], bk[:, 0:2], 1.0 / 512, 1e-6, ALU.mult, ALU.add, t1)
                free[b] = t
                t = vtt(st[:, 14:16], st[:, 12:14], half(2), ALU.pow, t, q=po)
                yield
                yield
                b, bk, fr = bank("s")
                for tb in range(2):
                    t1 = turnover(bk[:, tb * P:tb * P + P], st[:, 14 + tb:15 + tb].to_broadcast([P, P]), t, fr)
                t = vtt(cacc, cacc, bc(bk[:, 0:S], [P, 4, S]), ALU.mult, t1)
                free[b] = t
                yield
                ts = [act(sq[:, c], cacc[:, c], ACT.Sigmoid, t, scale=prm("ln_g", l, c, c + 1),
                          bias=prm("ln_b", l, c, c + 1)) for c in range(4)]
                tz = [vts(cacc[:, c], cacc[:, c], prm("ln_g", l, c, c + 1), prm("ln_b", l, c, c + 1),
                          ALU.mult, ALU.add, ts) for c in range(4)]
                t = vtt(cacc, cacc, sq, ALU.mult, tz)
                yield
                res["yb"] = split(F[0][0], F[0][1], cacc, t)
                yield

            sides[0].append(conv_branch())

            held, t = streamed(4, hh, t_h, toks=324, on=go)
            ti = []
            for tb, (b, bk, _) in enumerate(held):
                free[b] = act(ibuf[:, tb], bk[:, 0:324], ACT.Copy, t)
                ti.append(free[b])

            def indexer():
                tr_ = []
                for tb in range(2):
                    kx = ibuf[:, tb, 256:320]
                    s0 = 16 + 2 * tb
                    t = act(mk[:, tb, 0:64], kx, ACT.Square, ti[tb], accum_out=st[:, s0:s0 + 1])
                    t = vts(st[:, s0:s0 + 1], st[:, s0:s0 + 1], 1.0 / 64, 1e-6, ALU.mult, ALU.add, t)
                    t = vtt(st[:, s0 + 1:s0 + 2], st[:, s0:s0 + 1], half(1), ALU.pow, t, q=po)
                    t = vst(kx, kx, st[:, s0 + 1:s0 + 2], row("g_ki", l), ALU.mult, ALU.mult, t, GAIN)
                    v = ibuf[:, tb, 0:320].rearrange("p (h d) -> p h d", h=5)
                    tmp = mk[:, tb, 0:160].rearrange("p (a h d) -> p a h d", a=4, h=5)
                    tr_.append(rope(v, 5, 8, cs[:, tb, 16:24], cs[:, tb, 40:48], tmp, [t, at_start["cs"]]))
                for _ in range(4):
                    yield
                te = []
                for tb in range(2):
                    for hh, n in ((0, 4), (4, 1)):
                        b, bk, fr = bank("s")
                        for h in range(hh, hh + n):
                            t = turnover(bk[0:64, (h - hh) * P:(h - hh) * P + P],
                                         ibuf[:, tb, h * 64:h * 64 + 64], tr_[tb], fr)
                        t = act(iT[:, hh:hh + n, tb * P:tb * P + P],
                                bk[0:64, 0:n * P].rearrange("p (h k) -> p h k", h=n), ACT.Copy, t)
                        free[b] = t
                        te.append(t)
                yield
                for tb in range(2):
                    nk = P * (tb + 1)
                    tl = []
                    for hp in range(2):
                        b, bk, fr = bank("s")
                        for j in range(2):
                            h = 2 * hp + j
                            t = group(bk[:, j * nk:(j + 1) * nk],
                                      [(iT[:, h, tb * P:tb * P + P], iT[:, 4, 0:nk])], te, fr)
                        r = []
                        for j in range(2):
                            h = 2 * hp + j
                            r.append(vts(rl[:, h, 0:nk], bk[:, j * nk:(j + 1) * nk], 0.0,
                                         ibuf[:, tb, 320 + h:321 + h], ALU.max, ALU.mult, t))
                        free[b] = r
                        tl += r
                    t = vtt(rl[:, 0, 0:nk], rl[:, 0, 0:nk], rl[:, 1, 0:nk], ALU.add, tl)
                    t = vtt(rl[:, 0, 0:nk], rl[:, 0, 0:nk], rl[:, 2, 0:nk], ALU.add, t)
                    t = vtt(wk[:, tb, 0:nk], rl[:, 0, 0:nk], rl[:, 3, 0:nk], ALU.add, t)
                    t = vtt(wk[:, tb, nk - P:nk], wk[:, tb, nk - P:nk], con("causal"), ALU.add, t)
                    yield
                    for r in range(8):
                        if r:
                            yield
                        s0 = 32 + 8 * tb
                        src = wk[:, tb, 0:nk]
                        t = ve(lambda e, s0=s0, src=src: e.max(st[:, s0:s0 + 8], src), t)
                        t = ve(lambda e, s0=s0, src=src: e.match_replace(src, st[:, s0:s0 + 8], src, PICKED), t)
                    t = vts(mk[:, tb, 0:nk], wk[:, tb, 0:nk], -2e38, NEG, ALU.is_gt, ALU.mult, t)
                    t = vtt(mk[:, tb, nk - P:nk], mk[:, tb, nk - P:nk], con("causal"), ALU.add, t)
                    res["mask", tb] = t
                    yield

            sides[1].append(indexer())

            tq = [[], []]
            for part in range(2):
                held, t = streamed(4, hh, t_h, toks=512, on=go)
                for tb, (b, bk, _) in enumerate(held):
                    free[b] = act(qk[tb][:, 4 * part:4 * part + 4].rearrange("p h d -> p (h d)"), bk[:, :],
                                  ACT.Copy, t)
                    tq[tb].append(free[b])
            held, t = streamed(4, hh, t_h, toks=512, on=go)
            for tb, (b, bk, _) in enumerate(held):
                free[b] = t_vA = act(vA[:, tb], bk[:, :], ACT.Copy, t)

            def sparse():
                trs = []
                for tb in range(2):
                    v = qk[tb]
                    sq = xnf[:, 1024 * tb:1024 * tb + 1024].rearrange("p (h d) -> p h d", h=8)
                    t = act(sq, v, ACT.Square, tq[tb])
                    yield
                    s0 = 48 + 24 * tb
                    t = ve(lambda e, s0=s0, sq=sq: e.tensor_reduce(st[:, s0:s0 + 8], sq, AX.X, ALU.add), t)
                    t = vts(st[:, s0:s0 + 8], st[:, s0:s0 + 8], 1.0 / 128, 1e-6, ALU.mult, ALU.add, t)
                    yield
                    t = vtt(st[:, s0 + 8:s0 + 16], st[:, s0:s0 + 8], half(8), ALU.pow, t, q=po)
                    yield
                    t = vtt(v, v, bc(st[:, s0 + 8:s0 + 16], [P, 8, P], 2), ALU.mult, t)
                    yield
                    vtt(v[:, 0:4], v[:, 0:4], bc(row("g_q", l), [P, 4, P]), ALU.mult, t, GAIN)
                    t = vtt(v[:, 4:8], v[:, 4:8], bc(row("g_k", l), [P, 4, P]), ALU.mult, t, GAIN)
                    tmp = sq.rearrange("p h d -> p (h d)")[:, 0:512].rearrange("p (a h d) -> p a h d", a=4, h=8)
                    trs.append(rope(v, 8, 16, cs[:, tb, 0:16], cs[:, tb, 24:40], tmp, [t, at_start["cs"]]))
                    yield
                te = []
                yield
                for tb in range(2):
                    for hh in (0, 4):
                        b, bk, fr = bank("s")
                        for h in range(4):
                            t = turnover(bk[:, h * P:h * P + P], qk[tb][:, hh + h, :], trs[tb], fr)
                        t = act(qkT[:, hh:hh + 4, tb * P:tb * P + P],
                                bk[:, :].rearrange("p (h k) -> p h k", h=4), ACT.Copy, t, trs)
                        free[b] = t
                        te.append(t)
                    yield
                while ("mask", 1) not in res or "wo_c" not in res:
                    yield

                def outp(tb, bk, pr, nkb, aft):
                    for h in range(4):
                        t = group(bk[:, h * P:h * P + P], [pr(h, kb) for kb in range(nkb)], aft)
                    e_ = split(F[1][0][:, :, tb * P:tb * P + P], F[1][1][:, :, tb * P:tb * P + P],
                               bk[:, :].rearrange("p (h k) -> p h k", h=4), t, res["wo_c"])
                    res["ya", tb] = e_
                    return t, e_

                yield from attend(lgs, lambda h, tb: qkT[:, h, tb * P:tb * P + P],
                                  lambda h, k0, k1: qkT[:, 4 + h, k0:k1],
                                  lambda h, kb: vA[:, kb, h * P:h * P + P], te, t_vA, float(P) ** -0.5,
                                  lambda tb, hp: bc(mk[:, tb, 0:P * (tb + 1)], [P, 2, P * (tb + 1)]),
                                  [res["mask", 0], res["mask", 1]], outp, 96, pause=3)

            sides[1].append(sparse())
            tsq = []
            for dst, sc_ in ((sqT, float(P) ** -0.5), (skT, 1.0)):
                held, t = streamed(4, hh, t_h, chans=4, on=go)
                for p_, (b, bk, _) in enumerate(held):
                    free[b] = act(dst[:, 2 * p_:2 * p_ + 2].rearrange("p c s -> p (c s)"), bk[:, :], ACT.Copy, t,
                                  scale=sc_)
                    tsq.append(free[b])
            held, t = streamed(4, hh, t_h, toks=512, on=go)
            for tb, (b, bk, _) in enumerate(held):
                free[b] = act(sv[:, tb], bk[:, :], ACT.Copy, t)
                tsq.append(free[b])

            def stick():
                while "yb" not in res:
                    yield
                tls = []
                for g in range(3):
                    b, bk, fr = bank("s")
                    if g < 2:
                        for j in range(2):
                            h = 2 * g + j
                            t = group(bk[:, j * S:j * S + S], [(skT[:, h, 0:P], sqT[:, h, :])], tsq, fr)
                        dst, m = lk0[:, 2 * g:2 * g + 2].rearrange("p c s -> p (c s)"), bc(con("m0"), [P, 2, S])
                        shp = dict(c=2)
                    else:
                        for h in range(4):
                            t = group(bk[:, h * P:h * P + P], [(skT[:, h, P:S], sqT[:, h, P:S])], tsq, fr)
                        dst, m = lk1.rearrange("p c s -> p (c s)"), bc(con("m0", 0, P), [P, 4, P])
                        shp = dict(c=4)
                    t = act(dst, bk[:, :], ACT.Abs, t, res["yb"])
                    t = act(dst, dst, ACT.Exp, t, scale=-1.0)
                    t = act(dst, dst, ACT.Ln, t, bias=1.0)
                    t = vst(dst, bk[:, :], 0.0, dst, ALU.max, ALU.add, t)
                    free[b] = t
                    d3 = dst.rearrange("p (c s) -> p c s", **shp)
                    tls.append(vtt(d3, d3, m, ALU.mult, t))
                    yield
                for _ in range(2):
                    yield
                tas = []
                hold = []
                for g in range(2):
                    b, bk, fr = bank("s")
                    for j in range(2):
                        h = 2 * g + j
                        o = bk[:, j * S:j * S + S]
                        group(o, [(con("trirev"), lk0[:, h]), (skT[:, h, 0:P], sqT[:, h, :])], tls, fr, stop=False)
                        t = group(bk[:, j * S + P:j * S + S], [(onesb[:, :], lk1[:, h])], start=False)
                    hold.append((b, bk, t))
                b, bk, fr = bank("s")
                for h in range(4):
                    t = group(bk[:, h * P:h * P + P], [(con("trirev"), lk1[:, h]),
                                                       (skT[:, h, P:S], sqT[:, h, P:S])], fr)
                hold.append((b, bk, t))
                for g, (b, bk, t1) in enumerate(hold):
                    if g < 2:
                        dst, m, n = lk0[:, 2 * g:2 * g + 2], bc(con("n0"), [P, 2, S]), 2
                    else:
                        dst, m, n = lk1, bc(con("n0", 0, P), [P, 4, P]), 4
                    t = vst(dst, bk[:, :].rearrange("p (c s) -> p c s", c=n), 0.0, m, ALU.min, ALU.add, t)
                    free[b] = t
                    tas.append(act(dst, dst, ACT.Exp, t))
                for _ in range(3):
                    yield
                while "wo_b" not in res:
                    yield
                yd = []
                for g in range(2):
                    b, bk, fr = bank("s")
                    for j in range(2):
                        h = 2 * g + j
                        group(bk[:, j * S:j * S + S], [(sv[:, 0, h * P:h * P + P], lk0[:, h])], tas, fr, stop=False)
                        t = group(bk[:, j * S + P:j * S + S], [(sv[:, 1, h * P:h * P + P], lk1[:, h])], start=False)
                    yd += split(F[0][0][:, 2 * g:2 * g + 2], F[0][1][:, 2 * g:2 * g + 2],
                                bk[:, :].rearrange("p (c s) -> p c s", c=2), t, res["wo_b"])
                    free[b] = yd[-1]
                res["yd"] = yd
                yield

            sides[1].append(stick())

            held, t = streamed(4, hh, t_h, chans=4, on=go)
            for p_, (b, bk, _) in enumerate(held):
                free[b] = tgc = act(yc[:, 2 * p_:2 * p_ + 2].rearrange("p c s -> p (c s)"), bk[:, :], ACT.Copy, t)
            held, t = streamed(4, hh, t_h, chans=4, on=go)
            tc_ = []
            for p_, (b, bk, _) in enumerate(held):
                free[b] = vtt(ccp[:, 2 * p_:2 * p_ + 2, 2:258], bk[:, :].rearrange("p (c s) -> p c s", c=2),
                              yc[:, 2 * p_:2 * p_ + 2], ALU.mult, t, tgc)
                tc_.append(free[b])
            held, t = streamed(4, hh, t_h, chans=4, on=go)
            tb_ = []
            for p_, (b, bk, _) in enumerate(held):
                free[b] = act(gbS[:, 2 * p_:2 * p_ + 2].rearrange("p c s -> p (c s)"), bk[:, :], ACT.Copy, t,
                              (s_sc, 16))
                tb_.append(free[b])

            def short_branch():
                for j in range(3):
                    for c in range(4):
                        wv = prm("cc_w", l, c * 3 + j, c * 3 + j + 1)
                        if j == 0:
                            t = vts(yc[:, c], ccp[:, c, 0:S], wv, None, ALU.mult, None, tc_, PAR, z2)
                        else:
                            t = vst(yc[:, c], ccp[:, c, j:j + S], wv, yc[:, c], ALU.mult, ALU.add, t)
                    yield
                t = vtt(yc, yc, gbS, ALU.mult, t, tb_)
                res["yc"] = split(F[1][0], F[1][1], yc, t)
                yield

            sides[1].append(short_branch())

            mprev = [None] * 4
            for n_b, (bi, key, r) in enumerate(((1, "yb", 0), (2, "yc", 1), (3, "yd", 0), (0, "ya", 1))):
                for hf in range(2):
                    held, t = streamed(4, hh, t_h, chans=4, on=go)
                    tsg = []
                    for p_, (b, bk, _) in enumerate(held):
                        for j in range(2):
                            c = 8 * bi + 4 * hf + 2 * p_ + j
                            free[b] = act(sgb[:, 2 * p_ + j], bk[:, j * S:j * S + S], ACT.Sigmoid, t, PAR,
                                          res["sgb"], bias=prm("b_gate", l, c, c + 1))
                            tsg.append(free[b])
                    t_gate = t
                    if n_b == 3 and hf == 1:
                        for q_ in range(2):
                            mprev[q_] = split(hhi[:, 2 * q_:2 * q_ + 2], hlo[:, 2 * q_:2 * q_ + 2],
                                              mer1[:, 2 * q_:2 * q_ + 2], mprev[q_], t_gate)
                    keys = [("ya", 0), ("ya", 1)] if key == "ya" else [key]
                    while any(k_ not in res for k_ in keys):
                        tick(sides)
                    held, t = streamed(2, F[r], [res[k_] for k_ in keys], chans=4, on=go)
                    for p_, (b, bk, _) in enumerate(held):
                        q_ = 2 * hf + p_
                        m2 = mer1[:, 2 * q_:2 * q_ + 2]
                        g2 = sgb[:, 2 * p_:2 * p_ + 2]
                        b3 = bk[:, :].rearrange("p (c s) -> p c s", c=2)
                        if n_b == 0:
                            while ("mask", 1) not in res:
                                tick(sides)
                            mprev[q_] = free[b] = res["sgb"] = vtt(m2, b3, g2, ALU.mult, t, tsg, res["mask", 1])
                        else:
                            free[b] = vtt(g2, b3, g2, ALU.mult, t, tsg)
                            mprev[q_] = res["sgb"] = vtt(m2, m2, g2, ALU.add, free[b], mprev[q_],
                                                         q=ve if n_b == 3 else po)
                        if n_b == 3 and hf == 1:
                            mprev[q_] = split(hhi[:, 2 * q_:2 * q_ + 2], hlo[:, 2 * q_:2 * q_ + 2], m2,
                                              mprev[q_], t_gate)
                res["wo_" + "abcd"[bi]] = t
            drain(sides)
            t_x = row_out((hhi, hlo), mprev, t_x)

            t_h = normed_T(l, "g_ffn", t_x)
            z3 = ve(lambda e: e.memset(gpad[:, :, :, 0:2], 0.0), t_x)
            acc = [bank("s") for _ in range(4)]
            fre = [None, None]
            pend = None
            t_xo = [None] * 4
            y = A1.rearrange("p (c s) -> p c s", c=4)
            sg = B1.rearrange("p (c s) -> p c s", c=4)
            lastg = [z3, z3]

            def down(i6, kn, tf):
                t_nh = [None, None]
                for k in range(0, kn, 2):
                    for nh in range(2):
                        _, t_nh[nh] = streamed(1, F[i6 % 2], tf, toks=512, held=[acc[nh], acc[2 + nh]], k0=k,
                                         first_=i6 == 0 and k == 0, final=i6 == 5 and k == kn - 2)
                        if i6 == 5 and k == kn - 2:
                            add_half(acc, nh, t_nh[nh], t_xo)
                fre[i6 % 2] = t_nh[1]
                return t_nh

            for i6 in range(6):
                n = 4 if i6 < 5 else 2
                held, t = streamed(4, hh, t_h, chans=n)
                ty = [None] * 4
                for p_, (b, bk, _) in enumerate(held):
                    free[b] = t1 = act(gpad[:, p_, :, 2:258],
                                       bk[:, :].rearrange("p (c s) -> p c s", c=2), ACT.Copy, t, lastg[p_])
                    for k3 in range(3):
                        for j in range(2):
                            c = 4 * i6 + 2 * p_ + j
                            wv = prm("ffn_w", l, c * 3 + k3, c * 3 + k3 + 1)
                            yy = y[:, 2 * p_ + j]
                            if k3 == 0:
                                ty[2 * p_ + j] = vts(yy, gpad[:, p_, j, 0:S], wv, None, ALU.mult, None, t1, PAR)
                            else:
                                ty[2 * p_ + j] = vst(yy, gpad[:, p_, j, k3:k3 + S], wv, yy, ALU.mult, ALU.add,
                                                     ty[2 * p_ + j])
                    lastg[p_] = ty[2 * p_ + 1]
                held, t = streamed(4, hh, t_h, chans=n)
                t1 = act(sg[:, 0:n], y[:, 0:n], ACT.Sigmoid, ty[0:n])
                t1 = vtt(y[:, 0:n], y[:, 0:n], sg[:, 0:n], ALU.mult, t1)
                tf = Pairs()
                for p_, (b, bk, _) in enumerate(held):
                    y2 = y[:, 2 * p_:2 * p_ + 2]
                    free[b] = vtt(y2, y2, bk[:, :].rearrange("p (c s) -> p c s", c=2), ALU.mult, t1, t)
                    fh, fl = F[i6 % 2]
                    tf.append(split(fh[:, 2 * p_:2 * p_ + 2], fl[:, 2 * p_:2 * p_ + 2], y2, free[b], fre[i6 % 2]))
                if pend:
                    calm[0] = i6 == 5
                    down(*pend)
                pend = (i6, n, tf)
            down(*pend)
            calm[0] = False
            return t_xo

        def add_half(acc, nh, t, t_xo):
            for tb in range(2):
                b, bk = acc[2 * tb + nh][0:2]
                xs = x[:, tb, nh * 512:nh * 512 + 512]
                free[b] = t_xo[2 * tb + nh] = vtt(xs, bk[:, :], xs, ALU.add, t)

        def row_out(src, t_src, t_x, order=(0, 1, 2, 3), before=None, on=None, mid=None):
            acc = [bank("m") for _ in range(4)]
            t_xo = [None] * 4
            for n, c in enumerate(order):
                if before:
                    before(c)
                calm[0] = n > 1
                for nh in range(2):
                    _, t = streamed(1, src, t_src[c], toks=512, held=[acc[nh], acc[2 + nh]], k0=2 * c,
                                    first_=n == 0, final=n == 3, on=on, mid=mid)
                    if n == 3:
                        add_half(acc, nh, t, t_xo)
            calm[0] = False
            return t_xo

        def bias_tiles():
            yield
            for h in range(4):
                b, bk, fr = bank("s")
                t = group(bk[:, 0:S], [(bufB[:, 0:128], bufA[:, h * S:(h + 1) * S])], (s_bi, 64), (s_fl, 16), fr)
                t = vcp(bia[:, h, :], bk[:, 0:S], t)
                free[b] = t
                t_bias[0] = vtt(bia[:, h, 128:256], bia[:, h, 128:256], con("causal"), ALU.add, t)
                yield

        t_bias = [None]

        def block2(l, t_x):
            t_h = normed_T(l, "norm2", t_x)
            z4 = ve(lambda e: e.memset(gdp[:, :, :, 0:3], 0.0), t_x)
            dma(ac, wuq[:, :, :], a["mla_w_uq_2"][l].rearrange("(k p) n -> p k n", p=P), s_u, t_x)
            dma(ac, wukv[:, :], a["mla_w_ukv_2"][l], s_u)
            t_wu = (s_u, 32 * (l + 1))
            res = {}
            sides = ([], [])
            if l == 0:
                for h in range(4):
                    dma(ac, bufA[:, h * S:(h + 1) * S], a["toep"][h], s_bi, (s_sc, 16), t_x)
                dma(ac, bufB[:, 0:128], a["flip"], s_fl)
                sides[1].append(bias_tiles())
            yT = mer
            m0 = xn[:, :, 0:416]
            mtmp = xn[:, :, 416:1024]
            hh = (hhi, hlo)

            def go():
                tick(sides)

            def step():
                tick_ahead(sides[0])

            qm = [bufA[:, 0:384].rearrange("p (h d) -> p h d", h=4), bufB[:, 0:384].rearrange("p (h d) -> p h d", h=4)]
            km = [bufA[:, 384:768].rearrange("p (h d) -> p h d", h=4), bufB[:, 384:768].rearrange("p (h d) -> p h d", h=4)]
            vm = [bufA[:, 768:1024], bufB[:, 768:1024]]
            lgs = [bufC[:, :], bufD[:, :]]
            cqT = bufE[:, 0:512].rearrange("p (k s) -> p k s", k=2)
            ckT = bufE[:, 512:768]
            qmT = bufF[:, :].rearrange("p (h s) -> p h s", s=S)
            kmT = bufG[:, :].rearrange("p (h s) -> p h s", s=S)

            t_pad = []

            def latent():
                tn = []
                for tb in range(2):
                    s0 = 16 + 8 * tb
                    t1 = act(mtmp[:, tb, 0:256], m0[:, tb, 0:256], ACT.Square, tm[tb], accum_out=st[:, s0:s0 + 1])
                    t2 = act(bufC[:, 512 + 128 * tb:640 + 128 * tb], m0[:, tb, 256:384], ACT.Square, accum_out=st[:, s0 + 1:s0 + 2])
                    t1 = vts(st[:, s0:s0 + 1], st[:, s0:s0 + 1], 1.0 / 256, 1e-6, ALU.mult, ALU.add, t1)
                    t2 = vts(st[:, s0 + 1:s0 + 2], st[:, s0 + 1:s0 + 2], 1.0 / 128, 1e-6, ALU.mult, ALU.add, t2)
                    t = vtt(st[:, s0 + 2:s0 + 4], st[:, s0:s0 + 2], half(2), ALU.pow, [t1, t2], q=po)
                    vts(m0[:, tb, 0:256], m0[:, tb, 0:256], st[:, s0 + 2:s0 + 3], None, ALU.mult, None, t)
                    t = vts(m0[:, tb, 256:384], m0[:, tb, 256:384], st[:, s0 + 3:s0 + 4], None, ALU.mult, None, t)
                    tn.append(t)
                yield
                b, bk, fr = bank("s")
                for c in range(2):
                    for tb in range(2):
                        t = turnover(bk[:, c * S + tb * P:c * S + tb * P + P], m0[:, tb, c * P:c * P + P], tn[tb], fr)
                tc = [act(cqT[:, c], bk[:, c * S:c * S + S], ACT.Copy, t, scale=prm("qn2", l, c, c + 1))
                      for c in range(2)]
                free[b] = tc
                b, bk, fr = bank("s")
                for tb in range(2):
                    t = turnover(bk[:, tb * P:tb * P + P], m0[:, tb, 256:384], tn[tb], fr)
                tc.append(act(ckT, bk[:, 0:S], ACT.Copy, t, scale=prm("kvn2", l)))
                free[b] = tc[-1]
                yield
                tr_ = []
                for tb in range(2):
                    b, bk, fr = bank("s")
                    t = group(bk[:, 0:384], [(cqT[:, k, tb * P:tb * P + P], wuq[:, k]) for k in range(2)],
                              tc, t_wu, fr)
                    res["wu"] = t
                    t = vts(qm[tb].rearrange("p h d -> p (h d)"), bk[:, 0:384], float(96) ** -0.5, None,
                            ALU.mult, None, t)
                    free[b] = t
                    b, bk, fr = bank("s")
                    t2 = group(bk[:, :], [(ckT[:, tb * P:tb * P + P], wukv[:, :])], tc, fr)
                    res["wu"] = t2
                    kv = bk[:, :].rearrange("p (h d) -> p h d", h=4)
                    t3 = act(km[tb][:, :, 0:64], kv[:, :, 0:64], ACT.Copy, t2)
                    t4 = act(vm[tb].rearrange("p (h d) -> p h d", h=4), kv[:, :, 64:128], ACT.Copy, t2)
                    free[b] = t4
                    cos, sin = con("rope2", 32 * tb, 32 * tb + 16), con("rope2", 32 * tb + 16, 32 * tb + 32)
                    tmp = mtmp[:, tb, 0:256].rearrange("p (a h d) -> p a h d", a=4, h=4)
                    t = rope(qm[tb][:, :, 64:96], 4, 16, cos, sin, tmp, [t])
                    tmp = mtmp[:, tb, 256:320].rearrange("p (a h d) -> p a h d", a=4, h=1)
                    t5 = rope(m0[:, tb, 384:416].unsqueeze(1), 1, 16, cos, sin, tmp, [tm[tb]])
                    t5 = vcp(km[tb][:, :, 64:96], bc(m0[:, tb, 384:416], [P, 4, 32]), t5)
                    tr_.append([t, t3, t5])
                    res["vm"] = t4
                    yield
                te = []
                while not t_pad:
                    yield
                for tb in range(2):
                    for src, dst in ((qm[tb], qmT), (km[tb], kmT)):
                        b, bk, fr = bank("s")
                        for h in range(4):
                            t = turnover(bk[0:96, h * P:h * P + P], src[:, h, :], tr_[tb], fr)
                        t = act(dst[0:96, :, tb * P:tb * P + P],
                                bk[0:96, :].rearrange("p (h k) -> p h k", h=4), ACT.Copy, t, list(t_pad))
                        free[b] = t
                        te.append(t)
                yield

                def mask(tb, hp):
                    return bc(mk0 if tb == 0 else mk1, [P, 2, P * (tb + 1)])

                mk0 = con("causal")
                zo = CN["zero"][0]
                mk1 = cst[:, zo:zo + S]
                yield from attend(lgs, lambda h, tb: qmT[0:96, h, tb * P:tb * P + P],
                                  lambda h, k0, k1: kmT[0:96, h, k0:k1],
                                  lambda h, kb: vm[kb][:, h * 64:h * 64 + 64], te, res["vm"], 1.0,
                                  mask, CST, pair_out("mla", 0, "mg"), 96)
                while "moba_in" not in res:
                    yield

                def mqT(h, tb):
                    return cq[64 * (h % 2):64 * (h % 2) + 64, h // 2, tb * P:tb * P + P]

                def mkT(h, k0, k1):
                    return ck[64 * (h % 2):64 * (h % 2) + 64, h // 2, k0:k1]

                def mask2(tb, hp):
                    return bia[:, hp:hp + 3:2, 128:256] if tb == 0 else bia[:, hp:hp + 3:2, :]

                yield from attend(lgs, mqT, mkT, lambda h, kb: cv[:, kb, h * 64:h * 64 + 64],
                                  res["moba_in"], res["cv"], 1.0, mask2, t_bias[0], pair_out("moba", 6, "cg"), 96,
                                  rowtiles=True)

            mgs = big[:, 0:2 * S].rearrange("p (c s) -> p c s", s=S)
            cgs = big[:, 2 * S:4 * S].rearrange("p (c s) -> p c s", s=S)
            gate_of = {"mg": mgs, "cg": cgs}

            def pair_out(name, c0, gname):
                def outp(tb, bk, pr, nkb, aft):
                    for h in range(4):
                        o = bk[64 * (h % 2):64 * (h % 2) + 64, (h // 2) * P:(h // 2) * P + P]
                        t = group(o, [pr(h, kb) for kb in range(nkb)], aft)
                    e_ = act(yT[:, c0:c0 + 2, tb * P:tb * P + P],
                             bk[:, 0:2 * P].rearrange("p (h k) -> p h k", h=2), ACT.Copy, t)
                    res[name, tb] = e_
                    return t, e_
                return outp

            zs = big[:, 4 * S:8 * S].rearrange("p (h s) -> p h s", s=S)
            qc = big[:, 8 * S:12 * S].rearrange("p (h s) -> p h s", s=S)
            kc = big[:, 12 * S:16 * S].rearrange("p (h s) -> p h s", s=S)
            vc = big[:, 16 * S:20 * S].rearrange("p (h s) -> p h s", s=S)
            bg = st[:, 128:144].rearrange("p (t n) -> p t n", t=2)
            nst = [160]

            def cell(n):
                o = nst[0]
                nst[0] += n
                return st[:, o:o + n]

            beta = cell(8).rearrange("p (t h) -> p t h", t=2)
            gv = cell(8).rearrange("p (t h) -> p t h", t=2)
            gc = cell(8).rearrange("p (t h) -> p t h", t=2)
            ngc = cell(8).rearrange("p (t h) -> p t h", t=2)
            egc = cell(8).rearrange("p (t h) -> p t h", t=2)
            edl = cell(8).rearrange("p (t h) -> p t h", t=2)
            gend = cell(16).rearrange("p (t c h) -> p t c h", t=2, c=2)
            ss = cell(16).rearrange("p (q t h) -> p q t h", q=2, t=2)
            rs = cell(16).rearrange("p (q t h) -> p q t h", q=2, t=2)
            r1 = cell(8).rearrange("p (t h) -> p t h", t=2)
            r3 = cell(8).rearrange("p (t h) -> p t h", t=2)
            cw = cell(8).rearrange("p (t h) -> p t h", t=2)
            ckk = cell(8).rearrange("p (t h) -> p t h", t=2)
            ea = cell(4)
            t4a = cell(8).rearrange("p (t h) -> p t h", t=2)
            t4b = cell(8).rearrange("p (t h) -> p t h", t=2)
            assert nst[0] <= 512

            def decay_prep(t_rows):
                b, bk, fr = bank("s")
                for tb in range(2):
                    t = turnover(bk[:, 8 * tb:8 * tb + 8], rows8[:, tb * P:tb * P + P], t_rows, fr)
                free[b] = tbg = vcp(bg, bk[:, 0:16].rearrange("p (t n) -> p t n", t=2), t)
                t = act(beta, bg[:, :, 0:4], ACT.Sigmoid, tbg)
                ta = vtt(t4a, bg[:, :, 4:8], bc(prm("dtb", l), [P, 2, 4]), ALU.add, tbg)
                t1 = act(t4b, t4a, ACT.Abs, ta)
                t1 = act(t4b, t4b, ACT.Exp, t1, scale=-1.0)
                t1 = act(t4b, t4b, ACT.Ln, t1, bias=1.0)
                t2 = act(ea, prm("alog", l), ACT.Exp)
                t1 = vst(t4a, t4a, 0.0, t4b, ALU.max, ALU.add, t1, t2)
                t1 = vst(gv, t4a, -1.0, bc(ea, [P, 2, 4]), ALU.mult, ALU.mult, t1, t)
                for _ in range(5):
                    yield
                b, bk, fr = bank("s")
                for tb in range(2):
                    t = group(bk[:, 16 * tb:16 * tb + 4], [(con("tri"), gv[:, tb])], t1, fr)
                    t = group(bk[:, 16 * tb + 4:16 * tb + 8], [(con("blk"), gv[:, tb])])
                    t = group(bk[:, 16 * tb + 8:16 * tb + 12], [(con("half0"), gv[:, tb])])
                    t = group(bk[:, 16 * tb + 12:16 * tb + 16], [(con("half1"), gv[:, tb])])
                v = bk[:, 0:32].rearrange("p (t n) -> p t n", t=2)
                t2 = vcp(gc, v[:, :, 0:4], t)
                t3 = vts(ngc, v[:, :, 0:4], -1.0, None, ALU.mult, None, t)
                t4 = vtt(edl, v[:, :, 4:8], gc, ALU.subtract, t2)
                t5 = act(gend.rearrange("p t c h -> p t (c h)"), v[:, :, 8:16], ACT.Exp, t3, t4)
                t6 = act(egc, gc, ACT.Exp, t2)
                t7 = act(edl, edl, ACT.Exp, t4)
                free[b] = [t4, t5]
                res["dec"] = [t3, t7]
                yield


            lastg = [None, None]

            def conv4(dst, ci, tag):
                held, t = streamed(4, hh, t_h, chans=4, on=go, mid=step)
                te = []
                for p_, (b, bk, _) in enumerate(held):
                    free[b] = t1 = act(gdp[:, p_, :, 3:259], bk[:, :].rearrange("p (c s) -> p c s", c=2), ACT.Copy,
                                       t, lastg[p_], z4)
                    te.append(t1)
                war = res.get("silu")

                def taps():
                    tj = [None] * 4
                    for p_ in range(2):
                        for k4 in range(4):
                            for j in range(2):
                                c = 2 * p_ + j
                                wv = prm("gdn_w", l, (ci + c) * 4 + k4, (ci + c) * 4 + k4 + 1)
                                if k4 == 0:
                                    tj[c] = vts(dst[:, c], gdp[:, p_, j, 0:S], wv, None, ALU.mult, None, te[p_])
                                else:
                                    tj[c] = vst(dst[:, c], gdp[:, p_, j, k4:k4 + S], wv, dst[:, c],
                                                ALU.mult, ALU.add, tj[c])
                        lastg[p_] = tj[2 * p_:2 * p_ + 2]
                        if p_ == 0:
                            yield
                    tm_ = []
                    for p_ in range(2):
                        d2 = dst[:, 2 * p_:2 * p_ + 2].rearrange("p c s -> p (c s)")
                        tmp = sgb[:, 2 * p_:2 * p_ + 2].rearrange("p c s -> p (c s)")
                        t1 = act(tmp, d2, ACT.Sigmoid, tj[2 * p_:2 * p_ + 2], war)
                        tm_.append((d2, tmp, t1))
                    yield
                    for d2, tmp, t1 in tm_:
                        res["silu"] = t1 = vtt(d2, d2, tmp, ALU.mult, t1)
                    res[tag] = t1
                    yield

                g = taps()
                next(g)
                beside.append(g)

            ktk = big[:, 20 * S:24 * S].rearrange("p (t n) -> p t n", t=2)
            ke = big[:, 24 * S:28 * S].rearrange("p (t n) -> p t n", t=2)
            vb = big[:, 28 * S:32 * S].rearrange("p (t n) -> p t n", t=2)
            Dm = bufH[:, :].rearrange("p (t n) -> p t n", t=2)
            LT = bufI[:, :].rearrange("p (t n) -> p t n", t=2)
            AT = bufJ[:, :].rearrange("p (t n) -> p t n", t=2)
            qg = vc
            TT, Mm = halves(part2(23040, 1024)), halves(bufH)
            T_ = halves(big[:, 4 * S:8 * S])
            BT = halves(yT[:, 2:6].rearrange("p c s -> p (c s)"))
            WT = kc
            U = qc
            Ut = U.rearrange("p h s -> p (h s)").rearrange("p (t n) -> p t n", t=2)
            Sst = [gs[:, h // 2, h % 2] for h in range(4)]

            def delta():
                def turned(src, q_, tag, junk, after=None):
                    out_, tn_ = [], []
                    for tb in range(2):
                        b, bk, fr = bank("s")
                        for h in range(4):
                            t = turnover(bk[:, h * P:h * P + P], src[:, h, tb * P:tb * P + P], fr, res[tag])
                        tn_ += [act(junk[:, (4 * tb + h) * P:(4 * tb + h + 1) * P], bk[:, h * P:h * P + P],
                                    ACT.Square, t, after, accum_out=ss[:, q_, tb, h:h + 1]) for h in range(4)]
                        free[b] = tn_[-4:]
                        out_.append((b, bk))
                    t = vts(ss[:, q_], ss[:, q_], 1e-6, None, ALU.add, None, tn_)
                    return out_, vtt(rs[:, q_].rearrange("p t h -> p (t h)"), ss[:, q_].rearrange("p t h -> p (t h)"),
                                     half(8), ALU.pow, t, q=po)

                while "kc" not in res:
                    yield
                for _ in range(2):
                    yield
                kb_, tk_ = turned(kc, 0, "kc", bufH)
                for _ in range(4):
                    yield
                t1 = vtt(r1, rs[:, 0], beta, ALU.mult, tk_, res["dec"])
                t4 = vst(cw, r1, -1.0, egc, ALU.mult, ALU.mult, t1)
                t5 = vtt(ckk, rs[:, 0], edl, ALU.mult, tk_)
                for tb, (b, bk) in enumerate(kb_):
                    v3 = bk[:, :].rearrange("p (h d) -> p h d", h=4)
                    vtt(ktk[:, tb].rearrange("p (h d) -> p h d", h=4), v3, bc(cw[:, tb], [P, 4, P], 2),
                        ALU.mult, t4)
                    free[b] = vtt(ke[:, tb].rearrange("p (h d) -> p h d", h=4), v3, bc(ckk[:, tb], [P, 4, P], 2),
                                  ALU.mult, t5)
                yield
                def q4(v):
                    return v.rearrange("p (h d) -> p h d", h=4)

                def scores(tb, src, dst, dec, *after):
                    b, bk, fr = bank("s")
                    for h in range(4):
                        t = group(bk[:, h * P:h * P + P],
                                  [(kc[:, h, tb * P:tb * P + P], src[:, h, tb * P:tb * P + P])], fr, *after)
                    for h in range(4):
                        sl = slice(h * P, h * P + P)
                        tt = vst(dst[:, tb, sl], bk[:, sl], rs[:, 0, tb, h:h + 1], dec[:, tb, sl],
                                 ALU.mult, ALU.mult, t, *after)
                    free[b] = tt
                    return tt

                tDm, t_r1 = [], []
                for tb in range(2):
                    b, bk, fr = bank("s")
                    for h in range(4):
                        t = turnover(bk[:, h * P:h * P + P], gc[:, tb, h:h + 1].to_broadcast([P, P]), fr, tk_)
                    for h in range(4):
                        tt = vts(Dm[:, tb, h * P:h * P + P], bk[:, h * P:h * P + P], ngc[:, tb, h:h + 1], 0.0,
                                 ALU.add, ALU.min, t)
                    free[b] = tt
                    tDm.append(act(Dm[:, tb], Dm[:, tb], ACT.Exp, tt))
                    b, bk, fr = bank("s")
                    for h in range(4):
                        t = turnover(bk[:, h * P:h * P + P], r1[:, tb, h:h + 1].to_broadcast([P, P]), fr, t1)
                    t_r1.append((b, bk, t))
                yield
                yield
                for tb, (b, bk, t) in enumerate(t_r1):
                    td = vtt(q4(Dm[:, tb]), q4(Dm[:, tb]), bc(con("tri"), [P, 4, P]), ALU.mult, tDm[tb])
                    free[b] = tDm[tb] = vtt(LT[:, tb], Dm[:, tb], bk[:, :], ALU.mult, t, td)
                yield
                yield
                for tb in range(2):
                    tt = scores(tb, kc, LT, LT, tDm[tb])
                    l3 = q4(LT[:, tb])
                    res["L", tb] = vtt(l3, l3, bc(con("strict"), [P, 4, P]), ALU.mult, tt)
                yield
                yield

                def others():
                    while "qc" not in res:
                        yield
                    yield
                    yield
                    _, tq = turned(qc, 1, "qc", bufJ)
                    yield
                    tq = vts(rs[:, 1], rs[:, 1], float(P) ** -0.5, None, ALU.mult, None, tq)
                    res["rqq"] = tq = vtt(r3, rs[:, 1], rs[:, 1], ALU.mult, tq)
                    for tb in range(2):
                        res["A", tb] = scores(tb, qc, AT, Dm, tq)
                    yield
                    while "vc" not in res:
                        yield
                    yield
                    yield
                    tt3 = []
                    for tb in range(2):
                        b, bk, fr = bank("s")
                        for h in range(4):
                            t = turnover(bk[:, h * P:h * P + P], vc[:, h, tb * P:tb * P + P], fr, res["vc"])
                        free[b] = vtt(q4(vb[:, tb]), q4(bk[:, :]), bc(beta[:, tb], [P, 4, P], 2), ALU.mult, t)
                        tt3.append(free[b])
                        yield
                    for tb in range(2):
                        b, bk, fr = bank("s")
                        for h in range(4):
                            t = turnover(bk[:, h * P:h * P + P], egc[:, tb, h:h + 1].to_broadcast([P, P]), fr)
                        free[b] = vtt(qg[:, :, tb * P:tb * P + P], qc[:, :, tb * P:tb * P + P], q4(bk[:, :]),
                                      ALU.mult, t, tt3)
                        if tb:
                            res["qg"] = free[b]
                        yield

                beside.append(others())
                cur = {}
                for lv in range(6):
                    tB = [vtt(BT[tb].rearrange("p (h d) -> p h d", h=4),
                              LT[:, tb].rearrange("p (h d) -> p h d", h=4),
                              bc(con("lv", lv * P, lv * P + P), [P, 4, P]), ALU.mult,
                              res["L", tb], cur.get(("m", tb)), q=po if lv else ve) for tb in range(2)]
                    if lv == 0:
                        id4 = bc(ident, [P, 4, P])
                        for tb in range(2):
                            b, bk, fr = bank("s")
                            for h in range(4):
                                t = turnover(bk[:, h * P:h * P + P], BT[tb][:, h * P:h * P + P], tB[tb], fr)
                            cur["m", tb] = t
                            cur["T", tb] = vtt(T_[tb].rearrange("p (h d) -> p h d", h=4), id4,
                                               bk[:, :].rearrange("p (h d) -> p h d", h=4), ALU.subtract, t)
                            free[b] = cur["T", tb]
                            cur["TT", tb] = vtt(TT[tb].rearrange("p (h d) -> p h d", h=4), id4,
                                                BT[tb].rearrange("p (h d) -> p h d", h=4), ALU.subtract, tB[tb])
                            cur["m", tb] = [t, cur["TT", tb]]
                        yield
                        continue
                    while ("A", 1) not in res:
                        yield
                    tM = []
                    for tb in range(2):
                        b, bk, fr = bank("s")
                        for h in range(4):
                            sl = slice(h * P, h * P + P)
                            t = group(bk[:, sl], [(BT[tb][:, sl], T_[tb][:, sl])], tB[tb], cur["T", tb], fr)
                        cur["m", tb] = t
                        t = act(Mm[tb], bk[:, :], ACT.Copy, t, cur.get(("u", tb)), res["A", 1])
                        free[b] = t
                        tM.append(t)
                    yield
                    for tb in range(2):
                        b, bk, fr = bank("s")
                        for h in range(4):
                            sl = slice(h * P, h * P + P)
                            t = group(bk[:, sl], [(Mm[tb][:, sl], TT[tb][:, sl])], tM[tb], cur["TT", tb], fr)
                        if lv < 5:
                            b2, bk2, fr2 = bank("s")
                            for h in range(4):
                                sl = slice(h * P, h * P + P)
                                t_2 = group(bk2[:, sl], [(TT[tb][:, sl], Mm[tb][:, sl])], fr2)
                            cur["u", tb] = t_2
                            cur["T", tb] = vtt(T_[tb], T_[tb], bk2[:, :], ALU.subtract, t_2)
                            free[b2] = cur["T", tb]
                        else:
                            t_2 = t
                        cur["TT", tb] = vtt(TT[tb], TT[tb], bk[:, :], ALU.subtract, t_2)
                        free[b] = cur["TT", tb]
                    if lv == 5:
                        res["T_free"] = [cur["m", 0], cur["m", 1]]
                    yield
                tW = []
                for tb in range(2):
                    b, bk, fr = bank("s")
                    for h in range(4):
                        sl = slice(h * P, h * P + P)
                        t = group(bk[:, sl], [(ktk[:, tb, sl], TT[tb][:, sl])], cur["TT", tb], fr)
                    t = act(WT[:, :, tb * P:tb * P + P], bk[:, :].rearrange("p (h d) -> p h d", h=4), ACT.Copy, t,
                            res["A", 1])
                    free[b] = t
                    tW.append(t)
                yield
                while "qg" not in res:
                    yield
                tqg = res["qg"]
                tS = None
                for c in range(4):
                    tb, hf = c // 2, c % 2
                    rows = slice(64 * hf, 64 * hf + 64)
                    cols = slice(tb * P + 64 * hf, tb * P + 64 * hf + 64)
                    b, bk, fr = bank("s")
                    for h in range(4):
                        sl = slice(h * P, h * P + P)
                        pairs = [(TT[tb][:, sl], vb[:, tb, sl])]
                        if c:
                            pairs.append((WT[:, h, tb * P:tb * P + P], Sst[h]))
                        t = group(bk[:, sl], pairs, tW, tS, fr)
                    tU = vcp(Ut[rows, tb], bk[rows, :], t, res["A", 1], tqg)
                    free[b] = tU

                    def one(o, pr, *after, start=False, stop=False):
                        return pe(lambda e: e.matmul(o, pr[0], pr[1], start=start, stop=stop,
                                                     skip_group_check=True), *after)

                    bo, bko, fro = bank("s")
                    if c:
                        for h in range(4):
                            one(bko[:, h * 64:h * 64 + 64], (Sst[h], qg[:, h, cols]), tqg, fro, start=h == 0)
                    if c < 3:
                        b, bk, fr = bank("s")
                        for h in range(4):
                            t = group(bk[:, h * P:h * P + P],
                                      [(ke[rows, tb, h * P:h * P + P], Ut[rows, tb, h * P:h * P + P])], fr, tU)
                        if c == 0:
                            tS = vcp(gs, bk[:, :].rearrange("p (t a d) -> p t a d", t=2, a=2), t, tW)
                        else:
                            for h in range(4):
                                tS = vst(Sst[h], Sst[h], gend[:, tb, hf, h:h + 1], bk[:, h * P:h * P + P],
                                         ALU.mult, ALU.add, t)
                        free[b] = tS
                    for h in range(4):
                        t = one(bko[:, h * 64:h * 64 + 64],
                                (Ut[rows, tb, h * P:h * P + P], AT[rows, tb, h * P + 64 * hf:h * P + 64 * hf + 64]),
                                tU, fro, start=c == 0, stop=True)
                    to = act(yT[:, 2:6, cols], bko[:, 0:256].rearrange("p (h d) -> p h d", h=4), ACT.Copy, t)
                    free[bo] = to
                    yield
                o4 = yT[:, 2:6]
                sq = LT.rearrange("p t n -> p (t n)").rearrange("p (h s) -> p h s", s=S)
                t = act(sq, o4, ACT.Square, to)
                yield
                b, bk, fr = bank("s")
                for tb in range(2):
                    for h in range(4):
                        t1 = group(bk[:, tb * 4 + h:tb * 4 + h + 1],
                                   [(sq[:, h, tb * P:tb * P + P], onesb[:, 0:1])], t, fr)
                t = vst(ss[:, 0].rearrange("p t h -> p (t h)"), bk[:, 0:8], 1.0 / P,
                        r3.rearrange("p t h -> p (t h)"), ALU.mult, ALU.mult, t1, res["rqq"])
                free[b] = t
                t = vts(ss[:, 0], ss[:, 0], 1e-6, None, ALU.add, None, t)
                t = vtt(rs[:, 0].rearrange("p t h -> p (t h)"), ss[:, 0].rearrange("p t h -> p (t h)"), half(8),
                        ALU.pow, t, q=po)
                t = vtt(rs[:, 0], rs[:, 0], rs[:, 1], ALU.mult, t)
                yield
                for p_ in range(2):
                    b, bk, fr = bank("s")
                    for j in range(2):
                        for tb in range(2):
                            t1 = turnover(bk[:, j * S + tb * P:j * S + tb * P + P],
                                          rs[:, 0, tb, 2 * p_ + j:2 * p_ + j + 1].to_broadcast([P, P]), t, fr)
                    y2 = o4[:, 2 * p_:2 * p_ + 2]
                    t1 = vst(y2, y2, prm("gdn_n", l), bk[:, :].rearrange("p (c s) -> p c s", c=2),
                             ALU.mult, ALU.mult, t1, to)
                    free[b] = t1
                    while "zs" not in res:
                        yield
                    res["gdn", p_] = vtt(y2, y2, zs[:, 2 * p_:2 * p_ + 2], ALU.mult, t1, res["zs"])
                yield


            conv4(kc, 4, "kc")
            (b, bk, fr) = bank("m")
            pe.wait(fr, list(t_h))
            j, wh, wl, th, tl = take()
            ends = []
            for half_, tok in ((0, th), (1, tl)):
                pe.wait(tok)
                prs = [((wh, wl)[half_][:, k, :], s_[:, k, :]) for k in range(8)
                       for s_ in ((hhi, hlo) if half_ == 0 else (hhi,))]
                ends.append(group(bk[0:8, 0:S], prs, start=half_ == 0, stop=half_ == 1))
            done(j, *ends)
            rows8 = part2(23040, S)[0:8]
            free[b] = t_rows = act(rows8, bk[0:8, 0:S], ACT.Copy, ends[1])
            sides[0].append(decay_prep(t_rows))
            sides[0].append(delta())
            conv4(qc, 0, "qc")
            held, t = streamed(4, hh, t_h, toks=416, on=go, mid=step)
            tm = []
            for tb, (b, bk, _) in enumerate(held):
                free[b] = act(m0[:, tb], bk[:, 0:416], ACT.Copy, t)
                tm.append(free[b])
            sides[1].append(latent())
            conv4(vc, 8, "vc")
            t_pad += lastg

            cq = gm[:, 0:512].rearrange("p (c s) -> p c s", s=S)
            ck = gm[:, 512:1024].rearrange("p (c s) -> p c s", s=S)
            cv = gm[:, 1024:1536].rearrange("p (t n) -> p t n", t=2)
            held, t = streamed(4, hh, t_h, chans=4, on=go, mid=step)
            ins = []
            for p_, (b, bk, _) in enumerate(held):
                dst = (cq if p_ == 0 else ck).rearrange("p c s -> p (c s)")
                free[b] = act(dst, bk[:, :], ACT.Copy, t, scale=0.125 if p_ == 0 else 1.0)
                ins.append(free[b])

            def silu_of(b, bk, dst, tmp, *after):
                d2 = dst.rearrange("p c s -> p (c s)")
                t1 = act(tmp, bk[:, :], ACT.Sigmoid, *after)
                free[b] = vtt(d2, bk[:, :], tmp, ALU.mult, t1)
                return free[b]

            heldv, heldg = [bank("m") for _ in range(2)], [bank("m")]
            t = both(heldv, heldg, t_h, go, step)
            for tb, (b, bk, _) in enumerate(heldv):
                free[b] = res["cv"] = act(cv[:, tb], bk[:, 0:256], ACT.Copy, t)
            res["moba_in"] = ins
            tcg = silu_of(heldg[0][0], heldg[0][1], cgs, sgb[:, 0:2].rearrange("p c s -> p (c s)"), t, res["silu"])
            held, t = streamed(4, hh, t_h, chans=2, on=go, mid=step)
            tmg = silu_of(held[0][0], held[0][1], mgs, sgb[:, 2:4].rearrange("p c s -> p (c s)"), t, res["silu"])
            held, t = streamed(4, hh, t_h, chans=4, on=go, mid=step)
            t_last = t
            while ("mla", 1) not in res or "T_free" not in res:
                tick(sides)
            if l == L - 1:
                dma(ac, bufA, a["final_w"], s_fn, res["mla", 1])
            tfin = [None] * 4

            def finish(c, *after):
                tfin[c] = split(hhi[:, 2 * c:2 * c + 2], hlo[:, 2 * c:2 * c + 2], yT[:, 2 * c:2 * c + 2],
                                t_last, *after)

            def gated(name, c0, g, tg_):
                finish(c0 // 2, vtt(yT[:, c0:c0 + 2], yT[:, c0:c0 + 2], g, ALU.mult, tg_, res[name, 0],
                                    res[name, 1]))

            gated("mla", 0, mgs, tmg)
            for p_, (b, bk, _) in enumerate(held):
                res["zs"] = silu_of(b, bk, zs[:, 2 * p_:2 * p_ + 2],
                                    sgb[:, 2 * p_:2 * p_ + 2].rearrange("p c s -> p (c s)"), t, tcg, tmg,
                                    res["T_free"])

            def go_out():
                tick(sides)
                if ("moba", 1) in res and tfin[3] is None:
                    gated("moba", 6, cgs, tcg)

            def rest_of(c):
                while c == 3 and tfin[3] is None:
                    go_out()
                if c == 1:
                    drain(sides)
                    for c_ in (1, 2):
                        finish(c_, res["gdn", c_ - 1])

            return row_out(hh, tfin, t_x, (0, 3, 1, 2), before=rest_of, on=go_out, mid=step)

        def both(hv, hg, t_h, go, step):
            pe.wait([h_[2] for h_ in hv + hg], list(t_h))
            k0 = 0
            for q_ in range(4):
                j, wh, wl, th, tl = take()
                ends = []
                for half_, tok in ((0, th), (1, tl)):
                    pe.wait(tok)
                    w_ = (wh, wl)[half_]
                    for u in range(4):
                        for k in range(2):
                            for s_ in ((hhi, hlo) if half_ == 0 else (hhi,)):
                                opens = q_ == 0 and half_ == 0 and k == 0 and s_ is hhi and u != 3
                                if u < 2:
                                    o = hv[u][1][:, 0:256]
                                    l_, r_ = s_[:, k0 + k, u * P:u * P + P], w_[:, k, 0:256]
                                else:
                                    o = hg[0][1][:, (u - 2) * S:(u - 2) * S + S]
                                    l_, r_ = w_[:, k, u * P:u * P + P], s_[:, k0 + k, :]
                                stp = q_ == 3 and half_ == 1
                                f = (lambda e, o=o, l_=l_, r_=r_, opens=opens, stp=stp:
                                     e.matmul(o, l_, r_, start=opens, stop=stp, skip_group_check=True))
                                if u == 3 and k == 1 and (half_ == 1 or s_ is hlo):
                                    ends.append(pe(f))
                                else:
                                    pe.quiet(f)
                    if half_ == 0:
                        step()
                done(j, ends[0], ends[1])
                k0 += 2
                go()
            return ends[1]

        t_x = [XIN] * 4
        for l in range(L):
            t_x = block1(l, t_x)
        for l in range(L):
            t_x = block2(l, t_x)
        t = inv_rms(t_x)
        for nh in range(2):
            for tb in range(2):
                cols = slice(512 * nh, 512 * nh + 512)
                t2 = vst(xn[:, tb, cols], x[:, tb, cols], st[:, 6 + tb:7 + tb], bufA[:, cols], ALU.mult, ALU.mult,
                         t, (s_fn, 16))
                dma(sp if tb else ac, out[0, tb * P:tb * P + P, cols], xn[:, tb, cols], s_out, t2)
        sp.wait((s_out, 64))
        sp.wait((s_sc, 16))
        assert used[0] == len(parts)

        block = ctx.enter_context(nc.Block())

        @block.sync
        def _(e):
            sp.run(e)

        @block.gpsimd
        def _(e):
            po.run(e)

        @block.scalar
        def _(e):
            ac.run(e)

        @block.vector
        def _(e):
            ve.run(e)

        @block.tensor
        def _(e):
            pe.run(e)


def shape_constants():
    c = np.zeros((P, NCN), np.float32)

    def put(name, m):
        o, w = CN[name]
        c[0:m.shape[0], o:o + w] = m

    i = np.arange(P)
    r, q = i[:, None], i[None, :]
    same = (r // 64) == (q // 64)
    put("ident", np.eye(P))
    put("tri", same & (r <= q))
    put("strict", same & (r < q))
    lv = []
    for s in (1, 2, 4, 8, 16, 32):
        lv.append((r // (2 * s) == q // (2 * s)) & (q % (2 * s) >= s) & (r % (2 * s) < s))
    put("lv", np.concatenate(lv, 1))
    put("blk", same)
    put("half0", (r < 64) & (q >= 0))
    put("half1", (r >= 64) & (q >= 0))
    put("trirev", r >= q)
    put("causal", np.where(q <= r, 0.0, NEG))
    strict = (r < q).astype(np.float32)
    put("m0", np.concatenate([-strict, -np.ones((P, P))], 1))
    put("n0", np.concatenate([np.where(r < q, 0.0, NEG), np.zeros((P, P))], 1))
    n = np.maximum(255 - np.arange(512), 0)
    nf = np.maximum(n, 1).astype(np.float32)
    large = 16 + (np.log(nf / np.float32(16)) / np.float32(np.log(2048 / 16)) * np.float32(16)).astype(np.int32)
    bucket = np.where(n < 16, n, np.minimum(large, 31))
    oh = np.zeros((32, 512), np.float32)
    oh[bucket, np.arange(512)] = 1.0
    inv = [np.float32(500000.0) ** (-(np.arange(h, dtype=np.float32) * np.float32(2.0)) / np.float32(2 * h))
           for h in (16, 8)]
    put("invf", np.broadcast_to(np.concatenate(inv).astype(np.float32), (P, 24)))
    inv2 = (1.0 / (np.float32(10000.0) ** (np.arange(0, 32, 2, dtype=np.float32) / np.float32(32)))).astype(np.float32)
    ang = np.arange(S, dtype=np.float32)[:, None] * inv2[None, :]
    cc, ss = np.cos(ang.astype(np.float32)), np.sin(ang.astype(np.float32))
    put("rope2", np.concatenate([cc[:P], ss[:P], cc[P:], ss[P:]], 1))
    return c, oh, np.ascontiguousarray(np.eye(P, dtype=np.float32)[::-1])


def pack_params(a):
    cols = []
    for l in range(L):
        def ch(v):
            v = v.reshape(-1, v.shape[-1] // P, P)
            return v.transpose(2, 1, 0).reshape(P, -1)

        def rows(v):
            return np.broadcast_to(v[None, :], (P, v.shape[0]))

        part = {
            "g_mix": ch(a["g_mix"][l]), "b_gate": ch(a["b_gate"][l]), "cb_w": ch(a["cb_conv_w"][l]),
            "cb_b": ch(a["cb_conv_b"][l]), "ln_g": ch(a["cb_ln_g"][l]), "ln_b": ch(a["cb_ln_b"][l]),
            "cc_w": ch(a["cc_conv_w"][l]), "g_ffn": ch(a["g_ffn"][l]), "ffn_w": ch(a["ffn_conv_w"][l]),
            "norm2": ch(a["norm_w_2"][l]), "qn2": ch(a["mla_q_norm_2"][l]), "kvn2": ch(a["mla_kv_norm_2"][l]),
            "gdn_w": ch(a["gdn_conv_w_2"][l]), "gdn_n": ch(a["gdn_norm_w_2"][l]),
            "alog": rows(a["gdn_A_log_2"][l]), "dtb": rows(a["gdn_dt_bias_2"][l]),
        }
        for n in PL:
            cols.append(part[n])
    gains = [rows(a[n][l]) for l in range(L) for n in ("g_qa", "g_ka", "g_kidx")]
    return np.ascontiguousarray(np.concatenate(cols, 1)), np.ascontiguousarray(np.concatenate(gains, 1))


BIGS = ["x", "w_in", "w_oa", "w_ob", "w_oc", "w_od", "w_merge", "w_ffn_gate", "w_ffn_up", "w_ffn_down",
        "w_in_2", "mla_w_uq_2", "mla_w_ukv_2", "w_out_2", "t5_table_2"]


def kernel(**inputs):
    import concourse.bacc as bacc
    from concourse.bass_utils import run_bass_kernel_spmd

    h = {k: np.asarray(v) for k, v in inputs.items()}
    feed = {n: np.ascontiguousarray(h[n]) for n in BIGS}
    feed["pos"] = np.ascontiguousarray(h["positions"][0].reshape(2, P).T)
    feed["final_w"] = np.ascontiguousarray(np.broadcast_to(h["final_norm_w_2"][None, :], (P, D)))
    feed["params"], feed["gains"] = pack_params(h)
    feed["consts"], feed["onehot"], feed["flip"] = shape_constants()
    nc = bacc.Bacc("TRN2", target_bir_lowering=False, num_devices=1)
    a, arrays = {}, {}
    for n, v in feed.items():
        arrays[f"in_{n}"] = v
        a[n] = nc.dram_tensor(f"in_{n}", v.shape, mybir.dt.from_np(v.dtype), kind="ExternalInput").ap()
    out = nc.dram_tensor("out_x", (1, S, D), F32, kind="ExternalOutput").ap()
    scratch = nc.dram_tensor("toeplitz", (4, 512), F32, kind="Internal")
    sa = scratch.ap()
    a["scratch"] = sa
    a["toep"] = [bass.AP(tensor=sa.tensor, offset=h_ * 512, ap=[[1, P], [1, S]]) for h_ in range(4)]
    build(nc, a, out)
    r = run_bass_kernel_spmd(nc, [arrays], core_ids=[0])
    return r.results[0]["out_x"]
```
